# Optimizing a Trainium2 kernel written in Bass

```python
import jax, jax.numpy as jnp
from jax import lax
import numpy as np

D_MODEL = 2048
BATCH = 1
SEQ = 256
DEPTH = 1

N_BRANCH = 4
MIX_W = D_MODEL // 4
POOL_GROUPS = 4
POOL_WINDOWS = (2, 4, 8, 16)
POOL_GC = MIX_W // POOL_GROUPS
POOL_OUT = D_MODEL // POOL_GROUPS
CONF_W = MIX_W
CONF_KERNEL = 31
SC_W = MIX_W
SC_KERNEL = 3
FN_GROUPS = 4
FN_GC = MIX_W // FN_GROUPS
OFF_A = 0
OFF_B = OFF_A + MIX_W
OFF_C = OFF_B + 2 * CONF_W
OFF_D = OFF_C + 3 * SC_W
OFF_G = OFF_D + MIX_W
N_IN = OFF_G + N_BRANCH * D_MODEL
N_GROUPS = 4
EXPERTS_PER_GROUP = 8
N_EXPERTS = N_GROUPS * EXPERTS_PER_GROUP
TOP_K = 2
D_EXPERT = D_MODEL // 4
EXPERT_BLOCK = 128
EPS = 1e-6

kernel_name = "hybrid_pool_conformer_shortconv_fnet_hmoe_adaln"

def rmsnorm(x, g):
    x32 = x.astype(jnp.float32)
    y = x32 * lax.rsqrt(jnp.mean(x32 * x32, axis=-1, keepdims=True) + EPS)
    return (y * g.astype(jnp.float32)).astype(x.dtype)

def layernorm(x, g, b):
    x32 = x.astype(jnp.float32)
    mu = jnp.mean(x32, axis=-1, keepdims=True)
    var = jnp.mean(jnp.square(x32 - mu), axis=-1, keepdims=True)
    y = (x32 - mu) * lax.rsqrt(var + EPS) * g.astype(jnp.float32) + b.astype(jnp.float32)
    return y.astype(x.dtype)

def modulate(h, shift, scale):
    return h * (1.0 + scale[:, None, :]) + shift[:, None, :]

def depthwise_conv(v, w):
    k, ch = w.shape
    return lax.conv_general_dilated(
        v, w[:, None, :].astype(v.dtype), window_strides=(1,),
        padding=[(k // 2, k // 2)], dimension_numbers=("NWC", "WIO", "NWC"),
        feature_group_count=ch)

def pool_mixer(u, pool_w, pool_scale):
    b, s, _ = u.shape
    u32 = u.astype(jnp.float32).reshape(b, s, POOL_GROUPS, POOL_GC)
    cs = jnp.concatenate([jnp.zeros((b, 1, POOL_GROUPS, POOL_GC), jnp.float32),
                          jnp.cumsum(u32, axis=1)], axis=1)
    t = jnp.arange(s)
    outs = []
    for gi, w in enumerate(POOL_WINDOWS):
        left = w // 2
        right = w - 1 - left
        lo = jnp.clip(t - left, 0, s)
        hi = jnp.clip(t + right + 1, 0, s)
        cnt = (hi - lo).astype(jnp.float32)[None, :, None]
        outs.append((cs[:, hi, gi] - cs[:, lo, gi]) / cnt - u32[:, :, gi])
    p = jnp.stack(outs, axis=2).astype(u.dtype)
    y = jnp.einsum("bsgc,gcd->bsgd", p, pool_w).reshape(b, s, D_MODEL)
    return y * pool_scale

def conformer_conv(u, dw_w, dw_b, ln_g, ln_b, w_out):
    a, gate = jnp.split(u, 2, axis=-1)
    v = a * jax.nn.sigmoid(gate)
    v = depthwise_conv(v, dw_w) + dw_b
    v = jax.nn.silu(layernorm(v, ln_g, ln_b))
    return v @ w_out

def short_conv(u, conv_w, w_out):
    bg, cg, xv = jnp.split(u, 3, axis=-1)
    z = depthwise_conv(cg * xv, conv_w)
    return (bg * z) @ w_out

def fourier_mixer(u, w_out):
    b, s, _ = u.shape
    z = u.astype(jnp.float32).reshape(b, s, FN_GROUPS, FN_GC)
    f = jnp.fft.fft2(z, axes=(1, 3), norm="ortho").real
    return f.reshape(b, s, MIX_W).astype(u.dtype) @ w_out

def hier_moe(h, rg_w, rg_b, re_w, re_b, w1, w3, w2):
    b, s, d = h.shape
    t_tok = b * s
    ht = h.reshape(t_tok, d)
    pg = jax.nn.softmax((ht @ rg_w + rg_b).astype(jnp.float32), axis=-1)
    pg_top, g_idx = lax.top_k(pg, 1)
    le = (ht @ re_w + re_b).astype(jnp.float32).reshape(t_tok, N_GROUPS, EXPERTS_PER_GROUP)
    le = jnp.take_along_axis(le, g_idx[:, :, None], axis=1)[:, 0]
    pe = jax.nn.softmax(le, axis=-1)
    pe_top, e_idx = lax.top_k(pe, TOP_K)
    pe_top = pe_top / jnp.sum(pe_top, axis=-1, keepdims=True)
    weights = pg_top * pe_top
    experts = g_idx * EXPERTS_PER_GROUP + e_idx
    m = t_tok * TOP_K
    a_exp = experts.reshape(m)
    a_tok = jnp.repeat(jnp.arange(t_tok, dtype=jnp.int32), TOP_K)
    a_w = weights.reshape(m)
    order = jnp.argsort(a_exp)
    s_exp, s_tok, s_w = a_exp[order], a_tok[order], a_w[order]
    counts = jnp.bincount(a_exp, length=N_EXPERTS)
    starts = jnp.cumsum(counts) - counts
    pcounts = (counts + EXPERT_BLOCK - 1) // EXPERT_BLOCK * EXPERT_BLOCK
    pends = jnp.cumsum(pcounts)
    pstarts = pends - pcounts
    dest = pstarts[s_exp] + (jnp.arange(m) - starts[s_exp])
    n_rows = m + N_EXPERTS * EXPERT_BLOCK
    n_blocks = n_rows // EXPERT_BLOCK
    buf_tok = jnp.zeros((n_rows,), jnp.int32).at[dest].set(s_tok)
    buf_w = jnp.zeros((n_rows,), jnp.float32).at[dest].set(s_w)
    block_exp = jnp.clip(jnp.searchsorted(pends, jnp.arange(n_blocks) * EXPERT_BLOCK, side="right"),
                         0, N_EXPERTS - 1)
    xb = ht[buf_tok].reshape(n_blocks, EXPERT_BLOCK, d)

    def run_block(args):
        xblk, e = args
        return (jax.nn.silu(xblk @ w1[e]) * (xblk @ w3[e])) @ w2[e]

    yb = lax.map(run_block, (xb, block_exp)).reshape(n_rows, d)
    out = jnp.zeros((t_tok, d), jnp.float32).at[buf_tok].add(yb.astype(jnp.float32) * buf_w[:, None])
    return out.astype(h.dtype).reshape(b, s, d)

def setup_inputs(seed: int = 0) -> dict:
    key = jax.random.key(seed)
    ks = iter(jax.random.split(key, 32))
    L, D = DEPTH, D_MODEL

    def nrm(shape, scale):
        return jax.random.normal(next(ks), shape, jnp.float32) * scale

    return {
        "x": nrm((BATCH, SEQ, D), 1.0),
        "c": nrm((BATCH, D), 1.0),
        "ada_w": nrm((L, D, 6 * D), 0.5 * D ** -0.5),
        "ada_b": nrm((L, 6 * D), 0.01),
        "norm1_g": 1.0 + nrm((L, D), 0.02),
        "w_in": nrm((L, D, N_IN), D ** -0.5),
        "pool_w": nrm((L, POOL_GROUPS, POOL_GC, POOL_OUT), POOL_GC ** -0.5),
        "pool_scale": 1.0 + nrm((L, D), 0.02),
        "conf_dw_w": nrm((L, CONF_KERNEL, CONF_W), CONF_KERNEL ** -0.5),
        "conf_dw_b": nrm((L, CONF_W), 0.01),
        "conf_ln_g": 1.0 + nrm((L, CONF_W), 0.02),
        "conf_ln_b": nrm((L, CONF_W), 0.01),
        "conf_w_out": nrm((L, CONF_W, D), CONF_W ** -0.5),
        "sc_conv_w": nrm((L, SC_KERNEL, SC_W), SC_KERNEL ** -0.5),
        "sc_w_out": nrm((L, SC_W, D), SC_W ** -0.5),
        "fnet_w_out": nrm((L, MIX_W, D), MIX_W ** -0.5),
        "w_o": nrm((L, D, D), D ** -0.5),
        "norm2_g": 1.0 + nrm((L, D), 0.02),
        "rg_w": nrm((L, D, N_GROUPS), D ** -0.5),
        "rg_b": nrm((L, N_GROUPS), 0.01),
        "re_w": nrm((L, D, N_EXPERTS), D ** -0.5),
        "re_b": nrm((L, N_EXPERTS), 0.01),
        "exp_w1": nrm((L, N_EXPERTS, D, D_EXPERT), D ** -0.5),
        "exp_w3": nrm((L, N_EXPERTS, D, D_EXPERT), D ** -0.5),
        "exp_w2": nrm((L, N_EXPERTS, D_EXPERT, D), D_EXPERT ** -0.5),
        "final_g": 1.0 + nrm((D,), 0.02),
    }

def reference(x, c, ada_w, ada_b, norm1_g, w_in, pool_w, pool_scale, conf_dw_w, conf_dw_b,
              conf_ln_g, conf_ln_b, conf_w_out, sc_conv_w, sc_w_out, fnet_w_out, w_o, norm2_g,
              rg_w, rg_b, re_w, re_b, exp_w1, exp_w3, exp_w2, final_g):
    b, s, d = x.shape
    for l in range(DEPTH):
        mod = c @ ada_w[l] + ada_b[l]
        sh1, sc1, gt1, sh2, sc2, gt2 = jnp.split(mod, 6, axis=-1)
        h = modulate(rmsnorm(x, norm1_g[l]), sh1, sc1)
        u = h @ w_in[l]
        y_a = pool_mixer(u[..., OFF_A:OFF_B], pool_w[l], pool_scale[l])
        y_b = conformer_conv(u[..., OFF_B:OFF_C], conf_dw_w[l], conf_dw_b[l],
                             conf_ln_g[l], conf_ln_b[l], conf_w_out[l])
        y_c = short_conv(u[..., OFF_C:OFF_D], sc_conv_w[l], sc_w_out[l])
        y_d = fourier_mixer(u[..., OFF_D:OFF_G], fnet_w_out[l])
        gates = jax.nn.sigmoid(u[..., OFF_G:]).reshape(b, s, N_BRANCH, d)
        merged = (gates[:, :, 0] * y_a + gates[:, :, 1] * y_b
                  + gates[:, :, 2] * y_c + gates[:, :, 3] * y_d)
        x = x + gt1[:, None, :] * (merged @ w_o[l])
        h2 = modulate(rmsnorm(x, norm2_g[l]), sh2, sc2)
        x = x + gt2[:, None, :] * hier_moe(h2, rg_w[l], rg_b[l], re_w[l], re_b[l],
                                           exp_w1[l], exp_w3[l], exp_w2[l])
    return rmsnorm(x, final_g)


_drawn_inputs = setup_inputs


def setup_inputs(seed=0):
    import zlib

    import numpy as np

    out = dict(_drawn_inputs(seed))
    spreads = {}
    factors = {'pool_scale': 16.62,
     'conf_dw_b': 8.0,
     'conf_ln_g': 21.099,
     'conf_ln_b': 34.809,
     'rg_b': 22.033,
     're_b': 30.777,
     'final_g': 7.459,
     'norm2_g': 4.314}
    for name, (base, spread) in spreads.items():
        noise = np.random.default_rng([zlib.crc32(name.encode()), seed]).standard_normal(out[name].shape)
        drawn = base * np.exp(spread * noise) if base else spread * noise
        out[name] = __import__('jax').numpy.asarray(drawn.astype(out[name].dtype))
    for name, factor in factors.items():
        out[name] = (out[name] * factor).astype(out[name].dtype)
    return out
```

```python
from contextlib import ExitStack

import concourse.bass as bass
from concourse import mybir

F32 = mybir.dt.float32
I32 = mybir.dt.int32
ALU = mybir.AluOpType
ACT = mybir.ActivationFunctionType
AX_X = mybir.AxisListType.X

P = 128
D = 2048
S = 256
KT = D // P
TT = S // P
MIX = D // 4
MT = MIX // P
N_BRANCH = 4
GROUPS, PER_GROUP = 4, 8
NE = GROUPS * PER_GROUP
F = D // 4
FT = F // P
CONF_K, SC_K = 31, 3
EPS = 1e-6
POOL_WINDOWS = (2, 4, 8, 16)
OFF_A, OFF_B, OFF_C, OFF_D, OFF_G = 0, MIX, 3 * MIX, 6 * MIX, 7 * MIX

SLOT = 4096
N_SLOT = 7
W_SLOTS = 4
BW = 4
ADA_SLOTS = 2
ADA_FIRST = 4
NWIN = 64
MAXWIN = S // NWIN
PAIRS = S * 2
PADDED = PAIRS + NWIN

C_N1, C_ADA, C_N2 = 0, 16, 112
C_PS, C_DWB, C_LNG, C_LNB, C_SCW = 128, 144, 148, 152, 156
C_DW = 168
N_COL = C_DW + CONF_K * MT
SH1, SC1, GT1, SH2, SC2, GT2 = range(6)

K_ID, K_ONE, K_TRI, K_IO8 = 0, 128, 256, 384
N_KEEP = 400
N_MIXC = 1024 * 3 + 256


def build(nc, x, c, ada_w, ada_b, norm1_g, w_in, pool_w, pool_scale, conf_dw_w, conf_dw_b, conf_ln_g,
          conf_ln_b, branch_w, sc_conv_w, w_o, norm2_g, rg_w, rg_b, re_w, re_b, exp_w1, exp_w3,
          exp_w2, final_g, keep_consts, mix_consts, iota_const, out):
    with ExitStack() as ctx:
        def sb(name, shape, dt=F32):
            return ctx.enter_context(nc.sbuf_tensor(name, shape, dt))

        def sem(name):
            return ctx.enter_context(nc.semaphore(name))

        ring = sb("ring", [P, N_SLOT, SLOT])
        r_h = sb("r_h", [P, KT * S])
        r_b = sb("r_b", [P, KT * S])
        r_m = sb("r_m", [P, 4096 + 2048 + 2176 + 2048])
        r_c = sb("r_c", [P, N_MIXC])
        keep = sb("keep", [P, N_KEEP])
        col = sb("col", [P, N_COL])
        mod = sb("mod", [P, 6, KT])
        scale1 = sb("scale1", [P, KT])
        scale2 = sb("scale2", [P, KT])
        ccol = sb("ccol", [P, KT])
        stat = sb("stat", [P, 32])

        def slot(s):
            return ring[:, s, :]

        hT = r_h[:, :].rearrange("p (c t) -> p c t", c=KT)
        x1 = r_h[:, :].rearrange("p (t d) -> p t d", t=TT)
        brT = r_b[:, :].rearrange("p (b c t) -> p b c t", b=N_BRANCH, c=MT)
        xn2 = r_b[:, :].rearrange("p (t d) -> p t d", t=TT)
        mergedT = r_m[:, 0:4096].rearrange("p (c t) -> p c t", c=KT)
        x_in = r_m[:, 0:4096].rearrange("p (t d) -> p t d", t=TT)
        h2T = mergedT
        tmp = [r_m[:, 4096:5120], r_m[:, 5120:6144]]
        gt1row = r_m[:, 4096:6144]
        vpad = r_m[:, 6144:6144 + MT * (S + CONF_K - 1)].rearrange("p (c t) -> p c t", c=MT)
        o = 6144 + MT * (S + CONF_K - 1)
        cxpad = r_m[:, o:o + MT * (S + SC_K - 1)].rearrange("p (c t) -> p c t", c=MT)
        pq = r_m[:, 6144:6144 + 2048].rearrange("p (q n) -> p q n", q=4)
        diag = r_m[:, 6144:6144 + 2048].rearrange("p (c k) -> p c k", c=KT)
        junk = r_m[:, 6144:6144 + 2048]
        acc = r_m[:, 8320:8320 + 2048]
        iota = r_m[:, 8320:8320 + 512]
        YS = r_m[:, 0:KT * PADDED].rearrange("p (c j) -> p c j", c=KT)
        e0 = KT * PADDED
        rw = r_m[:, e0:e0 + KT * 36].rearrange("p (c n) -> p c n", c=KT)
        silu_sb = r_m[:, e0 + 576:e0 + 832]
        hid = r_m[:, e0 + 832:e0 + 1088].rearrange("p (f n) -> p f n", f=FT)
        pool_c = r_c[:, 0:2048].rearrange("p (s q t) -> p s q t", s=TT, q=4)
        dftp = r_c[:, 2048:3072].rearrange("p (s n) -> p s n", s=TT)
        dftc = r_c[:, 3072:3328]
        sel = r_c[:, 0:TT * PADDED].rearrange("p (t j) -> p t j", t=TT)
        wT = r_c[:, 1152:2176].rearrange("p (i t) -> p i t", i=4)
        xe = r_c[:, 2176:3200].rearrange("p (c n) -> p c n", c=KT)
        sel_e = r_c[:, 3200:3328].rearrange("p (t n) -> p t n", t=TT)
        ident, ones, tri = keep[:, 0:128], keep[:, 128:256], keep[:, 256:384]
        io8 = keep[:, 384:400].rearrange("p (t e) -> p t e", t=TT)
        prow = ring[:, 0, 0:384].rearrange("p (a b) -> p a b", a=3)
        crow = ring[0:KT, 0, 384:512]

        lg = sb("lg", [P, TT, 36])
        lrow = sb("lrow", [1, 36])
        ra = sb("ra", [P, TT, 4, PER_GROUP])
        m1 = sb("m1", [P, TT, 4, PER_GROUP])
        m2 = sb("m2", [P, TT, 4, PER_GROUP])
        r8 = sb("r8", [P, TT, 5, PER_GROUP])
        rs = sb("rs", [P, 16, TT])
        ct = sb("ct", [32, 2, P])
        st = sb("st", [P, 3, NE])
        tab = sb("tab", [1, 4, NE], I32)
        wtab = sb("wtab", [1, (MAXWIN - 1) * NE], I32)

        ps = ctx.enter_context(nc.psum_tensor("ps", [P, 8, 512], F32))

        def tiles(b, n=2):
            return ps[:, b:b + n, :].rearrange("p b (h t) -> p (b h) t", t=S)

        const_in = sem("const_in")
        mixc_in = sem("mixc_in")
        x_loaded = sem("x_loaded")
        ada_in = [sem(f"ada_in{i}") for i in range(ADA_FIRST)]
        ada2_in = [sem(f"ada2_in{i}") for i in range(ADA_SLOTS)]
        w_in_sem = [sem(f"w_in_sem{i}") for i in range(W_SLOTS)]
        w_used = sem("w_used")
        bw_in = sem("bw_in")
        cols_t = sem("cols_t")
        cols_ready = sem("cols_ready")
        xn_ready = sem("xn_ready")
        xT_done = sem("xT_done")
        xT_saved = sem("xT_saved")
        summed = sem("summed")
        mod_ready = sem("mod_ready")
        h_ready = sem("h_ready")
        unit_saved = sem("unit_saved")
        y_done = sem("y_done")
        y_saved = sem("y_saved")
        conv_done = sem("conv_done")
        ln_sum = sem("ln_sum")
        ln_step = sem("ln_step")
        sc_done = sem("sc_done")
        conf_ready = sem("conf_ready")
        pool_done = sem("pool_done")
        pool_ready = sem("pool_ready")
        dft_done = sem("dft_done")
        dft_saved = sem("dft_saved")
        chain_v = sem("chain_v")
        chain_a = sem("chain_a")
        inv_ready = sem("inv_ready")
        root_done = sem("root_done")
        diag_ready = sem("diag_ready")
        row_done = sem("row_done")
        row_saved = sem("row_saved")
        x_again = sem("x_again")
        iota_in = sem("iota_in")
        wo_done = sem("wo_done")
        x1_ready = sem("x1_ready")
        xn2_ready = sem("xn2_ready")
        h2_t = sem("h2_t")
        h2_ready = sem("h2_ready")
        logit_done = sem("logit_done")
        r_exp = sem("r_exp")
        r_ask = sem("r_ask")
        mask_ready = sem("mask_ready")
        pos_done = sem("pos_done")
        cnt_ready = sem("cnt_ready")
        start_done = sem("start_done")
        table_ready = sem("table_ready")
        selw_ready = sem("selw_ready")
        selw_t = sem("selw_t")
        wT_ready = sem("wT_ready")
        exp_in = [sem(f"exp_in{i}") for i in range(6)]
        exp_free = [sem(f"exp_free{i}") for i in range(6)]
        sel_ready = sem("sel_ready")
        gathered = sem("gathered")
        xe_mul = sem("xe_mul")
        xe_ready = sem("xe_ready")
        h1_done = sem("h1_done")
        h3_done = sem("h3_done")
        silu_done = sem("silu_done")
        hid_ready = sem("hid_ready")
        ye_done = sem("ye_done")
        ye_saved = sem("ye_saved")
        yT_done = sem("yT_done")
        yT_savedA = sem("yT_savedA")
        yT_savedV = sem("yT_savedV")
        comb_done = sem("comb_done")
        x2_ready = sem("x2_ready")
        sq_done = sem("sq_done")
        fin_ready = sem("fin_ready")
        fg_in = sem("fg_in")
        out_done = sem("out_done")
        acc_step = sem("acc_step")
        merge_step = sem("merge_step")

        ada_v = ada_w.rearrange("(k p) n -> p k n", p=P)
        win_v = w_in.rearrange("(k p) n -> p k n", p=P)
        wo_v = w_o.rearrange("(k p) n -> p k n", p=P)
        br_v = branch_w.rearrange("b (k p) n -> b p k n", p=P)
        x_v = x.rearrange("(t p) d -> p t d", p=P)
        out_v = out.rearrange("(t p) d -> p t d", p=P)
        e1_v = exp_w1.rearrange("e (k p) n -> e p k n", p=P)
        e3_v = exp_w3.rearrange("e (k p) n -> e p k n", p=P)
        e2_v = exp_w2.rearrange("e (k p) n -> e p k n", p=P)

        UNIT_COLS = [OFF_B + MIX, OFF_B, OFF_C + MIX, OFF_C + 2 * MIX, OFF_C, OFF_D, OFF_A]
        N_UNIT = len(UNIT_COLS)
        G0 = 2 * N_UNIT
        ADA0 = 16
        WO0 = G0 + N_BRANCH * 8
        UNITS = N_UNIT + 16

        def u_bank(n):
            return 4 * (n % 2)

        def y_bank(n):
            return 4 * (n % 2) + 2

        block = ctx.enter_context(nc.Block())

        @block.sync
        def _(sp):
            def load_ada(v, k, s, done):
                sp.dma_start(slot(s).rearrange("p (k n) -> p k n", k=2),
                             ada_v[:, 2 * k:2 * k + 2, bass.ds(v * D, D)]).then_inc(done, 16)

            def load_w(q, half, first):
                sp.dma_start(slot(q % W_SLOTS).rearrange("p (k n) -> p k n", k=8),
                             win_v[:, 8 * half:8 * half + 8, bass.ds(first, MIX)]
                             ).then_inc(w_in_sem[q % W_SLOTS], 16)

            sp.dma_start(x_in, x_v).then_inc(x_loaded, 16)
            for n in range(ADA0):
                if n >= ADA_FIRST:
                    sp.wait_ge(acc_step, 2 * (n - ADA_FIRST + 1))
                load_ada(n // 8, n % 8, 3 + n % ADA_FIRST, ada_in[n % ADA_FIRST])
            sp.wait_ge(cols_ready, 2)
            for q in range(G0):
                if q == 3:
                    sp.wait_ge(acc_step, 2 * (13))
                if q >= W_SLOTS:
                    sp.wait_ge(w_used, q - W_SLOTS + 1)
                load_w(q, q % 2, UNIT_COLS[q // 2])

            def gate_loads(g, i):
                for j in range(4):
                    if j == 0 and g is None:
                        sp.wait_ge(acc_step, 2 * (14))
                        sp.dma_start(slot(BW)[:, 0:2048].rearrange("p (q n) -> p q n", q=4),
                                     pool_w.rearrange("q c n -> c q n")).then_inc(bw_in, 16)
                    elif j % 2 == 0 and g is not None:
                        sp.wait_ge(y_done, 4 * g + j)
                        sp.dma_start(slot(BW).rearrange("p (k n) -> p k n", k=4),
                                     br_v[bass.ds(g - 1, 1), :, :, j * MIX:(j + 2) * MIX]
                                     .rearrange("b p k n -> (b p) k n")).then_inc(bw_in, 16)
                    for half in range(2):
                        q = 2 * j + half
                        sp.wait_ge(w_used, G0 + q - W_SLOTS + 1 + 8 * i)
                        load_w(G0 + q, half, OFF_G + j * MIX + i * D)
                    for k in (2 * j, 2 * j + 1):
                        sp.wait_ge(acc_step, 2 * (ADA0 + k - ADA_SLOTS + 1 + 8 * i))
                        load_ada(2 + i, k, 5 + k % 2, ada2_in[k % 2])

            gate_loads(None, 0)
            with sp.Fori(1, N_BRANCH) as g:
                gate_loads(g, g)
            for n in range(8):
                if n == 2:
                    sp.wait_ge(w_used, 2 * (UNITS))
                    sp.dma_start(x1, x_v).then_inc(x_again, 16)
                if n == 3:
                    sp.wait_ge(mod_ready, 6)
                    sp.dma_start(iota, iota_const).then_inc(iota_in, 16)
                    sp.dma_start(rw[:, :, 0:4], rg_w.rearrange("(k p) n -> p k n", p=P)).then_inc(iota_in, 16)
                    sp.dma_start(rw[:, :, 4:36], re_w.rearrange("(k p) n -> p k n", p=P)).then_inc(iota_in, 16)
                sp.wait_ge(w_used, WO0 + n - W_SLOTS + 1)
                sp.dma_start(slot((WO0 + n) % W_SLOTS).rearrange("p (k n) -> p k n", k=2),
                             wo_v[:, 2 * n:2 * n + 2, :]).then_inc(w_in_sem[(WO0 + n) % W_SLOTS], 16)

            def load_expert(e, s):
                if s < 4:
                    src = (e1_v, e3_v)[s // 2][bass.ds(e, 1), :, 8 * (s % 2):8 * (s % 2) + 8, :]
                    dst = slot(s).rearrange("p (k n) -> p k n", k=8)
                else:
                    src = e2_v[bass.ds(e, 1), :, 2 * (s - 4):2 * (s - 4) + 2, :]
                    dst = slot(s).rearrange("p (k n) -> p k n", k=2)
                sp.dma_start(dst, src.rearrange("e p k n -> (e p) k n")).then_inc(exp_in[s], 16)

            for s in (4, 5, 2, 3, 0, 1):
                if s == 4:
                    sp.wait_ge(y_done, 16)
                elif s == 5:
                    sp.wait_ge(acc_step, 2 * (6 * 8))
                elif s == 1:
                    sp.wait_ge(wo_done, 8)
                else:
                    sp.wait_ge(w_used, WO0 + 5 + (s - 2) % 4)
                load_expert(0, s)
            with sp.Fori(1, NE) as e:
                for s in range(6):
                    sp.wait_ge(exp_free[s], e)
                    load_expert(e, s)
            sp.dma_start(slot(6)[:, 0:D], final_g.rearrange("(o d) -> o d", o=1).broadcast_to([P, D])
                         ).then_inc(fg_in, 16)
            for t in range(TT):
                sp.wait_ge(fin_ready, t + 1)
                sp.dma_start(out_v[:, t, :], slot(2 + t // 2)[:, (t % 2) * D:(t % 2 + 1) * D]).then_inc(out_done, 16)
            sp.wait_ge(out_done, 32)

        @block.gpsimd
        def _(pool):
            pool.dma_start(r_c[:, :], mix_consts).then_inc(mixc_in, 16)

        @block.tensor
        def _(pe):
            mm = nc.tensor.matmul

            pe.wait_ge(const_in, 16 * 13)
            nc.tensor.transpose(ps[:, 7, 0:128], prow[:, 0, :], ident)
            nc.tensor.transpose(ps[:, 7, 128:168], prow[0:40, 1, :], ident[0:40, 0:40])
            nc.tensor.transpose(ps[:, 7, 168:168 + CONF_K * MT], prow[0:CONF_K * MT, 2, :],
                                ident[0:CONF_K * MT, 0:CONF_K * MT])
            nc.tensor.transpose(ps[:, 7, 320:336], crow, ident[0:KT, 0:KT]).then_inc(cols_t, 1)
            pe.wait_ge(cols_ready, 2)
            for t in range(TT):
                pe.wait_ge(xn_ready, t + 1)
            for b in range(8):
                for k in (2 * b, 2 * b + 1):
                    for t in range(TT):
                        last = nc.tensor.transpose(tiles(b, 1)[:, k % 2, t * P:(t + 1) * P],
                                                   x_in[:, t, k * P:(k + 1) * P], ident)
                last.then_inc(xT_done, 1)

            def sum_ada(n, bank):
                pe.wait_ge(acc_step, 16 * (n + 1))
                for k in range(KT):
                    last = mm(ps[:, bank, k:k + 1], acc[:, k * P:(k + 1) * P], ones[:, 0:1], start=True, stop=True)
                last.then_inc(summed, 1)

            pe.wait_ge(xT_saved, 8)
            sum_ada(SH1, 2)
            pe.wait_ge(mod_ready, 1)
            sum_ada(SC1, 2)

            def unit_T(n, loaded):
                u = tiles(u_bank(n))
                for half in range(2):
                    q = (2 * n + half) % W_SLOTS
                    pe.wait_ge(w_in_sem[q], loaded)
                    w = slot(q).rearrange("p (k n) -> p k n", k=8)
                    for kk in range(8):
                        k = 8 * half + kk
                        if n == 0:
                            pe.wait_ge(h_ready, k + 1)
                        for f in range(4):
                            last = mm(u[:, f, :], w[:, kk, f * P:(f + 1) * P], hT[:, k, :],
                                      start=(k == 0 and f % 2 == 0), stop=(k == KT - 1), skip_group_check=True)
                    last.then_inc(w_used, 1)

            def unit_N(n, loaded):
                for half in range(2):
                    q = (2 * n + half) % W_SLOTS
                    pe.wait_ge(w_in_sem[q], loaded)
                    w = slot(q).rearrange("p (k n) -> p k n", k=8)
                    for kk in range(8):
                        k = 8 * half + kk
                        for t in range(TT):
                            last = mm(ps[:, u_bank(n) + t, :], hT[:, k, t * P:(t + 1) * P], w[:, kk, :],
                                      start=(k == 0), stop=(k == KT - 1))
                    last.then_inc(w_used, 1)

            pe.wait_ge(mod_ready, 2)
            for n in range(5):
                if n >= 2:
                    pe.wait_ge(unit_saved, n - 1)
                unit_T(n, 16 * (n // 2 + 1))
                if n == 3:
                    pe.wait_ge(conv_done, 1)
                    for m in range(MT):
                        last = mm(ps[:, y_bank(n), 0:S], ones, brT[:, 1, m, :], start=(m == 0), stop=(m == MT - 1))
                    last.then_inc(ln_sum, 1)
                if n == 4:
                    pe.wait_ge(ln_step, 1)
                    pe.wait_ge(sc_done, 1)
                    for m in range(MT):
                        last = mm(ps[:, y_bank(n), 0:S], ones, pq[:, m, 0:S], start=(m == 0), stop=(m == MT - 1))
                    last.then_inc(ln_sum, 1)
            for n in (5, 6):
                pe.wait_ge(unit_saved, n - 1)
                unit_N(n, 16 * (n // 2 + 1))

            pe.wait_ge(unit_saved, 6)
            pe.wait_ge(ln_step, 2)
            pe.wait_ge(mixc_in, 16)
            for q in range(4):
                b = (2, 3, 6, 7)[q]
                for t in range(TT):
                    last = mm(ps[:, b, :], tmp[0][:, t * MIX + q * P:t * MIX + (q + 1) * P], dftp[:, t, :],
                              start=(t == 0), stop=(t == TT - 1))
                last.then_inc(dft_done, 1)
            pe.wait_ge(unit_saved, 7)
            pt = tiles(0)
            for q in range(4):
                for t in range(TT):
                    last = mm(pt[:, q, :], tmp[1][:, t * MIX + q * P:t * MIX + (q + 1) * P], pool_c[:, t, q, :],
                              start=(t == 0), stop=(t == TT - 1))
            last.then_inc(pool_done, 1)

            def gate_y(n, kts, lhs, rhs):
                y = tiles(y_bank(n))
                for f in range(4):
                    for k in range(kts):
                        last = mm(y[:, f, :], lhs(k, f), rhs(k), start=(k == 0), stop=(k == kts - 1))
                return last

            pw = slot(BW)[:, 0:2048].rearrange("p (q n) -> p q n", q=4)
            bw = slot(BW).rearrange("p (k n) -> p k n", k=4)
            for j in range(4):
                n = N_UNIT + j
                if j == 1:
                    pe.wait_ge(pool_ready, 1)
                elif j >= 2:
                    pe.wait_ge(unit_saved, n - 1)
                unit_T(n, 16 * (n // 2 + 1))
                if j == 0:
                    pe.wait_ge(bw_in, 16)
                    pe.wait_ge(dft_saved, 4)
                    pe.wait_ge(pool_ready, 1)
                if j >= 2:
                    pe.wait_ge(y_saved, j - 1)
                if j == 1:
                    pe.wait_ge(dft_saved, 5)
                last = gate_y(n, 1, lambda k, f: pw[:, j, f * P:(f + 1) * P], lambda k: brT[:, 0, j, :])
                last.then_inc(y_done, 1)
                if j == 0:
                    for q in range(4):
                        mm(tiles(2)[:, q, :], dftc[:, 0:128], pq[:, q, 0:S], start=True, stop=False)
                        last = mm(tiles(2)[:, q, :], dftc[:, 128:256], pq[:, q, S:2 * S], start=False, stop=True)
                    last.then_inc(dft_done, 1)
            with pe.Fori(1, N_BRANCH) as g:
                for j in range(4):
                    n = N_UNIT + j
                    if j == 0:
                        pe.wait_ge(y_saved, 4 * g - 1)
                        pe.wait_ge(acc_step, 16 * (2 + g))
                        for k in range(KT):
                            last = mm(ps[:, y_bank(n), k:k + 1], acc[:, k * P:(k + 1) * P], ones[:, 0:1],
                                      start=True, stop=True)
                        last.then_inc(summed, 1)
                    pe.wait_ge(unit_saved, N_UNIT - 1 + j + 4 * g)
                    unit_T(n, 16 * (n // 2 + 1) + 32 * g)
                    if j == 0:
                        pe.wait_ge(mod_ready, 2 + g)
                    if j % 2 == 0:
                        pe.wait_ge(bw_in, 16 * (2 * (g - 1) + j // 2 + 2))
                    pe.wait_ge(y_saved, 4 * g + j - 1)
                    last = gate_y(n, MT, lambda k, f: bw[:, k, (j % 2) * MIX + f * P:(j % 2) * MIX + (f + 1) * P],
                                  lambda k: r_b[:, bass.ds(g * MT * S + k * S, S)])
                    last.then_inc(y_done, 1)

            pe.wait_ge(diag_ready, 1)
            pe.wait_ge(y_saved, 15)
            pe.wait_ge(unit_saved, UNITS - 1)
            for n in range(4):
                last = mm(ps[:, 4 + n, :], ones, diag[:, 4 * n:4 * n + 4, :], start=True, stop=True)
            last.then_inc(row_done, 1)
            pe.wait_ge(y_saved, 16)
            sum_ada(5, 2)
            pe.wait_ge(mod_ready, 6)
            pe.wait_ge(unit_saved, UNITS)
            pe.wait_ge(row_saved, 1)
            for i in range(8):
                s = (WO0 + i) % W_SLOTS
                pe.wait_ge(w_in_sem[s], 16 * ((WO0 + i) // W_SLOTS + 1))
                w = slot(s).rearrange("p (k n) -> p k n", k=2)
                for t in range(TT):
                    for n in range(4):
                        for kk in range(2):
                            k = 2 * i + kk
                            last = mm(ps[:, 4 * t + n, :], mergedT[:, k, t * P:(t + 1) * P],
                                      w[:, kk, n * MIX:(n + 1) * MIX], start=(k == 0), stop=(k == KT - 1))
                        if i == 7:
                            last.then_inc(wo_done, 1)
                if i < 7:
                    last.then_inc(w_used, 1)

            pe.wait_ge(x1_ready, 8)
            for t in range(TT):
                pe.wait_ge(xn2_ready, t + 1)
            for b in range(8):
                for k in (2 * b, 2 * b + 1):
                    for t in range(TT):
                        last = nc.tensor.transpose(tiles(b, 1)[:, k % 2, t * P:(t + 1) * P],
                                                   xn2[:, t, k * P:(k + 1) * P], ident)
                last.then_inc(h2_t, 1)
            pe.wait_ge(h2_ready, 16)
            pe.wait_ge(iota_in, 48)
            for t in range(TT):
                for k in range(KT):
                    mm(ps[:, 0, t * 36:(t + 1) * 36], h2T[:, k, t * P:(t + 1) * P], rw[:, k, :],
                       start=(k == 0), stop=False)
                last = mm(ps[:, 0, t * 36:(t + 1) * 36], ones[0:1, :], lrow[0:1, :], start=False, stop=True)
            last.then_inc(logit_done, 1)
            pe.wait_ge(mask_ready, 1)
            mall = ra[:, :, :, :].rearrange("p t g e -> p t (g e)")
            mm(ps[:, 1, 0:32], tri, mall[:, 0, :], start=True, stop=True)
            mm(ps[:, 1, 32:64], ones, mall[:, 0, :], start=True, stop=False)
            mm(ps[:, 1, 32:64], tri, mall[:, 1, :], start=False, stop=True)
            mm(ps[0:32, 2, 0:P], mall[:, 0, :], ones, start=True, stop=False)
            mm(ps[0:32, 2, 0:P], mall[:, 1, :], ones, start=False, stop=True).then_inc(pos_done, 1)
            pe.wait_ge(cnt_ready, 1)
            mm(ps[:, 3, 0:32], ct[:, 0, :], tri[0:32, 0:32], start=True, stop=True)
            mm(ps[:, 3, 32:64], ct[:, 1, :], tri[0:32, 0:32], start=True, stop=True)
            mm(ps[:, 3, 64:96], ct[:, 1, :], ident[0:32, 0:32], start=True, stop=True).then_inc(start_done, 1)
            pe.wait_ge(selw_ready, 1)
            for i in range(4):
                for t in range(TT):
                    last = nc.tensor.transpose(tiles(4)[:, i, t * P:(t + 1) * P],
                                               slot(6)[:, t * PAIRS + i * P:t * PAIRS + (i + 1) * P], ident)
            last.then_inc(selw_t, 1)
            pe.wait_ge(wT_ready, 1)

            gat = ps[:, 0:2, :].rearrange("p b (c n) -> p (b c) n", n=NWIN)
            ye = ps[:, 4:6, :].rearrange("p b (c n) -> p (b c) n", n=NWIN)

            def expert_pass(e, p, free):
                pe.wait_ge(sel_ready, p + 1)
                for k in range(KT):
                    for t in range(TT):
                        last = mm(gat[:, k, :], xn2[:, t, k * P:(k + 1) * P], sel_e[:, t, :],
                                  start=(t == 0), stop=(t == TT - 1))
                last.then_inc(gathered, 1)
                pe.wait_ge(xe_ready, p + 1)
                for s in range(4):
                    pe.wait_ge(exp_in[s], 16 * e + 16)
                    w = slot(s).rearrange("p (k n) -> p k n", k=8)
                    for kk in range(8):
                        k = 8 * (s % 2) + kk
                        for f in range(FT):
                            last = mm(ps[:, 2 + s // 2, f * NWIN:(f + 1) * NWIN], w[:, kk, f * P:(f + 1) * P],
                                      xe[:, k, :], start=(k == 0 and f == 0), stop=(k == KT - 1),
                                      skip_group_check=True)
                    if s % 2:
                        last.then_inc((h1_done, h3_done)[s // 2], 1)
                    elif free:
                        last.then_inc(exp_free[s], 1)
                pe.wait_ge(hid_ready, p + 1)
                for s in (4, 5):
                    pe.wait_ge(exp_in[s], 16 * e + 16)
                    w = slot(s).rearrange("p (k n) -> p k n", k=2)
                    for kk in range(2):
                        k = 2 * (s - 4) + kk
                        for m in range(KT):
                            last = mm(ye[:, m, :], w[:, kk, m * P:(m + 1) * P], hid[:, k, :],
                                      start=(k == 0 and m % 8 == 0), stop=(k == FT - 1), skip_group_check=True)
                    if s == 4 and free:
                        last.then_inc(exp_free[s], 1)
                last.then_inc(ye_done, 1)

            pe.wait_ge(table_ready, 1)
            with pe.Fori(0, NE) as e:
                base = pe.value_load(tab[0:1, 2, bass.ds(e, 1)], min_val=0, max_val=48)
                more = pe.value_load(tab[0:1, 3, bass.ds(e, 1)], min_val=0, max_val=MAXWIN - 1)
                with pe.Fori(0, MAXWIN - 1) as w:
                    with pe.If(more > w):
                        expert_pass(e, base + w, False)
                expert_pass(e, base + more, True)

            for i in range(4):
                b = 4 * (i % 2)
                if i == 0:
                    pe.wait_ge(yT_savedV, 1)
                if i >= 2:
                    pe.wait_ge(yT_savedA, i - 1)
                    pe.wait_ge(yT_savedV, i)
                for k in range(KT):
                    last = nc.tensor.transpose(ps[:, b + k // 4, (k % 4) * P:(k % 4 + 1) * P],
                                               YS[:, k, i * P:(i + 1) * P], ident)
                last.then_inc(yT_done, 1)
            yn = ring[:, 0:2, :].rearrange("p s (i d) -> p (s i) d", d=D)
            for t in range(TT):
                pe.wait_ge(yT_savedA, 3 + t if t == 0 else 4)
                pe.wait_ge(yT_savedV, 4 + t if t == 0 else 5)
                if t == 0:
                    pe.wait_ge(yT_savedA, 4)
                    pe.wait_ge(yT_savedV, 5)
                for n in range(4):
                    for i in range(4):
                        last = mm(ps[:, 4 * t + n, :], wT[:, i, t * P:(t + 1) * P], yn[:, i, n * MIX:(n + 1) * MIX],
                                  start=(i == 0), stop=(i == 3))
                    last.then_inc(comb_done, 1)

        @block.scalar
        def _(act):
            A = nc.scalar.activation
            small = [
                (keep[:, :], keep_consts), (prow[0:16, 0, :], norm1_g.rearrange("(a p) -> a p", p=P)),
                (prow[16:112, 0, :], ada_b.rearrange("(a p) -> a p", p=P)),
                (prow[112:128, 0, :], norm2_g.rearrange("(a p) -> a p", p=P)),
                (prow[0:16, 1, :], pool_scale.rearrange("(a p) -> a p", p=P)),
                (prow[16:20, 1, :], conf_dw_b.rearrange("(a p) -> a p", p=P)),
                (prow[20:24, 1, :], conf_ln_g.rearrange("(a p) -> a p", p=P)),
                (prow[24:28, 1, :], conf_ln_b.rearrange("(a p) -> a p", p=P)),
                (prow[28:40, 1, :], sc_conv_w.rearrange("j (a p) -> (j a) p", p=P)),
                (prow[0:CONF_K * MT, 2, :], conf_dw_w.rearrange("j (a p) -> (j a) p", p=P)),
                (crow, c.rearrange("(a p) -> a p", p=P)),
                (lrow[0:1, 0:4], rg_b.rearrange("(o n) -> o n", o=1)),
                (lrow[0:1, 4:36], re_b.rearrange("(o n) -> o n", o=1)),
            ]
            for dst, src in small:
                act.dma_start(dst, src).then_inc(const_in, 16)
            act.wait_ge(x_loaded, 16)
            for t in range(TT):
                last = A(r_b[:, t * D:(t + 1) * D], x_in[:, t, :], ACT.Square, accum_out=stat[:, t:t + 1])
                last.then_inc(sq_done, 1)
            act.wait_ge(inv_ready, 1)
            A(stat[:, 2:4], stat[:, 2:4], ACT.Sqrt).then_inc(root_done, 1)
            act.wait_ge(root_done, 1)
            for t in range(TT):
                A(x_in[:, t, :], x_in[:, t, :], ACT.Copy, scale=stat[:, 2 + t:3 + t]).then_inc(xn_ready, 1)
            for b in range(8):
                act.wait_ge(xT_done, b + 1)
                A(r_h[:, b * 512:(b + 1) * 512], ps[:, b, :], ACT.Copy).then_inc(xT_saved, 1)
            act.wait_ge(mod_ready, 2)
            act.wait_ge(xT_saved, 8)
            act.wait_ge(cols_ready, 3)
            for k in range(KT):
                A(hT[:, k, :], hT[:, k, :], ACT.Identity, bias=mod[:, SH1, k:k + 1],
                  scale=scale1[:, k:k + 1]).then_inc(h_ready, 1)
            act.wait_ge(w_used, 2 * (1))
            A(tmp[0], ps[:, 0:2, :], ACT.Sigmoid).then_inc(unit_saved, 1)
            act.wait_ge(w_used, 2 * (3))
            act.wait_ge(unit_saved, 2)
            A(tmp[0], ps[:, 0:2, :], ACT.Copy).then_inc(unit_saved, 1)
            act.wait_ge(conv_done, 2)
            act.wait_ge(sc_done, 1)
            A(pq[:, :, 0:S], brT[:, 1, :, :], ACT.Square).then_inc(ln_step, 1)
            act.wait_ge(inv_ready, 2)
            A(tmp[1][:, 0:S], tmp[1][:, 0:S], ACT.Sqrt).then_inc(root_done, 1)
            act.wait_ge(conv_done, 3)
            for m in range(MT):
                A(brT[:, 1, m, :], brT[:, 1, m, :], ACT.Silu, bias=col[:, C_LNB + m:C_LNB + m + 1],
                  scale=col[:, C_LNG + m:C_LNG + m + 1]).then_inc(conf_ready, 1)
            act.wait_ge(w_used, 2 * (6))
            act.wait_ge(unit_saved, 5)
            A(tmp[0], ps[:, 4:6, :], ACT.Copy).then_inc(unit_saved, 1)
            act.wait_ge(w_used, 2 * (7))
            A(tmp[1], ps[:, 0:2, :], ACT.Copy).then_inc(unit_saved, 1)
            for q in range(4):
                act.wait_ge(dft_done, q + 1)
                act.wait_ge(ln_sum, 2)
                A(pq[:, q, :], ps[:, (2, 3, 6, 7)[q], :], ACT.Copy).then_inc(dft_saved, 1)
            act.wait_ge(pool_done, 1)
            A(r_b[:, 0:1024], ps[:, 0:2, :], ACT.Copy).then_inc(pool_ready, 1)

            def gate(done, n, y_before):
                act.wait_ge(w_used, 2 * (done))
                act.wait_ge(y_saved, y_before)
                A(tmp[n % 2], ps[:, u_bank(n):u_bank(n) + 2, :], ACT.Sigmoid).then_inc(unit_saved, 1)

            for j in range(4):
                gate(N_UNIT + j + 1, N_UNIT + j, max(j - 1, 0))
                if j == 0:
                    act.wait_ge(dft_done, 5)
                    A(r_b[:, 3072:4096], ps[:, 2:4, :], ACT.Copy).then_inc(dft_saved, 1)
            with act.Fori(1, N_BRANCH) as g:
                for j in range(4):
                    gate(N_UNIT + j + 1 + 4 * g, N_UNIT + j, 4 * g + j - 1)
            act.wait_ge(row_done, 1)
            act.wait_ge(y_saved, 16)
            A(gt1row, ps[:, 4:8, :], ACT.Copy).then_inc(row_saved, 1)

            for t in range(TT):
                act.wait_ge(x1_ready, 4 * t + 4)
                act.wait_ge(sq_done, 2 + t)
                A(junk, x1[:, t, :], ACT.Square, accum_out=stat[:, 4 + t:5 + t]).then_inc(sq_done, 1)
            for t in range(TT):
                r = stat[:, 6 + t:7 + t]
                act.wait_ge(inv_ready, 3 + t)
                A(r, r, ACT.Sqrt).then_inc(root_done, 1)
                act.wait_ge(root_done, 3 + t)
                A(xn2[:, t, :], x1[:, t, :], ACT.Copy, scale=stat[:, 6 + t:7 + t]).then_inc(xn2_ready, 1)
            for b in range(0, 8, 2):
                act.wait_ge(h2_t, b + 1)
                for k in (2 * b, 2 * b + 1):
                    A(h2T[:, k, :], tiles(b, 1)[:, k % 2, :], ACT.Identity, bias=mod[:, SH2, k:k + 1],
                      scale=scale2[:, k:k + 1]).then_inc(h2_ready, 1)
            act.wait_ge(r_ask, 1)
            A(r8[:, :, 1, 0:4], r8[:, :, 0, 0:4], ACT.Exp).then_inc(r_exp, 1)
            act.wait_ge(r_ask, 2)
            A(rs[:, 8, :], rs[:, 7, :], ACT.Exp).then_inc(r_exp, 1)
            act.wait_ge(selw_t, 1)
            A(wT[:, :, :], tiles(4), ACT.Copy).then_inc(wT_ready, 1)

            def expert_pass(p, off, free):
                A(sel_e[:, :, :], sel[:, :, bass.ds(off, NWIN)], ACT.Copy).then_inc(sel_ready, 1)
                act.wait_ge(h1_done, p + 1)
                if free:
                    act.sem_inc(exp_free[1], 1)
                A(silu_sb, ps[:, 2, 0:FT * NWIN], ACT.Silu).then_inc(silu_done, 1)

            act.wait_ge(table_ready, 1)
            with act.Fori(0, NE) as e:
                last_off = act.value_load(tab[0:1, 1, bass.ds(e, 1)], min_val=0, max_val=PAIRS)
                base = act.value_load(tab[0:1, 2, bass.ds(e, 1)], min_val=0, max_val=48)
                more = act.value_load(tab[0:1, 3, bass.ds(e, 1)], min_val=0, max_val=MAXWIN - 1)
                with act.Fori(0, MAXWIN - 1) as w:
                    with act.If(more > w):
                        off = act.value_load(wtab[0:1, bass.ds(w * NE + e, 1)], min_val=0, max_val=PAIRS)
                        expert_pass(base + w, off, False)
                expert_pass(base + more, last_off, True)

            yn = ring[:, 0:2, :].rearrange("p s (i d) -> p (s i) d", d=D)
            for i in range(4):
                b = 4 * (i % 2)
                act.wait_ge(yT_done, i + 1)
                A(yn[:, i, 0:1024], ps[:, b:b + 2, :], ACT.Copy).then_inc(yT_savedA, 1)
            for t in range(TT):
                for n in range(4):
                    act.wait_ge(x2_ready, 4 * t + n + 1)
                    if t:
                        act.wait_ge(sq_done, 4 + n + 1)
                    A(slot(4)[:, n * MIX:(n + 1) * MIX], x1[:, t, n * MIX:(n + 1) * MIX], ACT.Square,
                      accum_out=stat[:, 8 + 4 * t + n:9 + 4 * t + n]).then_inc(sq_done, 1)
                act.wait_ge(inv_ready, 5 + t)
                A(stat[:, 16 + t:17 + t], stat[:, 16 + t:17 + t], ACT.Sqrt).then_inc(root_done, 1)

        @block.vector
        def _(v):
            V = nc.vector
            steps = [0]

            def step(ins):
                steps[0] += 1
                ins.then_inc(chain_v, 1)
                v.wait_ge(chain_v, steps[0])

            v.wait_ge(cols_t, 1)
            V.tensor_copy(col[:, :], ps[:, 7, 0:N_COL]).then_inc(cols_ready, 1)
            V.tensor_copy(ccol[:, :], ps[:, 7, 320:336]).then_inc(cols_ready, 1)
            v.wait_ge(cols_ready, 2)
            v.wait_ge(sq_done, 2)
            step(V.tensor_scalar(stat[:, 2:4], stat[:, 0:2], 1.0 / D, EPS, ALU.mult, ALU.add))
            V.reciprocal(stat[:, 2:4], stat[:, 2:4]).then_inc(inv_ready, 1)

            def ada_chunk(s, k, first):
                w = slot(s).rearrange("p (k n) -> p k n", k=2)
                for i in range(2):
                    kk = 2 * k + i
                    if kk == 0:
                        ins = V.tensor_scalar(acc, w[:, i, :], ccol[:, kk:kk + 1], None, ALU.mult)
                    else:
                        ins = V.scalar_tensor_tensor(out=acc, in0=w[:, i, :], scalar=ccol[:, kk:kk + 1], in1=acc,
                                                     op0=ALU.mult, op1=ALU.add)
                    yield ins



            for n in range(ADA0):
                v.wait_ge(ada_in[n % ADA_FIRST], 16 * (n // ADA_FIRST + 1))
                if n == 8:
                    v.wait_ge(summed, 1)
                for i, ins in enumerate(ada_chunk(3 + n % ADA_FIRST, n % 8, n % 8 == 0)):
                    ins.then_inc(acc_step, 1)
                    v.wait_ge(acc_step, 2 * n + i + 1)
                if n % 8 == 7:
                    m = n // 8
                    v.wait_ge(summed, m + 1)
                    V.tensor_tensor(mod[:, m, :], ps[:, 2, 0:KT], col[:, C_ADA + m * KT:C_ADA + (m + 1) * KT],
                                    ALU.add).then_inc(mod_ready, 1)
            v.wait_ge(mod_ready, 2)
            V.scalar_tensor_tensor(out=scale1[:, :], in0=mod[:, SC1, :], scalar=1.0, in1=col[:, C_N1:C_N1 + KT],
                                   op0=ALU.add, op1=ALU.mult).then_inc(cols_ready, 1)
            V.memset(r_m[:, 6144:6144 + MT * (S + CONF_K - 1) + MT * (S + SC_K - 1)], 0.0).then_inc(cols_ready, 1)
            v.wait_ge(cols_ready, 4)

            v.wait_ge(w_used, 2 * (2))
            v.wait_ge(unit_saved, 1)
            step(V.tensor_tensor(vpad[:, :, 15:15 + S], tiles(4), tmp[0].rearrange("p (c t) -> p c t", c=MT), ALU.mult))
            v.sem_inc(unit_saved, 1)
            c0 = steps[0]
            for j in range(CONF_K):
                for m in range(MT):
                    wcol = col[:, C_DW + j * MT + m:C_DW + j * MT + m + 1]
                    if j:
                        v.wait_ge(chain_v, c0 + (j - 1) * MT + m + 1)
                        ins = V.scalar_tensor_tensor(out=brT[:, 1, m, :], in0=vpad[:, m, j:j + S], scalar=wcol,
                                                     in1=brT[:, 1, m, :], op0=ALU.mult, op1=ALU.add)
                    else:
                        ins = V.tensor_scalar(brT[:, 1, m, :], vpad[:, m, 0:S], wcol,
                                              col[:, C_DWB + m:C_DWB + m + 1], ALU.mult, ALU.add)
                    ins.then_inc(chain_v, 1)
            steps[0] += CONF_K * MT
            v.wait_ge(chain_v, steps[0])
            v.sem_inc(conv_done, 1)

            v.wait_ge(w_used, 2 * (4))
            v.wait_ge(unit_saved, 3)
            step(V.tensor_tensor(cxpad[:, :, 1:1 + S], tiles(4), tmp[0].rearrange("p (c t) -> p c t", c=MT), ALU.mult))
            v.sem_inc(unit_saved, 1)
            z = tmp[0].rearrange("p (c t) -> p c t", c=MT)
            c0 = steps[0]
            for j in range(SC_K):
                for m in range(MT):
                    wcol = col[:, C_SCW + j * MT + m:C_SCW + j * MT + m + 1]
                    if j:
                        v.wait_ge(chain_v, c0 + (j - 1) * MT + m + 1)
                        ins = V.scalar_tensor_tensor(out=z[:, m, :], in0=cxpad[:, m, j:j + S], scalar=wcol,
                                                     in1=z[:, m, :], op0=ALU.mult, op1=ALU.add)
                    else:
                        ins = V.tensor_scalar(z[:, m, :], cxpad[:, m, 0:S], wcol, None, ALU.mult)
                    ins.then_inc(chain_v, 1)
            steps[0] += SC_K * MT
            v.wait_ge(chain_v, steps[0])
            v.sem_inc(sc_done, 1)

            lb = y_bank(3)
            v.wait_ge(ln_sum, 1)
            mrow = tmp[1][:, 0:S]
            step(V.tensor_scalar(mrow, ps[:, lb, 0:S], 1.0 / MIX, None, ALU.mult))
            V.tensor_tensor(brT[:, 1, :, :], brT[:, 1, :, :], mrow.unsqueeze(1).broadcast_to([P, MT, S]),
                            ALU.subtract).then_inc(conv_done, 1)
            v.wait_ge(w_used, 2 * (5))
            V.tensor_tensor(brT[:, 2, :, :], tiles(0), z, ALU.mult).then_inc(unit_saved, 1)
            v.wait_ge(ln_sum, 2)
            step(V.tensor_scalar(mrow, ps[:, y_bank(4), 0:S], 1.0 / MIX, EPS, ALU.mult, ALU.add))
            v.sem_inc(ln_step, 1)
            V.reciprocal(mrow, mrow).then_inc(inv_ready, 1)
            v.wait_ge(root_done, 2)
            V.tensor_tensor(brT[:, 1, :, :], brT[:, 1, :, :], mrow.unsqueeze(1).broadcast_to([P, MT, S]),
                            ALU.mult).then_inc(conv_done, 1)

            def ada_two(i, j):
                for k in (2 * j, 2 * j + 1):
                    if k == 0:
                        v.wait_ge(summed, 2 + i)
                    v.wait_ge(ada2_in[k % 2], 16 * (k // 2 + 1) + 64 * i)
                    for a, ins in enumerate(ada_chunk(5 + k % 2, k, k == 0)):
                        ins.then_inc(acc_step, 1)
                        v.wait_ge(acc_step, 2 * ADA0 + 2 * k + a + 1 + 16 * i)

            for j in range(4):
                n = N_UNIT + j
                ada_two(0, j)
                v.wait_ge(y_done, j + 1)
                v.wait_ge(unit_saved, n + 1)
                for f in range(4):
                    ins = V.scalar_tensor_tensor(out=mergedT[:, 4 * j + f, :], in0=tiles(y_bank(n))[:, f, :],
                                                 scalar=col[:, C_PS + 4 * j + f:C_PS + 4 * j + f + 1],
                                                 in1=tmp[n % 2][:, f * S:(f + 1) * S], op0=ALU.mult, op1=ALU.mult)
                ins.then_inc(y_saved, 1)
            with v.Fori(1, N_BRANCH) as g:
                v.wait_ge(summed, 2 + g)
                V.tensor_tensor(mod[:, bass.ds(g + 1, 1), :].rearrange("p a k -> p (a k)"), ps[:, y_bank(N_UNIT), 0:KT],
                                col[:, bass.ds(C_ADA + (g + 1) * KT, KT)], ALU.add).then_inc(mod_ready, 1)
                for j in range(4):
                    n = N_UNIT + j
                    ada_two(g, j)
                    v.wait_ge(y_done, 4 * g + j + 1)
                    v.wait_ge(unit_saved, n + 1 + 4 * g)
                    gy = tmp[n % 2]
                    V.tensor_tensor(gy, ps[:, y_bank(n):y_bank(n) + 2, :].rearrange("p b n -> p (b n)"), gy,
                                    ALU.mult).then_inc(merge_step, 1)
                    v.wait_ge(merge_step, 4 * g + j - 3)
                    v.wait_ge(y_saved, 4 * g + j - 3)
                    m = r_m[:, j * 1024:(j + 1) * 1024]
                    V.tensor_tensor(m, m, gy, ALU.add).then_inc(y_saved, 1)
            v.wait_ge(mod_ready, 5)
            v.wait_ge(dft_done, 5)
            V.tensor_tensor(diag, ident.unsqueeze(1).broadcast_to([P, KT, P]),
                            mod[:, GT1, :].unsqueeze(2).broadcast_to([P, KT, P]), ALU.mult).then_inc(diag_ready, 1)
            v.wait_ge(summed, 6)
            V.tensor_tensor(mod[:, GT2, :], ps[:, 2, 0:KT], col[:, C_ADA + GT2 * KT:C_ADA + (GT2 + 1) * KT],
                            ALU.add).then_inc(mod_ready, 1)
            step(V.scalar_tensor_tensor(out=scale2[:, :], in0=mod[:, SC2, :], scalar=1.0, in1=col[:, C_N2:C_N2 + KT],
                                        op0=ALU.add, op1=ALU.mult))

            v.wait_ge(x_again, 16)
            v.wait_ge(row_saved, 1)
            for t in range(TT):
                for n in range(4):
                    v.wait_ge(wo_done, 4 * t + n + 1)
                    prod = slot(6)[:, (n % 2) * MIX:(n % 2 + 1) * MIX]
                    step(V.tensor_tensor(prod, ps[:, 4 * t + n, :], gt1row[:, n * MIX:(n + 1) * MIX], ALU.mult))
                    xs = x1[:, t, n * MIX:(n + 1) * MIX]
                    V.tensor_tensor(xs, xs, prod, ALU.add).then_inc(x1_ready, 1)
            for t in range(TT):
                v.wait_ge(sq_done, 3 + t)
                step(V.tensor_scalar(stat[:, 6 + t:7 + t], stat[:, 4 + t:5 + t], 1.0 / D, EPS, ALU.mult, ALU.add))
                V.reciprocal(stat[:, 6 + t:7 + t], stat[:, 6 + t:7 + t]).then_inc(inv_ready, 1)
            for b in range(1, 8, 2):
                v.wait_ge(h2_t, b + 1)
                for k in (2 * b, 2 * b + 1):
                    V.tensor_scalar(h2T[:, k, :], tiles(b, 1)[:, k % 2, :], scale2[:, k:k + 1], mod[:, SH2, k:k + 1],
                                    ALU.mult, ALU.add).then_inc(h2_ready, 1)

            def b8(ap, n):
                return ap.unsqueeze(2).broadcast_to([P, TT, n])

            def first_of(out_hot, key, least, n):
                step(V.scalar_tensor_tensor(out=key, in0=key, scalar=-float(PER_GROUP), in1=io8[:, :, 0:n],
                                            op0=ALU.mult, op1=ALU.add))
                step(V.tensor_reduce(least, key, AX_X, ALU.min))
                step(V.tensor_tensor(out_hot, key, b8(least, n), ALU.is_equal))

            v.wait_ge(logit_done, 1)
            step(V.tensor_copy(lg[:, :, :], ps[:, 0, 0:72].rearrange("p (t n) -> p t n", t=TT)))
            step(V.tensor_reduce(rs[:, 0, :], lg[:, :, 0:4], AX_X, ALU.max))
            V.tensor_tensor(r8[:, :, 0, 0:4], lg[:, :, 0:4], b8(rs[:, 0, :], 4), ALU.subtract).then_inc(r_ask, 1)
            ghot = r8[:, :, 2, 0:4]
            step(V.tensor_tensor(ghot, lg[:, :, 0:4], b8(rs[:, 0, :], 4), ALU.is_equal))
            first_of(ghot, ghot, rs[:, 1, :], 4)
            v.wait_ge(r_exp, 1)
            step(V.tensor_reduce(rs[:, 2, :], r8[:, :, 1, 0:4], AX_X, ALU.add))
            step(V.reciprocal(rs[:, 3, :], rs[:, 2, :]))
            for t in range(TT):
                step(V.tensor_tensor(ra[:, t, :, :], lg[:, t, 4:36].rearrange("p (g e) -> p g e", g=4),
                                     r8[:, t, 2, 0:4].unsqueeze(2).broadcast_to([P, 4, PER_GROUP]), ALU.mult))
            le = r8[:, :, 0, :]
            v.wait_ge(r_exp, 1)
            for t in range(TT):
                step(V.tensor_reduce(r8[:, t, 0, :], ra[:, t, :, :].rearrange("p g e -> p e g"), AX_X, ALU.add))
            hot1, hot2, le2 = r8[:, :, 3, :], r8[:, :, 4, :], r8[:, :, 1, :]
            step(V.tensor_reduce(rs[:, 4, :], le, AX_X, ALU.max))
            step(V.tensor_tensor(hot1, le, b8(rs[:, 4, :], 8), ALU.is_equal))
            first_of(hot1, hot1, rs[:, 5, :], 8)
            step(V.scalar_tensor_tensor(out=le2, in0=hot1, scalar=-3.0e38, in1=le, op0=ALU.mult, op1=ALU.add))
            step(V.tensor_reduce(rs[:, 6, :], le2, AX_X, ALU.max))
            step(V.tensor_tensor(rs[:, 7, :], rs[:, 6, :], rs[:, 4, :], ALU.subtract))
            v.sem_inc(r_ask, 1)
            step(V.tensor_tensor(hot2, le2, b8(rs[:, 6, :], 8), ALU.is_equal))
            first_of(hot2, hot2, rs[:, 9, :], 8)
            for t in range(TT):
                for m, hot in ((m1, 3), (m2, 4)):
                    step(V.tensor_tensor(m[:, t, :, :], r8[:, t, 2, 0:4].unsqueeze(2).broadcast_to([P, 4, PER_GROUP]),
                                         r8[:, t, hot, :].unsqueeze(1).broadcast_to([P, 4, PER_GROUP]), ALU.mult))
            flat = "p t g e -> p (t g e)"
            V.tensor_tensor(ra[:, :, :, :].rearrange(flat), m1[:, :, :, :].rearrange(flat),
                            m2[:, :, :, :].rearrange(flat), ALU.add).then_inc(mask_ready, 1)
            v.wait_ge(r_exp, 2)
            step(V.tensor_scalar(rs[:, 10, :], rs[:, 8, :], 1.0, None, ALU.add))
            step(V.reciprocal(rs[:, 10, :], rs[:, 10, :]))
            step(V.tensor_tensor(rs[:, 11, :], rs[:, 3, :], rs[:, 10, :], ALU.mult))
            step(V.tensor_tensor(rs[:, 12, :], rs[:, 11, :], rs[:, 8, :], ALU.mult))
            v.wait_ge(pos_done, 1)
            step(V.tensor_copy(ct[:, 0, :], ps[0:32, 2, 0:P]))
            step(V.tensor_scalar(ct[:, 1, :], ct[:, 0, :], float(NWIN), 1.0, ALU.is_gt, ALU.add))
            for w in range(2, MAXWIN):
                ins = V.scalar_tensor_tensor(out=ct[:, 1, :], in0=ct[:, 0, :], scalar=float(w * NWIN), in1=ct[:, 1, :],
                                             op0=ALU.is_gt, op1=ALU.add)
                if w < MAXWIN - 1:
                    step(ins)
            ins.then_inc(cnt_ready, 1)
            v.wait_ge(start_done, 1)
            step(V.tensor_copy(st[:, :, :], ps[:, 3, 0:96].rearrange("p (a e) -> p a e", a=3)))
            mall = ra[:, :, :, :].rearrange("p t g e -> p t (g e)")
            for t in range(TT):
                step(V.tensor_tensor(mall[:, t, :], ps[:, 1, t * 32:(t + 1) * 32], st[:, 0, :], ALU.add))
            for m, r in ((m1, 13), (m2, 14)):
                mm_ = m[:, :, :, :].rearrange("p t g e -> p t (g e)")
                step(V.tensor_tensor(mm_, mm_, mall, ALU.mult))
                step(V.tensor_reduce(rs[:, r, :], mm_, AX_X, ALU.add))
            trow = lg[0:1, 0, 0:32]
            for w in range(MAXWIN - 1):
                step(V.tensor_scalar(wtab[0:1, w * NE:(w + 1) * NE], st[0:1, 0, :], float(w * NWIN), float(PAIRS),
                                     ALU.add, ALU.min))
            step(V.tensor_copy(tab[0:1, 2, :], st[0:1, 1, :]))
            step(V.tensor_scalar(st[0:1, 2, :], st[0:1, 2, :], -1.0, None, ALU.add))
            step(V.tensor_copy(tab[0:1, 3, :], st[0:1, 2, :]))
            step(V.scalar_tensor_tensor(out=trow, in0=st[0:1, 2, :], scalar=float(NWIN), in1=st[0:1, 0, :],
                                        op0=ALU.mult, op1=ALU.add))
            step(V.tensor_copy(tab[0:1, 1, :], trow))
            v.wait_ge(iota_in, 48)
            for t in range(TT):
                step(V.tensor_scalar(sel[:, t, 0:PAIRS], iota, rs[:, 13, t:t + 1], None, ALU.is_equal))
                step(V.scalar_tensor_tensor(out=sel[:, t, 0:PAIRS], in0=iota, scalar=rs[:, 14, t:t + 1],
                                            in1=sel[:, t, 0:PAIRS], op0=ALU.is_equal, op1=ALU.add))
            step(V.memset(sel[:, :, PAIRS:PADDED], 0.0))
            v.sem_inc(table_ready, 1)
            for t in range(TT):
                sw = slot(6)[:, t * PAIRS:(t + 1) * PAIRS]
                sw2 = slot(6)[:, (2 + t) * PAIRS:(3 + t) * PAIRS]
                step(V.tensor_scalar(sw, iota, rs[:, 13, t:t + 1], rs[:, 11, t:t + 1], ALU.is_equal, ALU.mult))
                step(V.tensor_scalar(sw2, iota, rs[:, 14, t:t + 1], rs[:, 12, t:t + 1], ALU.is_equal, ALU.mult))
                step(V.tensor_tensor(sw, sw, sw2, ALU.add))
            v.sem_inc(selw_ready, 1)

            gat = ps[:, 0:2, :].rearrange("p b (c n) -> p (b c) n", n=NWIN)
            ye = ps[:, 4:6, :].rearrange("p b (c n) -> p (b c) n", n=NWIN)

            def wide(ap):
                return ap.unsqueeze(2).broadcast_to([P, KT, NWIN])

            def expert_pass(p, off, free):
                v.wait_ge(gathered, p + 1)
                V.tensor_tensor(xe, gat, wide(scale2[:, :]), ALU.mult).then_inc(xe_mul, 1)
                v.wait_ge(xe_mul, p + 1)
                V.tensor_tensor(xe, xe, wide(mod[:, SH2, :]), ALU.add).then_inc(xe_ready, 1)
                v.wait_ge(silu_done, p + 1)
                v.wait_ge(h3_done, p + 1)
                if free:
                    v.sem_inc(exp_free[3], 1)
                V.tensor_tensor(hid.rearrange("p f n -> p (f n)"), silu_sb, ps[:, 3, 0:FT * NWIN],
                                ALU.mult).then_inc(hid_ready, 1)
                v.wait_ge(ye_done, p + 1)
                if free:
                    v.sem_inc(exp_free[5], 1)
                V.tensor_tensor(YS[:, :, bass.ds(off, NWIN)], ye, wide(mod[:, GT2, :]), ALU.mult).then_inc(ye_saved, 1)

            v.wait_ge(h2_ready, 16)
            with v.Fori(0, NE) as e:
                last_off = v.value_load(tab[0:1, 1, bass.ds(e, 1)], min_val=0, max_val=PAIRS)
                base = v.value_load(tab[0:1, 2, bass.ds(e, 1)], min_val=0, max_val=48)
                more = v.value_load(tab[0:1, 3, bass.ds(e, 1)], min_val=0, max_val=MAXWIN - 1)
                with v.Fori(0, MAXWIN - 1) as w:
                    with v.If(more > w):
                        off = v.value_load(wtab[0:1, bass.ds(w * NE + e, 1)], min_val=0, max_val=PAIRS)
                        expert_pass(base + w, off, False)
                expert_pass(base + more, last_off, True)
                v.wait_ge(ye_saved, base + more + 1)
            step(V.memset(stat[:, 25:26], 0.0))
            v.sem_inc(yT_savedV, 1)

            yn = ring[:, 0:2, :].rearrange("p s (i d) -> p (s i) d", d=D)
            for i in range(4):
                b = 4 * (i % 2) + 2
                v.wait_ge(yT_done, i + 1)
                V.tensor_copy(yn[:, i, 1024:2048], ps[:, b:b + 2, :].rearrange("p b n -> p (b n)")).then_inc(yT_savedV, 1)
            for t in range(TT):
                for n in range(4):
                    v.wait_ge(comb_done, 4 * t + n + 1)
                    xs = x1[:, t, n * MIX:(n + 1) * MIX]
                    V.tensor_tensor(xs, xs, ps[:, 4 * t + n, :], ALU.add).then_inc(x2_ready, 1)
            v.wait_ge(fg_in, 16)
            for t in range(TT):
                v.wait_ge(sq_done, 4 + 4 * (t + 1))
                r = stat[:, 16 + t:17 + t]
                step(V.tensor_reduce(r, stat[:, 8 + 4 * t:12 + 4 * t], AX_X, ALU.add))
                step(V.tensor_scalar(r, r, 1.0 / D, EPS, ALU.mult, ALU.add))
                V.reciprocal(r, r).then_inc(inv_ready, 1)
                v.wait_ge(root_done, 5 + t)
                V.scalar_tensor_tensor(out=slot(2)[:, t * D:(t + 1) * D], in0=x1[:, t, :], scalar=r,
                                       in1=slot(6)[:, 0:D], op0=ALU.mult, op1=ALU.mult).then_inc(fin_ready, 1)


def constants():
    import numpy as np

    i = np.arange(P)
    keep = np.zeros((P, N_KEEP), np.float32)
    keep[:, 0:128] = np.eye(P)
    keep[:, 128:256] = 1.0
    keep[:, 256:384] = i[:, None] < i[None, :]
    keep[:, 384:400] = np.tile(np.arange(8), 2)
    t = np.arange(S)
    pool = np.zeros((S, 4, S))
    for q, w in enumerate(POOL_WINDOWS):
        left = w // 2
        lo, hi = np.clip(t - left, 0, S), np.clip(t + w - left, 0, S)
        inside = (t[:, None] >= lo[None, :]) & (t[:, None] < hi[None, :])
        pool[:, q, :] = inside / (hi - lo)[None, :] - np.eye(S)
    a = 2 * np.pi * (np.outer(t, t) % S) / S
    norm = 1 / np.sqrt(S * P)
    pos = np.concatenate([np.cos(a), np.sin(a)], 1) * norm
    b = 2 * np.pi * (np.outer(i, i) % P) / P
    ch = np.concatenate([np.cos(b), -np.sin(b)], 1)
    halves = lambda m: m.reshape(2, P, -1).transpose(1, 0, 2).reshape(P, -1)
    mix = np.concatenate([halves(pool.reshape(S, -1)), halves(pos), ch], 1).astype(np.float32)
    iota = np.tile(np.arange(512, dtype=np.float32), (P, 1))
    return keep, np.ascontiguousarray(mix), iota


_INS = ["x", "c", "ada_w", "ada_b", "norm1_g", "w_in", "pool_w", "pool_scale", "conf_dw_w", "conf_dw_b", "conf_ln_g",
        "conf_ln_b", "branch_w", "sc_conv_w", "w_o", "norm2_g", "rg_w", "rg_b", "re_w", "re_b", "exp_w1", "exp_w3",
        "exp_w2", "final_g"]


def kernel(**inputs):
    import numpy as _np
    import concourse.bacc as _bacc
    from concourse import mybir as _mybir
    from concourse.bass_utils import run_bass_kernel_spmd as _run

    given = dict(inputs)
    given["branch_w"] = _np.stack([_np.asarray(inputs[n])[0] for n in ("conf_w_out", "sc_w_out", "fnet_w_out")])
    nc = _bacc.Bacc("TRN2", target_bir_lowering=False, num_devices=1)
    arrays, args = {}, []
    for name in _INS:
        a = _np.asarray(given[name])
        if name not in ("final_g", "branch_w"):
            a = a[0]
        a = _np.ascontiguousarray(a)
        arrays[f"in_{name}"] = a
        args.append(nc.dram_tensor(f"in_{name}", a.shape, _mybir.dt.from_np(a.dtype), kind="ExternalInput").ap())
    for name, a in zip(("keep_consts", "mix_consts", "iota_const"), constants()):
        arrays[f"in_{name}"] = a
        args.append(nc.dram_tensor(f"in_{name}", a.shape, _mybir.dt.from_np(a.dtype), kind="ExternalInput").ap())
    args.append(nc.dram_tensor("out_0", (S, D), F32, kind="ExternalOutput").ap())
    build(nc, *args)
    r = _run(nc, [arrays], core_ids=[0])
    return r.results[0]["out_0"].reshape(1, S, D)
```

```python
from contextlib import ExitStack

import concourse.bass as bass
from concourse import mybir

F32 = mybir.dt.float32
F32R = mybir.dt.float32r
BF16 = mybir.dt.bfloat16
I32 = mybir.dt.int32
ALU = mybir.AluOpType
ACT = mybir.ActivationFunctionType
AX_X = mybir.AxisListType.X

P = 128
D = 2048
S = 256
KT = D // P
TT = S // P
MIX = D // 4
MT = MIX // P
N_BRANCH = 4
GROUPS, PER_GROUP = 4, 8
NE = GROUPS * PER_GROUP
F = D // 4
FT = F // P
CONF_K, SC_K = 31, 3
EPS = 1e-6
POOL_WINDOWS = (2, 4, 8, 16)
OFF_A, OFF_B, OFF_C, OFF_D, OFF_G = 0, MIX, 3 * MIX, 6 * MIX, 7 * MIX

SLOT = 4096
N_SLOT = 7
W_SLOTS = 4
BW = 4
ADA_SLOTS = 2
ADA_FIRST = 4
NWIN = 64
MAXWIN = S // NWIN
PIECES = 16
RING2 = 4
PAIRS = S * 2
PADDED = PAIRS + NWIN
MAXPASS = NE + (PAIRS - 1) // (NWIN + 1)
NPT = MAXPASS + 1

C_N1, C_ADA, C_N2 = 0, 16, 112
C_PS, C_DWB, C_LNG, C_LNB, C_SCW = 128, 144, 148, 152, 156
C_DW = 168
N_COL = C_DW + CONF_K * MT
SH1, SC1, GT1, SH2, SC2, GT2 = range(6)

K_ID, K_ONE, K_TRI, K_IO8 = 0, 128, 256, 384
K_II, K_IDX, K_PASS = 400, 464, 465
N_KEEP = K_PASS + MAXPASS
N_MIXC = 1024 * 3 + 256


def build(nc, x, c, ada_w, ada_b, norm1_g, w_in, pool_w, pool_scale, conf_dw_w, conf_dw_b, conf_ln_g,
          conf_ln_b, branch_w, sc_conv_w, w_o, norm2_g, rg_w, rg_b, re_w, re_b, exp_w1, exp_w3,
          exp_w2, final_g, keep_consts, mix_consts, iota_const, out):
    with ExitStack() as ctx:
        def sb(name, shape, dt=F32):
            return ctx.enter_context(nc.sbuf_tensor(name, shape, dt))

        def sem(name):
            return ctx.enter_context(nc.semaphore(name))

        base = (nc.sbuf_base + 31) // 32 * 32
        ring = sb("ring", [P, N_SLOT, SLOT])
        r_h = sb("r_h", [P, KT * S])
        r_b = sb("r_b", [P, KT * S])
        r_m = sb("r_m", [P, 4096 + 2048 + 2176 + 2048])
        r_c = sb("r_c", [P, N_MIXC])
        keep = sb("keep", [P, N_KEEP])
        col = sb("col", [P, N_COL])
        mod = sb("mod", [P, 6, KT])
        scale1 = sb("scale1", [P, KT])
        scale2 = sb("scale2", [P, KT])
        ccol = sb("ccol", [P, KT])
        stat = sb("stat", [P, 32])

        def slot(s):
            return ring[:, s, :]

        hT = r_h[:, :].rearrange("p (c t) -> p c t", c=KT)
        x1 = r_h[:, :].rearrange("p (t d) -> p t d", t=TT)
        brT = r_b[:, :].rearrange("p (b c t) -> p b c t", b=N_BRANCH, c=MT)
        xn2 = r_b[:, :].rearrange("p (t d) -> p t d", t=TT)
        mergedT = r_m[:, 0:4096].rearrange("p (c t) -> p c t", c=KT)
        x_in = r_m[:, 0:4096].rearrange("p (t d) -> p t d", t=TT)
        h2T = mergedT
        tmp = [r_m[:, 4096:5120], r_m[:, 5120:6144]]
        gt1row = r_m[:, 4096:6144]
        vpad = r_m[:, 6144:6144 + MT * (S + CONF_K - 1)].rearrange("p (c t) -> p c t", c=MT)
        o = 6144 + MT * (S + CONF_K - 1)
        cxpad = r_m[:, o:o + MT * (S + SC_K - 1)].rearrange("p (c t) -> p c t", c=MT)
        pq = r_m[:, 6144:6144 + 2048].rearrange("p (q n) -> p q n", q=4)
        diag = r_m[:, 6144:6144 + 2048].rearrange("p (c k) -> p c k", c=KT)
        junk = r_m[:, 6144:6144 + 2048]
        acc = r_m[:, 8320:8320 + 2048]
        iota = r_m[:, 8320:8320 + 512]
        YS = r_m[:, 0:KT * PADDED].rearrange("p (c j) -> p c j", c=KT)
        e0 = KT * PADDED
        rw = r_m[:, e0:e0 + KT * 36].rearrange("p (c n) -> p c n", c=KT)
        silu_sb = r_m[:, e0 + 576:e0 + 832]
        pool_c = r_c[:, 0:2048].rearrange("p (s q t) -> p s q t", s=TT, q=4)
        dftp = r_c[:, 2048:3072].rearrange("p (s n) -> p s n", s=TT)
        dftc = r_c[:, 3072:3328]
        def at(name, shape, dt, offset):
            return nc.alloc_sbuf_tensor_at(name, shape, dt, offset=base + offset)

        def chunk(s):
            return ring[:, s // 2, (s % 2) * 2048:(s % 2 + 1) * 2048]

        w_hi = at("w_hi", [P, 2, 1024], F32R, 65536)
        w_lo = at("w_lo", [P, 2, 1024], F32R, 73728)
        xe = at("xe", [P, KT, 2 * NWIN], F32R, 81920)
        xparts = at("xparts", [P, 3, TT, D], BF16, 90112)
        sel = r_c[:, 0:576].bitcast(BF16).rearrange("p (t j) -> p t j", t=TT)
        sel_e = r_c[:, 576:640].bitcast(BF16).rearrange("p (t n) -> p t n", t=TT)
        wT = r_c[:, 640:1664].rearrange("p (i t) -> p i t", i=4)
        hid = r_c[:, 1664:2176].rearrange("p (f n) -> p f n", f=FT)
        xs = r_c[:, 2176:3200].rearrange("p (c n) -> p c n", c=KT)
        h_sb = [r_b[:, 0:512], r_b[:, 512:1024]]
        selw = r_b[:, 1024:3072]
        fgrow = r_b[:, 2048:4096]
        squares = r_b[:, 0:2048]
        remain = r_b
        ii = keep[:, K_II:K_II + 64]
        ident, ones, tri = keep[:, 0:128], keep[:, 128:256], keep[:, 256:384]
        io8 = keep[:, 384:400].rearrange("p (t e) -> p t e", t=TT)
        prow = ring[:, 0, 0:384].rearrange("p (a b) -> p a b", a=3)
        crow = ring[0:KT, 0, 384:512]

        lg = sb("lg", [P, TT, 36])
        lrow = sb("lrow", [1, 36])
        ra = sb("ra", [P, TT, 4, PER_GROUP])
        m1 = sb("m1", [P, TT, 4, PER_GROUP])
        m2 = sb("m2", [P, TT, 4, PER_GROUP])
        r8 = sb("r8", [P, TT, 5, PER_GROUP])
        rs = sb("rs", [P, 16, TT])
        ct = sb("ct", [32, 2, P])
        st = sb("st", [P, 3, NE])
        etab = sb("etab", [1, NPT], I32)
        otab = sb("otab", [1, NPT + 1], I32)
        ntab = sb("ntab", [1, 1], I32)
        ec = sb("ec", [32, 16])
        eh = sb("eh", [32, 3, MAXPASS])

        ps = ctx.enter_context(nc.psum_tensor("ps", [P, 8, 512], F32))

        def tiles(b, n=2):
            return ps[:, b:b + n, :].rearrange("p b (h t) -> p (b h) t", t=S)

        const_in = sem("const_in")
        mixc_in = sem("mixc_in")
        x_loaded = sem("x_loaded")
        ada_in = [sem(f"ada_in{i}") for i in range(ADA_FIRST)]
        ada2_in = [sem(f"ada2_in{i}") for i in range(ADA_SLOTS)]
        w_in_sem = [sem(f"w_in_sem{i}") for i in range(W_SLOTS)]
        w_used = sem("w_used")
        bw_in = sem("bw_in")
        cols_t = sem("cols_t")
        cols_ready = sem("cols_ready")
        xn_ready = sem("xn_ready")
        xT_done = sem("xT_done")
        xT_saved = sem("xT_saved")
        summed = sem("summed")
        mod_ready = sem("mod_ready")
        h_ready = sem("h_ready")
        unit_saved = sem("unit_saved")
        y_done = sem("y_done")
        y_saved = sem("y_saved")
        conv_done = sem("conv_done")
        ln_sum = sem("ln_sum")
        ln_step = sem("ln_step")
        sc_done = sem("sc_done")
        conf_ready = sem("conf_ready")
        pool_done = sem("pool_done")
        pool_ready = sem("pool_ready")
        dft_done = sem("dft_done")
        dft_saved = sem("dft_saved")
        chain_v = sem("chain_v")
        chain_a = sem("chain_a")
        inv_ready = sem("inv_ready")
        root_done = sem("root_done")
        diag_ready = sem("diag_ready")
        row_done = sem("row_done")
        row_saved = sem("row_saved")
        x_again = sem("x_again")
        iota_in = sem("iota_in")
        wo_done = sem("wo_done")
        x1_ready = sem("x1_ready")
        xn2_ready = sem("xn2_ready")
        h2_t = sem("h2_t")
        h2_ready = sem("h2_ready")
        logit_done = sem("logit_done")
        r_exp = sem("r_exp")
        r_ask = sem("r_ask")
        mask_ready = sem("mask_ready")
        pos_done = sem("pos_done")
        cnt_ready = sem("cnt_ready")
        start_done = sem("start_done")
        table_ready = sem("table_ready")
        selw_ready = sem("selw_ready")
        selw_t = sem("selw_t")
        wT_ready = sem("wT_ready")
        w13_in = [sem(f"w13_in{i}") for i in range(RING2)]
        w2_in = [sem(f"w2_in{i}") for i in range(RING2)]
        hi_done = sem("hi_done")
        lo_done = sem("lo_done")
        piece_used = sem("piece_used")
        w2_used = sem("w2_used")
        sel_ready = sem("sel_ready")
        gathered = sem("gathered")
        xe_step = sem("xe_step")
        xs_ready = sem("xs_ready")
        xhi_done = sem("xhi_done")
        xe_ready = sem("xe_ready")
        h1_saved = sem("h1_saved")
        h3_saved = sem("h3_saved")
        t1_done = sem("t1_done")
        t3_done = sem("t3_done")
        silu_done = sem("silu_done")
        hid_ready = sem("hid_ready")
        ye_saved = sem("ye_saved")
        parts_sub = sem("parts_sub")
        parts_act = sem("parts_act")
        col_done = sem("col_done")
        pass_hot = sem("pass_hot")
        pass_done = sem("pass_done")
        yT_done = sem("yT_done")
        yT_savedA = sem("yT_savedA")
        yT_savedV = sem("yT_savedV")
        comb_done = sem("comb_done")
        x2_ready = sem("x2_ready")
        sq_done = sem("sq_done")
        fin_ready = sem("fin_ready")
        fg_in = sem("fg_in")
        out_done = sem("out_done")
        acc_step = sem("acc_step")
        merge_step = sem("merge_step")

        ada_v = ada_w.rearrange("(k p) n -> p k n", p=P)
        win_v = w_in.rearrange("(k p) n -> p k n", p=P)
        wo_v = w_o.rearrange("(k p) n -> p k n", p=P)
        br_v = branch_w.rearrange("b (k p) n -> b p k n", p=P)
        x_v = x.rearrange("(t p) d -> p t d", p=P)
        out_v = out.rearrange("(t p) d -> p t d", p=P)
        e1_v = exp_w1.rearrange("e (k p) n -> e p k n", p=P)
        e3_v = exp_w3.rearrange("e (k p) n -> e p k n", p=P)
        e2_v = exp_w2.rearrange("e (k p) n -> e p k n", p=P)

        UNIT_COLS = [OFF_B + MIX, OFF_B, OFF_C + MIX, OFF_C + 2 * MIX, OFF_C, OFF_D, OFF_A]
        N_UNIT = len(UNIT_COLS)
        G0 = 2 * N_UNIT
        ADA0 = 16
        WO0 = G0 + N_BRANCH * 8
        UNITS = N_UNIT + 16

        def u_bank(n):
            return 4 * (n % 2)

        def y_bank(n):
            return 4 * (n % 2) + 2

        block = ctx.enter_context(nc.Block())

        @block.sync
        def _(sp):
            def load_ada(v, k, s, done):
                sp.dma_start(slot(s).rearrange("p (k n) -> p k n", k=2),
                             ada_v[:, 2 * k:2 * k + 2, bass.ds(v * D, D)]).then_inc(done, 16)

            def load_w(q, half, first):
                sp.dma_start(slot(q % W_SLOTS).rearrange("p (k n) -> p k n", k=8),
                             win_v[:, 8 * half:8 * half + 8, bass.ds(first, MIX)]
                             ).then_inc(w_in_sem[q % W_SLOTS], 16)

            sp.dma_start(x_in, x_v).then_inc(x_loaded, 16)
            for n in range(ADA0):
                if n >= ADA_FIRST:
                    sp.wait_ge(acc_step, 2 * (n - ADA_FIRST + 1))
                load_ada(n // 8, n % 8, 3 + n % ADA_FIRST, ada_in[n % ADA_FIRST])
            sp.wait_ge(cols_ready, 2)
            for q in range(G0):
                if q == 3:
                    sp.wait_ge(acc_step, 2 * (13))
                if q >= W_SLOTS:
                    sp.wait_ge(w_used, q - W_SLOTS + 1)
                load_w(q, q % 2, UNIT_COLS[q // 2])

            def gate_loads(g, i):
                for j in range(4):
                    if j == 0 and g is None:
                        sp.wait_ge(acc_step, 2 * (14))
                        sp.dma_start(slot(BW)[:, 0:2048].rearrange("p (q n) -> p q n", q=4),
                                     pool_w.rearrange("q c n -> c q n")).then_inc(bw_in, 16)
                    elif j % 2 == 0 and g is not None:
                        sp.wait_ge(y_done, 4 * g + j)
                        sp.dma_start(slot(BW).rearrange("p (k n) -> p k n", k=4),
                                     br_v[bass.ds(g - 1, 1), :, :, j * MIX:(j + 2) * MIX]
                                     .rearrange("b p k n -> (b p) k n")).then_inc(bw_in, 16)
                    for half in range(2):
                        q = 2 * j + half
                        sp.wait_ge(w_used, G0 + q - W_SLOTS + 1 + 8 * i)
                        load_w(G0 + q, half, OFF_G + j * MIX + i * D)
                    for k in (2 * j, 2 * j + 1):
                        sp.wait_ge(acc_step, 2 * (ADA0 + k - ADA_SLOTS + 1 + 8 * i))
                        load_ada(2 + i, k, 5 + k % 2, ada2_in[k % 2])

            gate_loads(None, 0)
            with sp.Fori(1, N_BRANCH) as g:
                gate_loads(g, g)
            for n in range(8):
                if n == 2:
                    sp.wait_ge(w_used, 2 * (UNITS))
                    sp.dma_start(x1, x_v).then_inc(x_again, 16)
                if n == 3:
                    sp.wait_ge(mod_ready, 6)
                    sp.dma_start(iota, iota_const).then_inc(iota_in, 16)
                    sp.dma_start(rw[:, :, 0:4], rg_w.rearrange("(k p) n -> p k n", p=P)).then_inc(iota_in, 16)
                    sp.dma_start(rw[:, :, 4:36], re_w.rearrange("(k p) n -> p k n", p=P)).then_inc(iota_in, 16)
                sp.wait_ge(w_used, WO0 + n - W_SLOTS + 1)
                sp.dma_start(slot((WO0 + n) % W_SLOTS).rearrange("p (k n) -> p k n", k=2),
                             wo_v[:, 2 * n:2 * n + 2, :]).then_inc(w_in_sem[(WO0 + n) % W_SLOTS], 16)

            def load_w13(e, c, p):
                src = (e1_v, e3_v)[c // 4][bass.ds(e, 1), :, 4 * (c % 4):4 * (c % 4) + 4, :]
                sp.dma_start(chunk(c % 4).rearrange("p (k n) -> p k n", k=4), src.rearrange("e p k n -> (e p) k n")
                             ).then_inc(w13_in[c % 4], 16)

            def load_w2(e, j):
                src = e2_v[bass.ds(e, 1), :, j, :]
                sp.dma_start(chunk(4 + j), src.rearrange("e p n -> (e p) n")).then_inc(w2_in[j], 16)

            for s in (2, 3, 0, 1):
                if s == 1:
                    sp.wait_ge(wo_done, 8)
                else:
                    sp.wait_ge(w_used, WO0 + 5 + (s - 2) % 4)
                for h in range(2):
                    if s < 2:
                        load_w13(0, 2 * s + h, 0)
                    else:
                        load_w2(0, 2 * (s - 2) + h)
            sp.wait_ge(table_ready, 1)
            n_pass = sp.value_load(ntab[0:1, 0:1], min_val=NE, max_val=MAXPASS)
            with sp.Fori(0, MAXPASS) as p:
                with sp.If(p < n_pass):
                    e = sp.value_load(etab[0:1, bass.ds(p, 1)], min_val=0, max_val=NE - 1)
                    with sp.If(p > 0):
                        for c in range(4):
                            sp.wait_ge(lo_done, 16 * p + 2 * c + 2)
                            load_w13(e, c, p)
                    for c in range(4, 8):
                        sp.wait_ge(lo_done, 16 * p + 2 * c + 2)
                        load_w13(e, c, p)
                    with sp.If(p > 0):
                        for j in range(4):
                            sp.wait_ge(w2_used, 4 * p + j + 1)
                            load_w2(e, j)
            sp.wait_ge(selw_t, 1)
            sp.dma_start(fgrow, final_g.rearrange("(o d) -> o d", o=1).broadcast_to([P, D])).then_inc(fg_in, 16)
            for t in range(TT):
                sp.wait_ge(fin_ready, t + 1)
                sp.dma_start(out_v[:, t, :], slot(2)[:, t * D:(t + 1) * D]).then_inc(out_done, 16)
            sp.wait_ge(out_done, 32)

        @block.gpsimd
        def _(pool):
            pool.dma_start(r_c[:, :], mix_consts).then_inc(mixc_in, 16)
            flat = "p t d -> p (t d)"
            for i in range(2):
                pool.wait_ge(parts_act, i + 1)
                dst = remain[:, :] if i == 0 else xparts[:, 2, :, :].rearrange(flat)
                if i == 0:
                    pool.wait_ge(h2_t, 8)
                nc.gpsimd.tensor_tensor(dst, r_b[:, :], xparts[:, i, :, :].rearrange(flat),
                                        ALU.subtract).then_inc(parts_sub, 1)

        @block.tensor
        def _(pe):
            mm = nc.tensor.matmul

            pe.wait_ge(const_in, 16 * 13)
            nc.tensor.transpose(ps[:, 7, 0:128], prow[:, 0, :], ident)
            nc.tensor.transpose(ps[:, 7, 128:168], prow[0:40, 1, :], ident[0:40, 0:40])
            nc.tensor.transpose(ps[:, 7, 168:168 + CONF_K * MT], prow[0:CONF_K * MT, 2, :],
                                ident[0:CONF_K * MT, 0:CONF_K * MT])
            nc.tensor.transpose(ps[:, 7, 320:336], crow, ident[0:KT, 0:KT]).then_inc(cols_t, 1)
            pe.wait_ge(cols_ready, 2)
            for t in range(TT):
                pe.wait_ge(xn_ready, t + 1)
            for b in range(8):
                for k in (2 * b, 2 * b + 1):
                    for t in range(TT):
                        last = nc.tensor.transpose(tiles(b, 1)[:, k % 2, t * P:(t + 1) * P],
                                                   x_in[:, t, k * P:(k + 1) * P], ident)
                last.then_inc(xT_done, 1)

            def sum_ada(n, bank):
                pe.wait_ge(acc_step, 16 * (n + 1))
                for k in range(KT):
                    last = mm(ps[:, bank, k:k + 1], acc[:, k * P:(k + 1) * P], ones[:, 0:1], start=True, stop=True)
                last.then_inc(summed, 1)

            pe.wait_ge(xT_saved, 8)
            sum_ada(SH1, 2)
            pe.wait_ge(mod_ready, 1)
            sum_ada(SC1, 2)

            def unit_T(n, loaded):
                u = tiles(u_bank(n))
                for half in range(2):
                    q = (2 * n + half) % W_SLOTS
                    pe.wait_ge(w_in_sem[q], loaded)
                    w = slot(q).rearrange("p (k n) -> p k n", k=8)
                    for kk in range(8):
                        k = 8 * half + kk
                        if n == 0:
                            pe.wait_ge(h_ready, k + 1)
                        for f in range(4):
                            last = mm(u[:, f, :], w[:, kk, f * P:(f + 1) * P], hT[:, k, :],
                                      start=(k == 0 and f % 2 == 0), stop=(k == KT - 1), skip_group_check=True)
                    last.then_inc(w_used, 1)

            def unit_N(n, loaded):
                for half in range(2):
                    q = (2 * n + half) % W_SLOTS
                    pe.wait_ge(w_in_sem[q], loaded)
                    w = slot(q).rearrange("p (k n) -> p k n", k=8)
                    for kk in range(8):
                        k = 8 * half + kk
                        for t in range(TT):
                            last = mm(ps[:, u_bank(n) + t, :], hT[:, k, t * P:(t + 1) * P], w[:, kk, :],
                                      start=(k == 0), stop=(k == KT - 1))
                    last.then_inc(w_used, 1)

            pe.wait_ge(mod_ready, 2)
            for n in range(5):
                if n >= 2:
                    pe.wait_ge(unit_saved, n - 1)
                unit_T(n, 16 * (n // 2 + 1))
                if n == 3:
                    pe.wait_ge(conv_done, 1)
                    for m in range(MT):
                        last = mm(ps[:, y_bank(n), 0:S], ones, brT[:, 1, m, :], start=(m == 0), stop=(m == MT - 1))
                    last.then_inc(ln_sum, 1)
                if n == 4:
                    pe.wait_ge(ln_step, 1)
                    pe.wait_ge(sc_done, 1)
                    for m in range(MT):
                        last = mm(ps[:, y_bank(n), 0:S], ones, pq[:, m, 0:S], start=(m == 0), stop=(m == MT - 1))
                    last.then_inc(ln_sum, 1)
            for n in (5, 6):
                pe.wait_ge(unit_saved, n - 1)
                unit_N(n, 16 * (n // 2 + 1))

            pe.wait_ge(unit_saved, 6)
            pe.wait_ge(ln_step, 2)
            pe.wait_ge(mixc_in, 16)
            for q in range(4):
                b = (2, 3, 6, 7)[q]
                for t in range(TT):
                    last = mm(ps[:, b, :], tmp[0][:, t * MIX + q * P:t * MIX + (q + 1) * P], dftp[:, t, :],
                              start=(t == 0), stop=(t == TT - 1))
                last.then_inc(dft_done, 1)
            pe.wait_ge(unit_saved, 7)
            pt = tiles(0)
            for q in range(4):
                for t in range(TT):
                    last = mm(pt[:, q, :], tmp[1][:, t * MIX + q * P:t * MIX + (q + 1) * P], pool_c[:, t, q, :],
                              start=(t == 0), stop=(t == TT - 1))
            last.then_inc(pool_done, 1)

            def gate_y(n, kts, lhs, rhs):
                y = tiles(y_bank(n))
                for f in range(4):
                    for k in range(kts):
                        last = mm(y[:, f, :], lhs(k, f), rhs(k), start=(k == 0), stop=(k == kts - 1))
                return last

            pw = slot(BW)[:, 0:2048].rearrange("p (q n) -> p q n", q=4)
            bw = slot(BW).rearrange("p (k n) -> p k n", k=4)
            for j in range(4):
                n = N_UNIT + j
                if j == 1:
                    pe.wait_ge(pool_ready, 1)
                elif j >= 2:
                    pe.wait_ge(unit_saved, n - 1)
                unit_T(n, 16 * (n // 2 + 1))
                if j == 0:
                    pe.wait_ge(bw_in, 16)
                    pe.wait_ge(dft_saved, 4)
                    pe.wait_ge(pool_ready, 1)
                if j >= 2:
                    pe.wait_ge(y_saved, j - 1)
                if j == 1:
                    pe.wait_ge(dft_saved, 5)
                last = gate_y(n, 1, lambda k, f: pw[:, j, f * P:(f + 1) * P], lambda k: brT[:, 0, j, :])
                last.then_inc(y_done, 1)
                if j == 0:
                    for q in range(4):
                        mm(tiles(2)[:, q, :], dftc[:, 0:128], pq[:, q, 0:S], start=True, stop=False)
                        last = mm(tiles(2)[:, q, :], dftc[:, 128:256], pq[:, q, S:2 * S], start=False, stop=True)
                    last.then_inc(dft_done, 1)
            with pe.Fori(1, N_BRANCH) as g:
                for j in range(4):
                    n = N_UNIT + j
                    if j == 0:
                        pe.wait_ge(y_saved, 4 * g - 1)
                        pe.wait_ge(acc_step, 16 * (2 + g))
                        for k in range(KT):
                            last = mm(ps[:, y_bank(n), k:k + 1], acc[:, k * P:(k + 1) * P], ones[:, 0:1],
                                      start=True, stop=True)
                        last.then_inc(summed, 1)
                    pe.wait_ge(unit_saved, N_UNIT - 1 + j + 4 * g)
                    unit_T(n, 16 * (n // 2 + 1) + 32 * g)
                    if j == 0:
                        pe.wait_ge(mod_ready, 2 + g)
                    if j % 2 == 0:
                        pe.wait_ge(bw_in, 16 * (2 * (g - 1) + j // 2 + 2))
                    pe.wait_ge(y_saved, 4 * g + j - 1)
                    last = gate_y(n, MT, lambda k, f: bw[:, k, (j % 2) * MIX + f * P:(j % 2) * MIX + (f + 1) * P],
                                  lambda k: r_b[:, bass.ds(g * MT * S + k * S, S)])
                    last.then_inc(y_done, 1)

            pe.wait_ge(diag_ready, 1)
            pe.wait_ge(y_saved, 15)
            pe.wait_ge(unit_saved, UNITS - 1)
            for n in range(4):
                last = mm(ps[:, 4 + n, :], ones, diag[:, 4 * n:4 * n + 4, :], start=True, stop=True)
            last.then_inc(row_done, 1)
            pe.wait_ge(y_saved, 16)
            sum_ada(5, 2)
            pe.wait_ge(mod_ready, 6)
            pe.wait_ge(unit_saved, UNITS)
            pe.wait_ge(row_saved, 1)
            for i in range(8):
                s = (WO0 + i) % W_SLOTS
                pe.wait_ge(w_in_sem[s], 16 * ((WO0 + i) // W_SLOTS + 1))
                w = slot(s).rearrange("p (k n) -> p k n", k=2)
                for t in range(TT):
                    for n in range(4):
                        for kk in range(2):
                            k = 2 * i + kk
                            last = mm(ps[:, 4 * t + n, :], mergedT[:, k, t * P:(t + 1) * P],
                                      w[:, kk, n * MIX:(n + 1) * MIX], start=(k == 0), stop=(k == KT - 1))
                        if i == 7:
                            last.then_inc(wo_done, 1)
                if i < 7:
                    last.then_inc(w_used, 1)

            pe.wait_ge(x1_ready, 8)
            for t in range(TT):
                pe.wait_ge(xn2_ready, t + 1)
            for b in range(8):
                for k in (2 * b, 2 * b + 1):
                    for t in range(TT):
                        last = nc.tensor.transpose(tiles(b, 1)[:, k % 2, t * P:(t + 1) * P],
                                                   xn2[:, t, k * P:(k + 1) * P], ident)
                last.then_inc(h2_t, 1)
            pe.wait_ge(h2_ready, 16)
            pe.wait_ge(iota_in, 48)
            for t in range(TT):
                for k in range(KT):
                    mm(ps[:, 0, t * 36:(t + 1) * 36], h2T[:, k, t * P:(t + 1) * P], rw[:, k, :],
                       start=(k == 0), stop=False)
                last = mm(ps[:, 0, t * 36:(t + 1) * 36], ones[0:1, :], lrow[0:1, :], start=False, stop=True)
            last.then_inc(logit_done, 1)
            pe.wait_ge(mask_ready, 1)
            mall = ra[:, :, :, :].rearrange("p t g e -> p t (g e)")
            mm(ps[:, 1, 0:32], tri, mall[:, 0, :], start=True, stop=True)
            mm(ps[:, 1, 32:64], ones, mall[:, 0, :], start=True, stop=False)
            mm(ps[:, 1, 32:64], tri, mall[:, 1, :], start=False, stop=True)
            mm(ps[0:32, 2, 0:P], mall[:, 0, :], ones, start=True, stop=False)
            mm(ps[0:32, 2, 0:P], mall[:, 1, :], ones, start=False, stop=True).then_inc(pos_done, 1)
            pe.wait_ge(cnt_ready, 1)
            mm(ps[:, 3, 0:32], ct[:, 0, :], tri[0:32, 0:32], start=True, stop=True)
            mm(ps[0:32, 3, 32:33], tri[0:32, 0:32], ct[:, 0, 0:1], start=True, stop=True)
            mm(ps[0:32, 3, 33:34], tri[0:32, 0:32], ct[:, 1, 0:1], start=True, stop=True).then_inc(start_done, 1)
            pe.wait_ge(pass_hot, 1)
            mm(ps[0:1, 2, 0:MAXPASS], keep[0:32, K_IDX:K_IDX + 1], eh[:, 0, :], start=True, stop=True)
            mm(ps[0:1, 2, 64:64 + MAXPASS], ones[0:32, 0:1], eh[:, 1, :], start=True, stop=True)
            mm(ps[0:1, 2, 128:129], ones[0:32, 0:1], ct[:, 1, 0:1], start=True, stop=True).then_inc(pass_done, 1)
            gat = ps[:, 0:2, :].rearrange("p b (c n) -> p (b c) n", n=NWIN)
            ye = ps[:, 4:8, :].rearrange("p b (c n) -> p (b c) n", n=P)

            def gather():
                for k in range(KT):
                    for t in range(TT):
                        for i in range(3):
                            last = mm(gat[:, k, :], xparts[:, i, t, k * P:(k + 1) * P], sel_e[:, t, :],
                                      start=(t == 0 and i == 0), stop=(t == TT - 1 and i == 2))
                last.then_inc(gathered, 1)

            def turn(m):
                pe.wait_ge((h1_saved, h3_saved)[m], p + 1)
                for f in range(FT):
                    last = mm(ps[:, 2 + m, f * NWIN:(f + 1) * NWIN], h_sb[m][:, f * P:(f + 1) * P], ii,
                              start=True, stop=True)
                last.then_inc((t1_done, t3_done)[m], 1)

            pe.sem_inc(piece_used, 2)
            pe.sem_inc(w2_used, 4)
            pe.wait_ge(sel_ready, 1)
            pe.wait_ge(parts_sub, 2)
            gather()
            pe.wait_ge(selw_ready, 1)
            for i in range(4):
                for t in range(TT):
                    last = nc.tensor.transpose(tiles(4)[:, i, t * P:(t + 1) * P],
                                               selw[:, t * PAIRS + i * P:t * PAIRS + (i + 1) * P], ident)
            last.then_inc(selw_t, 1)
            pe.wait_ge(wT_ready, 1)
            n_pass = pe.value_load(ntab[0:1, 0:1], min_val=NE, max_val=MAXPASS)
            with pe.Fori(0, MAXPASS) as p:
                with pe.If(p < n_pass):
                    pe.wait_ge(xe_ready, p + 1)
                    for i in range(PIECES):
                        pe.wait_ge(lo_done, 16 * p + i + 1 + 8)
                        for kk in range(2):
                            k = 2 * (i % 8) + kk
                            for part in (w_hi, w_lo):
                                last = mm(ps[:, 2 + i // 8, :], xe[:, k, :], part[:, i % 2, kk * F:(kk + 1) * F],
                                          start=(k == 0 and part is w_hi), stop=(k == KT - 1 and part is w_lo))
                        last.then_inc(piece_used, 1)
                        if i == 11:
                            turn(0)
                    pe.wait_ge(sel_ready, p + 2)
                    gather()
                    turn(1)
                    pe.wait_ge(hid_ready, p + 1)
                    for j in range(4):
                        pe.wait_ge(w2_in[j], 16 * p + 16)
                        for m in range(KT):
                            last = mm(ye[:, m, :], chunk(4 + j)[:, m * P:(m + 1) * P], hid[:, j, :],
                                      start=(j == 0 and m % 4 == 0), stop=(j == FT - 1), skip_group_check=True)
                        last.then_inc(w2_used, 1)

            for i in range(4):
                b = 4 * (i % 2)
                if i == 0:
                    pe.wait_ge(yT_savedV, 1)
                if i >= 2:
                    pe.wait_ge(yT_savedA, i - 1)
                    pe.wait_ge(yT_savedV, i)
                for k in range(KT):
                    last = nc.tensor.transpose(ps[:, b + k // 4, (k % 4) * P:(k % 4 + 1) * P],
                                               YS[:, k, i * P:(i + 1) * P], ident)
                last.then_inc(yT_done, 1)
            yn = ring[:, 0:2, :].rearrange("p s (i d) -> p (s i) d", d=D)
            for t in range(TT):
                pe.wait_ge(yT_savedA, 3 + t if t == 0 else 4)
                pe.wait_ge(yT_savedV, 4 + t if t == 0 else 5)
                if t == 0:
                    pe.wait_ge(yT_savedA, 4)
                    pe.wait_ge(yT_savedV, 5)
                for n in range(4):
                    for i in range(4):
                        last = mm(ps[:, 4 * t + n, :], wT[:, i, t * P:(t + 1) * P], yn[:, i, n * MIX:(n + 1) * MIX],
                                  start=(i == 0), stop=(i == 3))
                    last.then_inc(comb_done, 1)

        @block.scalar
        def _(act):
            A = nc.scalar.activation
            small = [
                (keep[:, :], keep_consts), (prow[0:16, 0, :], norm1_g.rearrange("(a p) -> a p", p=P)),
                (prow[16:112, 0, :], ada_b.rearrange("(a p) -> a p", p=P)),
                (prow[112:128, 0, :], norm2_g.rearrange("(a p) -> a p", p=P)),
                (prow[0:16, 1, :], pool_scale.rearrange("(a p) -> a p", p=P)),
                (prow[16:20, 1, :], conf_dw_b.rearrange("(a p) -> a p", p=P)),
                (prow[20:24, 1, :], conf_ln_g.rearrange("(a p) -> a p", p=P)),
                (prow[24:28, 1, :], conf_ln_b.rearrange("(a p) -> a p", p=P)),
                (prow[28:40, 1, :], sc_conv_w.rearrange("j (a p) -> (j a) p", p=P)),
                (prow[0:CONF_K * MT, 2, :], conf_dw_w.rearrange("j (a p) -> (j a) p", p=P)),
                (crow, c.rearrange("(a p) -> a p", p=P)),
                (lrow[0:1, 0:4], rg_b.rearrange("(o n) -> o n", o=1)),
                (lrow[0:1, 4:36], re_b.rearrange("(o n) -> o n", o=1)),
            ]
            for dst, src in small:
                act.dma_start(dst, src).then_inc(const_in, 16)
            act.wait_ge(x_loaded, 16)
            for t in range(TT):
                last = A(r_b[:, t * D:(t + 1) * D], x_in[:, t, :], ACT.Square, accum_out=stat[:, t:t + 1])
                last.then_inc(sq_done, 1)
            act.wait_ge(inv_ready, 1)
            A(stat[:, 2:4], stat[:, 2:4], ACT.Sqrt).then_inc(root_done, 1)
            act.wait_ge(root_done, 1)
            for t in range(TT):
                A(x_in[:, t, :], x_in[:, t, :], ACT.Copy, scale=stat[:, 2 + t:3 + t]).then_inc(xn_ready, 1)
            for b in range(8):
                act.wait_ge(xT_done, b + 1)
                A(r_h[:, b * 512:(b + 1) * 512], ps[:, b, :], ACT.Copy).then_inc(xT_saved, 1)
            act.wait_ge(mod_ready, 2)
            act.wait_ge(xT_saved, 8)
            act.wait_ge(cols_ready, 3)
            for k in range(KT):
                A(hT[:, k, :], hT[:, k, :], ACT.Identity, bias=mod[:, SH1, k:k + 1],
                  scale=scale1[:, k:k + 1]).then_inc(h_ready, 1)
            act.wait_ge(w_used, 2 * (1))
            A(tmp[0], ps[:, 0:2, :], ACT.Sigmoid).then_inc(unit_saved, 1)
            act.wait_ge(w_used, 2 * (3))
            act.wait_ge(unit_saved, 2)
            A(tmp[0], ps[:, 0:2, :], ACT.Copy).then_inc(unit_saved, 1)
            act.wait_ge(conv_done, 2)
            act.wait_ge(sc_done, 1)
            A(pq[:, :, 0:S], brT[:, 1, :, :], ACT.Square).then_inc(ln_step, 1)
            act.wait_ge(inv_ready, 2)
            A(tmp[1][:, 0:S], tmp[1][:, 0:S], ACT.Sqrt).then_inc(root_done, 1)
            act.wait_ge(conv_done, 3)
            for m in range(MT):
                A(brT[:, 1, m, :], brT[:, 1, m, :], ACT.Silu, bias=col[:, C_LNB + m:C_LNB + m + 1],
                  scale=col[:, C_LNG + m:C_LNG + m + 1]).then_inc(conf_ready, 1)
            act.wait_ge(w_used, 2 * (6))
            act.wait_ge(unit_saved, 5)
            A(tmp[0], ps[:, 4:6, :], ACT.Copy).then_inc(unit_saved, 1)
            act.wait_ge(w_used, 2 * (7))
            A(tmp[1], ps[:, 0:2, :], ACT.Copy).then_inc(unit_saved, 1)
            for q in range(4):
                act.wait_ge(dft_done, q + 1)
                act.wait_ge(ln_sum, 2)
                A(pq[:, q, :], ps[:, (2, 3, 6, 7)[q], :], ACT.Copy).then_inc(dft_saved, 1)
            act.wait_ge(pool_done, 1)
            A(r_b[:, 0:1024], ps[:, 0:2, :], ACT.Copy).then_inc(pool_ready, 1)

            def gate(done, n, y_before):
                act.wait_ge(w_used, 2 * (done))
                act.wait_ge(y_saved, y_before)
                A(tmp[n % 2], ps[:, u_bank(n):u_bank(n) + 2, :], ACT.Sigmoid).then_inc(unit_saved, 1)

            for j in range(4):
                gate(N_UNIT + j + 1, N_UNIT + j, max(j - 1, 0))
                if j == 0:
                    act.wait_ge(dft_done, 5)
                    A(r_b[:, 3072:4096], ps[:, 2:4, :], ACT.Copy).then_inc(dft_saved, 1)
            with act.Fori(1, N_BRANCH) as g:
                for j in range(4):
                    gate(N_UNIT + j + 1 + 4 * g, N_UNIT + j, 4 * g + j - 1)
            act.wait_ge(row_done, 1)
            act.wait_ge(y_saved, 16)
            A(gt1row, ps[:, 4:8, :], ACT.Copy).then_inc(row_saved, 1)

            for t in range(TT):
                act.wait_ge(x1_ready, 4 * t + 4)
                act.wait_ge(sq_done, 2 + t)
                A(junk, x1[:, t, :], ACT.Square, accum_out=stat[:, 4 + t:5 + t]).then_inc(sq_done, 1)
            for t in range(TT):
                r = stat[:, 6 + t:7 + t]
                act.wait_ge(inv_ready, 3 + t)
                A(r, r, ACT.Sqrt).then_inc(root_done, 1)
                act.wait_ge(root_done, 3 + t)
                A(xn2[:, t, :], x1[:, t, :], ACT.Copy, scale=stat[:, 6 + t:7 + t]).then_inc(xn2_ready, 1)
            act.wait_ge(xn2_ready, 2)
            act.wait_ge(x1_ready, 8)
            A(xparts[:, 0, :, :], xn2, ACT.Copy).then_inc(parts_act, 1)
            for b in range(0, 8, 2):
                act.wait_ge(h2_t, b + 1)
                for k in (2 * b, 2 * b + 1):
                    A(h2T[:, k, :], tiles(b, 1)[:, k % 2, :], ACT.Identity, bias=mod[:, SH2, k:k + 1],
                      scale=scale2[:, k:k + 1]).then_inc(h2_ready, 1)
            act.wait_ge(r_ask, 1)
            A(r8[:, :, 1, 0:4], r8[:, :, 0, 0:4], ACT.Exp).then_inc(r_exp, 1)
            act.wait_ge(r_ask, 2)
            A(rs[:, 8, :], rs[:, 7, :], ACT.Exp).then_inc(r_exp, 1)
            act.wait_ge(parts_sub, 1)
            A(xparts[:, 1, :, :].rearrange("p t d -> p (t d)"), remain[:, :], ACT.Copy).then_inc(parts_act, 1)
            act.wait_ge(table_ready, 1)
            A(sel_e, sel[:, :, 0:NWIN], ACT.Copy).then_inc(sel_ready, 1)
            act.wait_ge(xs_ready, 1)
            A(xe[:, :, 0:NWIN], xs, ACT.Copy).then_inc(xhi_done, 1)
            act.wait_ge(selw_t, 1)
            A(wT[:, :, :], tiles(4), ACT.Copy).then_inc(wT_ready, 1)

            n_pass = act.value_load(ntab[0:1, 0:1], min_val=NE, max_val=MAXPASS)
            with act.Fori(0, MAXPASS) as p:
                with act.If(p < n_pass):
                    off = act.value_load(otab[0:1, bass.ds(p + 2, 1)], min_val=0, max_val=PAIRS)
                    act.wait_ge(gathered, p + 1)
                    A(sel_e, sel[:, :, bass.ds(off, NWIN)], ACT.Copy).then_inc(sel_ready, 1)
                    for i in range(PIECES):
                        if i == 10:
                            act.wait_ge(piece_used, 16 * p + 8 + 2)
                            A(h_sb[0], ps[:, 2, :], ACT.Copy).then_inc(h1_saved, 1)
                        if i == 14:
                            act.wait_ge(t1_done, p + 1)
                            A(silu_sb, ps[:, 2, 0:FT * NWIN], ACT.Silu).then_inc(silu_done, 1)
                        if i % 2 == 0:
                            act.wait_ge(w13_in[i // 2 % 4], 32 * p + 16 * (i // 8) + 16)
                        act.wait_ge(piece_used, 16 * p + i + 1)
                        A(w_hi[:, i % 2, :], chunk(i // 2 % 4)[:, (i % 2) * 1024:(i % 2 + 1) * 1024], ACT.Copy
                          ).then_inc(hi_done, 1)
                    act.wait_ge(xs_ready, p + 2)
                    A(xe[:, :, 0:NWIN], xs, ACT.Copy).then_inc(xhi_done, 1)

            yn = ring[:, 0:2, :].rearrange("p s (i d) -> p (s i) d", d=D)
            for i in range(4):
                b = 4 * (i % 2)
                act.wait_ge(yT_done, i + 1)
                A(yn[:, i, 0:1024], ps[:, b:b + 2, :], ACT.Copy).then_inc(yT_savedA, 1)
            for t in range(TT):
                for n in range(4):
                    act.wait_ge(x2_ready, 4 * t + n + 1)
                    if t:
                        act.wait_ge(sq_done, 4 + n + 1)
                    A(squares[:, n * MIX:(n + 1) * MIX], x1[:, t, n * MIX:(n + 1) * MIX], ACT.Square,
                      accum_out=stat[:, 8 + 4 * t + n:9 + 4 * t + n]).then_inc(sq_done, 1)
                act.wait_ge(inv_ready, 5 + t)
                A(stat[:, 16 + t:17 + t], stat[:, 16 + t:17 + t], ACT.Sqrt).then_inc(root_done, 1)

        @block.vector
        def _(v):
            V = nc.vector
            steps = [0]

            def step(ins):
                steps[0] += 1
                ins.then_inc(chain_v, 1)
                v.wait_ge(chain_v, steps[0])

            v.wait_ge(cols_t, 1)
            V.tensor_copy(col[:, :], ps[:, 7, 0:N_COL]).then_inc(cols_ready, 1)
            V.tensor_copy(ccol[:, :], ps[:, 7, 320:336]).then_inc(cols_ready, 1)
            v.wait_ge(cols_ready, 2)
            v.wait_ge(sq_done, 2)
            step(V.tensor_scalar(stat[:, 2:4], stat[:, 0:2], 1.0 / D, EPS, ALU.mult, ALU.add))
            V.reciprocal(stat[:, 2:4], stat[:, 2:4]).then_inc(inv_ready, 1)

            def ada_chunk(s, k, first):
                w = slot(s).rearrange("p (k n) -> p k n", k=2)
                for i in range(2):
                    kk = 2 * k + i
                    if kk == 0:
                        ins = V.tensor_scalar(acc, w[:, i, :], ccol[:, kk:kk + 1], None, ALU.mult)
                    else:
                        ins = V.scalar_tensor_tensor(out=acc, in0=w[:, i, :], scalar=ccol[:, kk:kk + 1], in1=acc,
                                                     op0=ALU.mult, op1=ALU.add)
                    yield ins



            for n in range(ADA0):
                v.wait_ge(ada_in[n % ADA_FIRST], 16 * (n // ADA_FIRST + 1))
                if n == 8:
                    v.wait_ge(summed, 1)
                for i, ins in enumerate(ada_chunk(3 + n % ADA_FIRST, n % 8, n % 8 == 0)):
                    ins.then_inc(acc_step, 1)
                    v.wait_ge(acc_step, 2 * n + i + 1)
                if n % 8 == 7:
                    m = n // 8
                    v.wait_ge(summed, m + 1)
                    V.tensor_tensor(mod[:, m, :], ps[:, 2, 0:KT], col[:, C_ADA + m * KT:C_ADA + (m + 1) * KT],
                                    ALU.add).then_inc(mod_ready, 1)
            v.wait_ge(mod_ready, 2)
            V.scalar_tensor_tensor(out=scale1[:, :], in0=mod[:, SC1, :], scalar=1.0, in1=col[:, C_N1:C_N1 + KT],
                                   op0=ALU.add, op1=ALU.mult).then_inc(cols_ready, 1)
            V.memset(r_m[:, 6144:6144 + MT * (S + CONF_K - 1) + MT * (S + SC_K - 1)], 0.0).then_inc(cols_ready, 1)
            v.wait_ge(cols_ready, 4)

            v.wait_ge(w_used, 2 * (2))
            v.wait_ge(unit_saved, 1)
            step(V.tensor_tensor(vpad[:, :, 15:15 + S], tiles(4), tmp[0].rearrange("p (c t) -> p c t", c=MT), ALU.mult))
            v.sem_inc(unit_saved, 1)
            c0 = steps[0]
            for j in range(CONF_K):
                for m in range(MT):
                    wcol = col[:, C_DW + j * MT + m:C_DW + j * MT + m + 1]
                    if j:
                        v.wait_ge(chain_v, c0 + (j - 1) * MT + m + 1)
                        ins = V.scalar_tensor_tensor(out=brT[:, 1, m, :], in0=vpad[:, m, j:j + S], scalar=wcol,
                                                     in1=brT[:, 1, m, :], op0=ALU.mult, op1=ALU.add)
                    else:
                        ins = V.tensor_scalar(brT[:, 1, m, :], vpad[:, m, 0:S], wcol,
                                              col[:, C_DWB + m:C_DWB + m + 1], ALU.mult, ALU.add)
                    ins.then_inc(chain_v, 1)
            steps[0] += CONF_K * MT
            v.wait_ge(chain_v, steps[0])
            v.sem_inc(conv_done, 1)

            v.wait_ge(w_used, 2 * (4))
            v.wait_ge(unit_saved, 3)
            step(V.tensor_tensor(cxpad[:, :, 1:1 + S], tiles(4), tmp[0].rearrange("p (c t) -> p c t", c=MT), ALU.mult))
            v.sem_inc(unit_saved, 1)
            z = tmp[0].rearrange("p (c t) -> p c t", c=MT)
            c0 = steps[0]
            for j in range(SC_K):
                for m in range(MT):
                    wcol = col[:, C_SCW + j * MT + m:C_SCW + j * MT + m + 1]
                    if j:
                        v.wait_ge(chain_v, c0 + (j - 1) * MT + m + 1)
                        ins = V.scalar_tensor_tensor(out=z[:, m, :], in0=cxpad[:, m, j:j + S], scalar=wcol,
                                                     in1=z[:, m, :], op0=ALU.mult, op1=ALU.add)
                    else:
                        ins = V.tensor_scalar(z[:, m, :], cxpad[:, m, 0:S], wcol, None, ALU.mult)
                    ins.then_inc(chain_v, 1)
            steps[0] += SC_K * MT
            v.wait_ge(chain_v, steps[0])
            v.sem_inc(sc_done, 1)

            lb = y_bank(3)
            v.wait_ge(ln_sum, 1)
            mrow = tmp[1][:, 0:S]
            step(V.tensor_scalar(mrow, ps[:, lb, 0:S], 1.0 / MIX, None, ALU.mult))
            V.tensor_tensor(brT[:, 1, :, :], brT[:, 1, :, :], mrow.unsqueeze(1).broadcast_to([P, MT, S]),
                            ALU.subtract).then_inc(conv_done, 1)
            v.wait_ge(w_used, 2 * (5))
            V.tensor_tensor(brT[:, 2, :, :], tiles(0), z, ALU.mult).then_inc(unit_saved, 1)
            v.wait_ge(ln_sum, 2)
            step(V.tensor_scalar(mrow, ps[:, y_bank(4), 0:S], 1.0 / MIX, EPS, ALU.mult, ALU.add))
            v.sem_inc(ln_step, 1)
            V.reciprocal(mrow, mrow).then_inc(inv_ready, 1)
            v.wait_ge(root_done, 2)
            V.tensor_tensor(brT[:, 1, :, :], brT[:, 1, :, :], mrow.unsqueeze(1).broadcast_to([P, MT, S]),
                            ALU.mult).then_inc(conv_done, 1)

            def ada_two(i, j):
                for k in (2 * j, 2 * j + 1):
                    if k == 0:
                        v.wait_ge(summed, 2 + i)
                    v.wait_ge(ada2_in[k % 2], 16 * (k // 2 + 1) + 64 * i)
                    for a, ins in enumerate(ada_chunk(5 + k % 2, k, k == 0)):
                        ins.then_inc(acc_step, 1)
                        v.wait_ge(acc_step, 2 * ADA0 + 2 * k + a + 1 + 16 * i)

            for j in range(4):
                n = N_UNIT + j
                ada_two(0, j)
                v.wait_ge(y_done, j + 1)
                v.wait_ge(unit_saved, n + 1)
                for f in range(4):
                    ins = V.scalar_tensor_tensor(out=mergedT[:, 4 * j + f, :], in0=tiles(y_bank(n))[:, f, :],
                                                 scalar=col[:, C_PS + 4 * j + f:C_PS + 4 * j + f + 1],
                                                 in1=tmp[n % 2][:, f * S:(f + 1) * S], op0=ALU.mult, op1=ALU.mult)
                ins.then_inc(y_saved, 1)
            with v.Fori(1, N_BRANCH) as g:
                v.wait_ge(summed, 2 + g)
                V.tensor_tensor(mod[:, bass.ds(g + 1, 1), :].rearrange("p a k -> p (a k)"), ps[:, y_bank(N_UNIT), 0:KT],
                                col[:, bass.ds(C_ADA + (g + 1) * KT, KT)], ALU.add).then_inc(mod_ready, 1)
                for j in range(4):
                    n = N_UNIT + j
                    ada_two(g, j)
                    v.wait_ge(y_done, 4 * g + j + 1)
                    v.wait_ge(unit_saved, n + 1 + 4 * g)
                    gy = tmp[n % 2]
                    V.tensor_tensor(gy, ps[:, y_bank(n):y_bank(n) + 2, :].rearrange("p b n -> p (b n)"), gy,
                                    ALU.mult).then_inc(merge_step, 1)
                    v.wait_ge(merge_step, 4 * g + j - 3)
                    v.wait_ge(y_saved, 4 * g + j - 3)
                    m = r_m[:, j * 1024:(j + 1) * 1024]
                    V.tensor_tensor(m, m, gy, ALU.add).then_inc(y_saved, 1)
            v.wait_ge(mod_ready, 5)
            v.wait_ge(dft_done, 5)
            V.tensor_tensor(diag, ident.unsqueeze(1).broadcast_to([P, KT, P]),
                            mod[:, GT1, :].unsqueeze(2).broadcast_to([P, KT, P]), ALU.mult).then_inc(diag_ready, 1)
            v.wait_ge(summed, 6)
            V.tensor_tensor(mod[:, GT2, :], ps[:, 2, 0:KT], col[:, C_ADA + GT2 * KT:C_ADA + (GT2 + 1) * KT],
                            ALU.add).then_inc(mod_ready, 1)
            step(V.scalar_tensor_tensor(out=scale2[:, :], in0=mod[:, SC2, :], scalar=1.0, in1=col[:, C_N2:C_N2 + KT],
                                        op0=ALU.add, op1=ALU.mult))

            v.wait_ge(x_again, 16)
            v.wait_ge(row_saved, 1)
            for t in range(TT):
                for n in range(4):
                    v.wait_ge(wo_done, 4 * t + n + 1)
                    prod = slot(6)[:, (n % 2) * MIX:(n % 2 + 1) * MIX]
                    step(V.tensor_tensor(prod, ps[:, 4 * t + n, :], gt1row[:, n * MIX:(n + 1) * MIX], ALU.mult))
                    x1n = x1[:, t, n * MIX:(n + 1) * MIX]
                    V.tensor_tensor(x1n, x1n, prod, ALU.add).then_inc(x1_ready, 1)
            for t in range(TT):
                v.wait_ge(sq_done, 3 + t)
                step(V.tensor_scalar(stat[:, 6 + t:7 + t], stat[:, 4 + t:5 + t], 1.0 / D, EPS, ALU.mult, ALU.add))
                V.reciprocal(stat[:, 6 + t:7 + t], stat[:, 6 + t:7 + t]).then_inc(inv_ready, 1)
            for b in range(1, 8, 2):
                v.wait_ge(h2_t, b + 1)
                for k in (2 * b, 2 * b + 1):
                    V.tensor_scalar(h2T[:, k, :], tiles(b, 1)[:, k % 2, :], scale2[:, k:k + 1], mod[:, SH2, k:k + 1],
                                    ALU.mult, ALU.add).then_inc(h2_ready, 1)

            def b8(ap, n):
                return ap.unsqueeze(2).broadcast_to([P, TT, n])

            def first_of(out_hot, key, least, n):
                step(V.scalar_tensor_tensor(out=key, in0=key, scalar=-float(PER_GROUP), in1=io8[:, :, 0:n],
                                            op0=ALU.mult, op1=ALU.add))
                step(V.tensor_reduce(least, key, AX_X, ALU.min))
                step(V.tensor_tensor(out_hot, key, b8(least, n), ALU.is_equal))

            v.wait_ge(logit_done, 1)
            step(V.tensor_copy(lg[:, :, :], ps[:, 0, 0:72].rearrange("p (t n) -> p t n", t=TT)))
            step(V.tensor_reduce(rs[:, 0, :], lg[:, :, 0:4], AX_X, ALU.max))
            V.tensor_tensor(r8[:, :, 0, 0:4], lg[:, :, 0:4], b8(rs[:, 0, :], 4), ALU.subtract).then_inc(r_ask, 1)
            ghot = r8[:, :, 2, 0:4]
            step(V.tensor_tensor(ghot, lg[:, :, 0:4], b8(rs[:, 0, :], 4), ALU.is_equal))
            first_of(ghot, ghot, rs[:, 1, :], 4)
            v.wait_ge(r_exp, 1)
            step(V.tensor_reduce(rs[:, 2, :], r8[:, :, 1, 0:4], AX_X, ALU.add))
            step(V.reciprocal(rs[:, 3, :], rs[:, 2, :]))
            for t in range(TT):
                step(V.tensor_tensor(ra[:, t, :, :], lg[:, t, 4:36].rearrange("p (g e) -> p g e", g=4),
                                     r8[:, t, 2, 0:4].unsqueeze(2).broadcast_to([P, 4, PER_GROUP]), ALU.mult))
            le = r8[:, :, 0, :]
            v.wait_ge(r_exp, 1)
            for t in range(TT):
                step(V.tensor_reduce(r8[:, t, 0, :], ra[:, t, :, :].rearrange("p g e -> p e g"), AX_X, ALU.add))
            hot1, hot2, le2 = r8[:, :, 3, :], r8[:, :, 4, :], r8[:, :, 1, :]
            step(V.tensor_reduce(rs[:, 4, :], le, AX_X, ALU.max))
            step(V.tensor_tensor(hot1, le, b8(rs[:, 4, :], 8), ALU.is_equal))
            first_of(hot1, hot1, rs[:, 5, :], 8)
            step(V.scalar_tensor_tensor(out=le2, in0=hot1, scalar=-3.0e38, in1=le, op0=ALU.mult, op1=ALU.add))
            step(V.tensor_reduce(rs[:, 6, :], le2, AX_X, ALU.max))
            step(V.tensor_tensor(rs[:, 7, :], rs[:, 6, :], rs[:, 4, :], ALU.subtract))
            v.sem_inc(r_ask, 1)
            step(V.tensor_tensor(hot2, le2, b8(rs[:, 6, :], 8), ALU.is_equal))
            first_of(hot2, hot2, rs[:, 9, :], 8)
            for t in range(TT):
                for m, hot in ((m1, 3), (m2, 4)):
                    step(V.tensor_tensor(m[:, t, :, :], r8[:, t, 2, 0:4].unsqueeze(2).broadcast_to([P, 4, PER_GROUP]),
                                         r8[:, t, hot, :].unsqueeze(1).broadcast_to([P, 4, PER_GROUP]), ALU.mult))
            flat = "p t g e -> p (t g e)"
            V.tensor_tensor(ra[:, :, :, :].rearrange(flat), m1[:, :, :, :].rearrange(flat),
                            m2[:, :, :, :].rearrange(flat), ALU.add).then_inc(mask_ready, 1)
            v.wait_ge(r_exp, 2)
            step(V.tensor_scalar(rs[:, 10, :], rs[:, 8, :], 1.0, None, ALU.add))
            step(V.reciprocal(rs[:, 10, :], rs[:, 10, :]))
            step(V.tensor_tensor(rs[:, 11, :], rs[:, 3, :], rs[:, 10, :], ALU.mult))
            step(V.tensor_tensor(rs[:, 12, :], rs[:, 11, :], rs[:, 8, :], ALU.mult))
            v.wait_ge(pos_done, 1)
            step(V.tensor_copy(ct[:, 0, :], ps[0:32, 2, 0:P]))
            step(V.tensor_scalar(ct[:, 1, :], ct[:, 0, :], float(NWIN), 1.0, ALU.is_gt, ALU.add))
            for w in range(2, MAXWIN):
                ins = V.scalar_tensor_tensor(out=ct[:, 1, :], in0=ct[:, 0, :], scalar=float(w * NWIN), in1=ct[:, 1, :],
                                             op0=ALU.is_gt, op1=ALU.add)
                if w < MAXWIN - 1:
                    step(ins)
            ins.then_inc(cnt_ready, 1)
            v.wait_ge(start_done, 1)
            v.wait_ge(cnt_ready, 1)
            step(V.tensor_copy(st[:, 0, :], ps[:, 3, 0:32]))
            step(V.tensor_copy(ec[:, 0:2], ps[0:32, 3, 32:34]))
            passes = keep[0:32, K_PASS:K_PASS + MAXPASS]
            for w in range(MAXWIN):
                step(V.tensor_scalar(ec[:, 2:3], ec[:, 1:2], float(w), None, ALU.add))
                step(V.tensor_scalar(ec[:, 3:4], ct[:, 1, 0:1], float(w), None, ALU.is_gt))
                step(V.tensor_scalar(ec[:, 4:5], ec[:, 0:1], float(w * NWIN), None, ALU.add))
                hot = eh[:, 2, :] if w else eh[:, 0, :]
                step(V.tensor_scalar(hot, passes, ec[:, 2:3], ec[:, 3:4], ALU.is_equal, ALU.mult))
                if w == 0:
                    step(V.tensor_scalar(eh[:, 1, :], hot, ec[:, 4:5], None, ALU.mult))
                else:
                    step(V.scalar_tensor_tensor(out=eh[:, 1, :], in0=hot, scalar=ec[:, 4:5], in1=eh[:, 1, :],
                                                op0=ALU.mult, op1=ALU.add))
                    step(V.tensor_tensor(eh[:, 0, :], eh[:, 0, :], hot, ALU.add))
            v.sem_inc(pass_hot, 1)
            mall = ra[:, :, :, :].rearrange("p t g e -> p t (g e)")
            for t in range(TT):
                step(V.tensor_tensor(mall[:, t, :], ps[:, 1, t * 32:(t + 1) * 32], st[:, 0, :], ALU.add))
            for m, r in ((m1, 13), (m2, 14)):
                mm_ = m[:, :, :, :].rearrange("p t g e -> p t (g e)")
                step(V.tensor_tensor(mm_, mm_, mall, ALU.mult))
                step(V.tensor_reduce(rs[:, r, :], mm_, AX_X, ALU.add))
            step(V.memset(otab[:, :], 0))
            step(V.memset(etab[:, :], 0))
            v.wait_ge(pass_done, 1)
            step(V.tensor_copy(etab[0:1, 0:MAXPASS], ps[0:1, 2, 0:MAXPASS]))
            step(V.tensor_copy(otab[0:1, 1:1 + MAXPASS], ps[0:1, 2, 64:64 + MAXPASS]))
            step(V.tensor_copy(ntab[:, :], ps[0:1, 2, 128:129]))
            v.wait_ge(iota_in, 48)
            for t in range(TT):
                step(V.tensor_scalar(sel[:, t, 0:PAIRS], iota, rs[:, 13, t:t + 1], None, ALU.is_equal))
                step(V.scalar_tensor_tensor(out=sel[:, t, 0:PAIRS], in0=iota, scalar=rs[:, 14, t:t + 1],
                                            in1=sel[:, t, 0:PAIRS], op0=ALU.is_equal, op1=ALU.add))
            step(V.memset(sel[:, :, PAIRS:PADDED], 0.0))
            v.sem_inc(table_ready, 1)
            v.wait_ge(parts_act, 2)
            v.wait_ge(parts_sub, 2)
            for t in range(TT):
                sw = selw[:, t * PAIRS:(t + 1) * PAIRS]
                sw2 = selw[:, (2 + t) * PAIRS:(3 + t) * PAIRS]
                step(V.tensor_scalar(sw, iota, rs[:, 13, t:t + 1], rs[:, 11, t:t + 1], ALU.is_equal, ALU.mult))
                step(V.tensor_scalar(sw2, iota, rs[:, 14, t:t + 1], rs[:, 12, t:t + 1], ALU.is_equal, ALU.mult))
                step(V.tensor_tensor(sw, sw, sw2, ALU.add))
            v.sem_inc(selw_ready, 1)

            gat = ps[:, 0:2, :].rearrange("p b (c n) -> p (b c) n", n=NWIN)
            ye = ps[:, 4:8, :].rearrange("p b (c n) -> p (b c) n", n=P)[:, :, 0:NWIN]

            def wide(ap):
                return ap.unsqueeze(2).broadcast_to([P, KT, NWIN])

            def tokens(n):
                v.wait_ge(gathered, n)
                V.tensor_tensor(xs, gat, wide(scale2[:, :]), ALU.mult).then_inc(xe_step, 1)
                v.wait_ge(xe_step, n)
                V.tensor_tensor(xs, xs, wide(mod[:, SH2, :]), ALU.add).then_inc(xs_ready, 1)
                v.wait_ge(xhi_done, n)
                V.tensor_tensor(xe[:, :, NWIN:2 * NWIN], xs, xe[:, :, 0:NWIN].bitcast(F32), ALU.subtract
                                ).then_inc(xe_ready, 1)

            def save_output(off):
                V.tensor_tensor(YS[:, :, bass.ds(off, NWIN)], ye, wide(mod[:, GT2, :]), ALU.mult).then_inc(ye_saved, 1)

            v.wait_ge(h2_ready, 16)
            step(V.memset(hid, 0.0))
            v.sem_inc(lo_done, 8)
            tokens(1)
            n_pass = v.value_load(ntab[0:1, 0:1], min_val=NE, max_val=MAXPASS)
            with v.Fori(0, MAXPASS) as p:
                with v.If(p < n_pass):
                    for i in range(PIECES):
                        if i == 2:
                            with v.If(p > 0):
                                off = v.value_load(otab[0:1, bass.ds(p, 1)], min_val=0, max_val=PAIRS)
                                v.wait_ge(w2_used, 4 * p + 4)
                                save_output(off)
                        v.wait_ge(hi_done, 16 * p + i + 1)
                        V.tensor_tensor(w_lo[:, i % 2, :], chunk(i // 2 % 4)[:, (i % 2) * 1024:(i % 2 + 1) * 1024],
                                        w_hi[:, i % 2, :].bitcast(F32), ALU.subtract).then_inc(lo_done, 1)
                    v.wait_ge(piece_used, 16 * p + 16 + 2)
                    V.tensor_copy(h_sb[1], ps[:, 3, :]).then_inc(h3_saved, 1)
                    v.wait_ge(silu_done, p + 1)
                    v.wait_ge(t3_done, p + 1)
                    V.tensor_tensor(hid[:, :, 0:NWIN], silu_sb.rearrange("p (f n) -> p f n", f=FT),
                                    ps[:, 3, 0:FT * NWIN].rearrange("p (f n) -> p f n", f=FT), ALU.mult
                                    ).then_inc(hid_ready, 1)
                    tokens(p + 2)
            last_off = v.value_load(otab[0:1, bass.ds(n_pass, 1)], min_val=0, max_val=PAIRS)
            v.wait_ge(w2_used, 4 * n_pass + 4)
            save_output(last_off)
            v.wait_ge(ye_saved, n_pass)
            v.sem_inc(yT_savedV, 1)

            yn = ring[:, 0:2, :].rearrange("p s (i d) -> p (s i) d", d=D)
            for i in range(4):
                b = 4 * (i % 2) + 2
                v.wait_ge(yT_done, i + 1)
                V.tensor_copy(yn[:, i, 1024:2048], ps[:, b:b + 2, :].rearrange("p b n -> p (b n)")).then_inc(yT_savedV, 1)
            for t in range(TT):
                for n in range(4):
                    v.wait_ge(comb_done, 4 * t + n + 1)
                    x1n = x1[:, t, n * MIX:(n + 1) * MIX]
                    V.tensor_tensor(x1n, x1n, ps[:, 4 * t + n, :], ALU.add).then_inc(x2_ready, 1)
            v.wait_ge(fg_in, 16)
            for t in range(TT):
                v.wait_ge(sq_done, 4 + 4 * (t + 1))
                r = stat[:, 16 + t:17 + t]
                step(V.tensor_reduce(r, stat[:, 8 + 4 * t:12 + 4 * t], AX_X, ALU.add))
                step(V.tensor_scalar(r, r, 1.0 / D, EPS, ALU.mult, ALU.add))
                V.reciprocal(r, r).then_inc(inv_ready, 1)
                v.wait_ge(root_done, 5 + t)
                V.scalar_tensor_tensor(out=slot(2)[:, t * D:(t + 1) * D], in0=x1[:, t, :], scalar=r,
                                       in1=fgrow, op0=ALU.mult, op1=ALU.mult).then_inc(fin_ready, 1)


def constants():
    import numpy as np

    i = np.arange(P)
    keep = np.zeros((P, N_KEEP), np.float32)
    keep[:, 0:128] = np.eye(P)
    keep[:, 128:256] = 1.0
    keep[:, 256:384] = i[:, None] < i[None, :]
    keep[:, 384:400] = np.tile(np.arange(8), 2)
    keep[:, K_II:K_II + 64] = i[:, None] % 64 == np.arange(64)
    keep[:, K_IDX] = i
    keep[:, K_PASS:] = np.arange(MAXPASS)
    t = np.arange(S)
    pool = np.zeros((S, 4, S))
    for q, w in enumerate(POOL_WINDOWS):
        left = w // 2
        lo, hi = np.clip(t - left, 0, S), np.clip(t + w - left, 0, S)
        inside = (t[:, None] >= lo[None, :]) & (t[:, None] < hi[None, :])
        pool[:, q, :] = inside / (hi - lo)[None, :] - np.eye(S)
    a = 2 * np.pi * (np.outer(t, t) % S) / S
    norm = 1 / np.sqrt(S * P)
    pos = np.concatenate([np.cos(a), np.sin(a)], 1) * norm
    b = 2 * np.pi * (np.outer(i, i) % P) / P
    ch = np.concatenate([np.cos(b), -np.sin(b)], 1)
    halves = lambda m: m.reshape(2, P, -1).transpose(1, 0, 2).reshape(P, -1)
    mix = np.concatenate([halves(pool.reshape(S, -1)), halves(pos), ch], 1).astype(np.float32)
    iota = np.tile(np.arange(512, dtype=np.float32), (P, 1))
    return keep, np.ascontiguousarray(mix), iota


_INS = ["x", "c", "ada_w", "ada_b", "norm1_g", "w_in", "pool_w", "pool_scale", "conf_dw_w", "conf_dw_b", "conf_ln_g",
        "conf_ln_b", "branch_w", "sc_conv_w", "w_o", "norm2_g", "rg_w", "rg_b", "re_w", "re_b", "exp_w1", "exp_w3",
        "exp_w2", "final_g"]


def kernel(**inputs):
    import numpy as _np
    import concourse.bacc as _bacc
    from concourse import mybir as _mybir
    from concourse.bass_utils import run_bass_kernel_spmd as _run

    given = dict(inputs)
    given["branch_w"] = _np.stack([_np.asarray(inputs[n])[0] for n in ("conf_w_out", "sc_w_out", "fnet_w_out")])
    nc = _bacc.Bacc("TRN2", target_bir_lowering=False, num_devices=1)
    arrays, args = {}, []
    for name in _INS:
        a = _np.asarray(given[name])
        if name not in ("final_g", "branch_w"):
            a = a[0]
        a = _np.ascontiguousarray(a)
        arrays[f"in_{name}"] = a
        args.append(nc.dram_tensor(f"in_{name}", a.shape, _mybir.dt.from_np(a.dtype), kind="ExternalInput").ap())
    for name, a in zip(("keep_consts", "mix_consts", "iota_const"), constants()):
        arrays[f"in_{name}"] = a
        args.append(nc.dram_tensor(f"in_{name}", a.shape, _mybir.dt.from_np(a.dtype), kind="ExternalInput").ap())
    args.append(nc.dram_tensor("out_0", (S, D), F32, kind="ExternalOutput").ap())
    build(nc, *args)
    r = _run(nc, [arrays], core_ids=[0])
    return r.results[0]["out_0"].reshape(1, S, D)
```

```python
from contextlib import ExitStack

import concourse.bass as bass
from concourse import mybir

F32 = mybir.dt.float32
F32R = mybir.dt.float32r
BF16 = mybir.dt.bfloat16
I32 = mybir.dt.int32
ALU = mybir.AluOpType
ACT = mybir.ActivationFunctionType
AX_X = mybir.AxisListType.X

P = 128
D = 2048
S = 256
KT = D // P
TT = S // P
MIX = D // 4
MT = MIX // P
N_BRANCH = 4
GROUPS, PER_GROUP = 4, 8
NE = GROUPS * PER_GROUP
F = D // 4
FT = F // P
CONF_K, SC_K = 31, 3
EPS = 1e-6
POOL_WINDOWS = (2, 4, 8, 16)
OFF_A, OFF_B, OFF_C, OFF_D, OFF_G = 0, MIX, 3 * MIX, 6 * MIX, 7 * MIX

SLOT = 4096
N_SLOT = 7
W_SLOTS = 4
BW = 4
ADA = 5
H_HI = 6
AHEAD = 3
GATE_PIECES = KT // 2
ADA_FIRST = 4
NWIN = 64
MAXWIN = S // NWIN
PIECES = KT
HALF = KT // 2
ST2 = 3
RING2 = 4
PAIRS = S * 2
PADDED = PAIRS + NWIN
MAXPASS = NE + (PAIRS - 1) // (NWIN + 1)
NPT = MAXPASS + 1

C_N1, C_ADA, C_N2 = 0, 16, 112
C_PS, C_DWB, C_LNG, C_LNB, C_SCW = 128, 144, 148, 152, 156
C_DW = 168
N_COL = C_DW + CONF_K * MT
SH1, SC1, GT1, SH2, SC2, GT2 = range(6)

K_ID, K_ONE, K_TRI, K_IO8 = 0, 128, 256, 384
K_II, K_IDX, K_PASS = 400, 464, 465
N_KEEP = K_PASS + MAXPASS
N_MIXC = 1024 * 3 + 256


def build(nc, x, c, ada_w, ada_b, norm1_g, w_in, pool_w, pool_scale, conf_dw_w, conf_dw_b, conf_ln_g,
          conf_ln_b, branch_w, sc_conv_w, w_o, norm2_g, rg_w, rg_b, re_w, re_b, exp_w1, exp_w3,
          exp_w2, final_g, keep_consts, mix_consts, iota_const, out):
    with ExitStack() as ctx:
        def sb(name, shape, dt=F32):
            return ctx.enter_context(nc.sbuf_tensor(name, shape, dt))

        def sem(name):
            return ctx.enter_context(nc.semaphore(name))

        base = (nc.sbuf_base + 31) // 32 * 32
        ring = sb("ring", [P, N_SLOT, SLOT])
        r_h = sb("r_h", [P, KT * S])
        r_b = sb("r_b", [P, KT * S])
        r_m = sb("r_m", [P, 4096 + 2048 + 2176 + 2048])
        r_c = sb("r_c", [P, N_MIXC])
        keep = sb("keep", [P, N_KEEP])
        col = sb("col", [P, N_COL])
        mod = sb("mod", [P, 6, KT])
        scale1 = sb("scale1", [P, KT])
        scale2 = sb("scale2", [P, KT])
        ccol = sb("ccol", [P, KT])
        stat = sb("stat", [P, 32])

        def slot(s):
            return ring[:, s, :]

        hT = r_h[:, :].rearrange("p (c t) -> p c t", c=KT)
        x1 = r_h[:, :].rearrange("p (t d) -> p t d", t=TT)
        brT = r_b[:, :].rearrange("p (b c t) -> p b c t", b=N_BRANCH, c=MT)
        xn2 = r_b[:, :].rearrange("p (t d) -> p t d", t=TT)
        mergedT = r_m[:, 0:4096].rearrange("p (c t) -> p c t", c=KT)
        x_in = r_m[:, 0:4096].rearrange("p (t d) -> p t d", t=TT)
        h2T = mergedT
        tmp = [r_m[:, 4096:5120], r_m[:, 5120:6144]]
        gt1row = ring[:, 5, 2048:4096]
        vpad = r_m[:, 6144:6144 + MT * (S + CONF_K - 1)].rearrange("p (c t) -> p c t", c=MT)
        o = 6144 + MT * (S + CONF_K - 1)
        cxpad = r_m[:, o:o + MT * (S + SC_K - 1)].rearrange("p (c t) -> p c t", c=MT)
        pq = r_m[:, 6144:6144 + 2048].rearrange("p (q n) -> p q n", q=4)
        diag = r_m[:, 8320:8320 + 2048].rearrange("p (c k) -> p c k", c=KT)
        acc = r_m[:, 8320:8320 + 2048]
        iota = r_m[:, 8320:8320 + 512]
        YS = r_m[:, 0:KT * PADDED].rearrange("p (c j) -> p c j", c=KT)
        e0 = KT * PADDED
        rw = r_m[:, e0:e0 + KT * 36].rearrange("p (c n) -> p c n", c=KT)
        silu_sb = r_m[:, e0 + 576:e0 + 832]
        logitT = r_m[0:36, e0 + 576:e0 + 832]
        pool_c = r_c[:, 0:2048].rearrange("p (s q t) -> p s q t", s=TT, q=4)
        dftp = r_c[:, 2048:3072].rearrange("p (s n) -> p s n", s=TT)
        dftc = r_c[:, 3072:3328]
        def at(name, shape, dt, offset):
            return nc.alloc_sbuf_tensor_at(name, shape, dt, offset=base + offset)

        def chunk(s):
            return ring[:, s // 2, (s % 2) * 2048:(s % 2 + 1) * 2048]

        h_hi = at("h_hi", [P, KT, S], F32R, H_HI * SLOT * 4)
        h_lo = at("h_lo", [P, KT, S], F32R, N_SLOT * SLOT * 4)
        g_lo = at("g_lo", [P, W_SLOTS, SLOT], F32R, 0)
        mix_hi = at("mix_hi", [P, 3, 1024], F32R, 188928)
        pad_hi = at("pad_hi", [P, 1024], F32R, 172032)
        m_hi_a, m_hi_b = (at(f"m_hi_{i}", [P, KT // 2, S], F32R, i * SLOT * 4) for i in (5, 6))
        m_lo = at("m_lo", [P, KT, S], F32R, 147456)
        g_hi = [mix_hi[:, 0, :], mix_hi[:, 1, :], mix_hi[:, 2, :], pad_hi[:, :]]
        hi_a, lo_a = at("hi_a", [P, 2, 1024], F32R, 65536), at("lo_a", [P, 2, 1024], F32R, 73728)
        hi_b, lo_b = at("hi_b", [P, 2, 1024], F32R, 131072), at("lo_b", [P, 2, 1024], F32R, 139264)
        w_hi = [hi_a[:, 0, :], hi_a[:, 1, :], hi_b[:, 0, :], hi_b[:, 1, :]]
        w_lo = [lo_a[:, 0, :], lo_a[:, 1, :], lo_b[:, 0, :], lo_b[:, 1, :]]
        xe = at("xe", [P, KT, 2 * NWIN], F32R, 81920)
        xparts = at("xparts", [P, 3, TT, D], BF16, 90112)
        sel = r_c[:, 0:576].bitcast(BF16).rearrange("p (t j) -> p t j", t=TT)
        sel_e = r_c[:, 576:640].bitcast(BF16).rearrange("p (t n) -> p t n", t=TT)
        wT = r_c[:, 640:1664].rearrange("p (i t) -> p i t", i=4)
        hid = r_c[:, 1664:2176].rearrange("p (f n) -> p f n", f=FT)
        xs = r_c[:, 2176:2688].rearrange("p (c n) -> p c n", c=HALF)
        h_sb = [r_m[:, e0:e0 + 512], r_c[:, 2688:3200]]
        selw = r_b[:, 1024:3072]
        fgrow = r_b[:, 2048:4096]
        squares = r_b[:, 0:2048]
        remain = r_b
        ii = keep[:, K_II:K_II + 64]
        ident, ones, tri = keep[:, 0:128], keep[:, 128:256], keep[:, 256:384]
        io8 = keep[:, 384:400].rearrange("p (t e) -> p t e", t=TT)
        prow = ring[:, 0, 0:384].rearrange("p (a b) -> p a b", a=3)
        crow = ring[0:KT, 0, 384:512]

        lg = sb("lg", [P, TT, 36])
        lrow = sb("lrow", [1, 36])
        ra = sb("ra", [P, TT, 4, PER_GROUP])
        m1 = sb("m1", [P, TT, 4, PER_GROUP])
        m2 = sb("m2", [P, TT, 4, PER_GROUP])
        r8 = sb("r8", [P, TT, 5, PER_GROUP])
        rs = sb("rs", [P, 16, TT])
        ct = sb("ct", [32, 2, P])
        st = sb("st", [P, 3, NE])
        etab = sb("etab", [1, NPT], I32)
        otab = sb("otab", [1, NPT + 1], I32)
        ntab = sb("ntab", [1, 1], I32)
        ec = sb("ec", [32, 16])
        eh = sb("eh", [32, 3, MAXPASS])

        ps = ctx.enter_context(nc.psum_tensor("ps", [P, 8, 512], F32))

        def tiles(b, n=2):
            return ps[:, b:b + n, :].rearrange("p b (h t) -> p (b h) t", t=S)

        const_in = sem("const_in")
        mixc_in = sem("mixc_in")
        x_loaded = sem("x_loaded")
        ada_in = [sem(f"ada_in{i}") for i in range(ADA_FIRST)]
        ada_more = [sem(f"ada_more{i}") for i in range(2)]
        ada_tile = [sem(f"ada_tile{i}") for i in range(2)]
        w_in_sem = [sem(f"w_in_sem{i}") for i in range(W_SLOTS)]
        w_used = sem("w_used")
        h_split = sem("h_split")
        h_parts = sem("h_parts")
        g_hi_done = sem("g_hi_done")
        g_lo_done = sem("g_lo_done")
        g_used = sem("g_used")
        m_hi_done = sem("m_hi_done")
        m_parts = sem("m_parts")
        bw_in = sem("bw_in")
        cols_t = sem("cols_t")
        cols_ready = sem("cols_ready")
        xn_ready = sem("xn_ready")
        xT_done = sem("xT_done")
        xT_saved = sem("xT_saved")
        summed = sem("summed")
        mod_ready = sem("mod_ready")
        h_ready = sem("h_ready")
        unit_saved = sem("unit_saved")
        y_done = sem("y_done")
        y_saved = sem("y_saved")
        conv_done = sem("conv_done")
        ln_sum = sem("ln_sum")
        ln_step = sem("ln_step")
        sc_done = sem("sc_done")
        conf_ready = sem("conf_ready")
        pool_done = sem("pool_done")
        pool_ready = sem("pool_ready")
        dft_done = sem("dft_done")
        dft_saved = sem("dft_saved")
        chain_v = sem("chain_v")
        inv_ready = sem("inv_ready")
        root_done = sem("root_done")
        diag_ready = sem("diag_ready")
        row_done = sem("row_done")
        row_saved = sem("row_saved")
        x_again = sem("x_again")
        iota_in = sem("iota_in")
        wo_done = sem("wo_done")
        x1_ready = sem("x1_ready")
        xn2_ready = sem("xn2_ready")
        h2_t = sem("h2_t")
        h2_ready = sem("h2_ready")
        h2_readyV = sem("h2_readyV")
        logit_saved = sem("logit_saved")
        logit_t = sem("logit_t")
        logit_done = sem("logit_done")
        r_exp = sem("r_exp")
        r_ask = sem("r_ask")
        mask_ready = sem("mask_ready")
        pos_done = sem("pos_done")
        cnt_ready = sem("cnt_ready")
        start_done = sem("start_done")
        table_ready = sem("table_ready")
        selw_ready = sem("selw_ready")
        selw_t = sem("selw_t")
        wT_ready = sem("wT_ready")
        w13_in = [sem(f"w13_in{i}") for i in range(RING2)]
        w2_in = [sem(f"w2_in{i}") for i in range(RING2)]
        hi_done = sem("hi_done")
        lo_done = sem("lo_done")
        piece_used = sem("piece_used")
        w2_used = sem("w2_used")
        sel_ready = sem("sel_ready")
        gathered = sem("gathered")
        xe_step = sem("xe_step")
        xs_ready = sem("xs_ready")
        xhi_done = sem("xhi_done")
        xe_ready = sem("xe_ready")
        h1_saved = sem("h1_saved")
        h3_saved = sem("h3_saved")
        turned = sem("turned")
        silu_done = sem("silu_done")
        hid_ready = sem("hid_ready")
        ye_saved = sem("ye_saved")
        parts_sub = sem("parts_sub")
        parts_act = sem("parts_act")
        pass_hot = sem("pass_hot")
        pass_done = sem("pass_done")
        yT_done = sem("yT_done")
        yT_savedA = sem("yT_savedA")
        yT_savedV = sem("yT_savedV")
        comb_done = sem("comb_done")
        x2_ready = sem("x2_ready")
        sq_done = sem("sq_done")
        fin_ready = sem("fin_ready")
        fg_in = sem("fg_in")
        out_done = sem("out_done")
        acc_zero = sem("acc_zero")
        acc_step = sem("acc_step")
        merge_step = sem("merge_step")

        ada_v = ada_w.rearrange("(k p) n -> p k n", p=P)
        ada_kp = ada_w.rearrange("(k p) n -> k p n", p=P)
        win_v = w_in.rearrange("(k p) n -> p k n", p=P)
        wo_v = w_o.rearrange("(k p) n -> p k n", p=P)
        br_v = branch_w.rearrange("b (k p) n -> b p k n", p=P)
        x_v = x.rearrange("(t p) d -> p t d", p=P)
        out_v = out.rearrange("(t p) d -> p t d", p=P)
        e1_v = exp_w1.rearrange("e (k p) n -> e p k n", p=P)
        e3_v = exp_w3.rearrange("e (k p) n -> e p k n", p=P)
        e2_v = exp_w2.rearrange("e (k p) n -> e p k n", p=P)

        UNIT_COLS = [OFF_B + MIX, OFF_B, OFF_C + MIX, OFF_C + 2 * MIX, OFF_C, OFF_D, OFF_A]
        N_UNIT = len(UNIT_COLS)
        G0 = 2 * N_UNIT
        ADA0 = 16
        WO0 = G0 + N_BRANCH * 8
        UNITS = N_UNIT + 16

        def u_bank(n):
            return 4 * (n % 2)

        def y_bank(n):
            return 4 * (n % 2) + 2

        block = ctx.enter_context(nc.Block())

        @block.sync
        def _(sp):
            def load_ada(v, k, s, done):
                sp.dma_start(slot(s).rearrange("p (k n) -> p k n", k=2),
                             ada_v[:, 2 * k:2 * k + 2, bass.ds(v * D, D)]).then_inc(done, 16)

            def load_w(q, half, first):
                sp.dma_start(slot(q % W_SLOTS).rearrange("p (k n) -> p k n", k=8),
                             win_v[:, 8 * half:8 * half + 8, bass.ds(first, MIX)]
                             ).then_inc(w_in_sem[q % W_SLOTS], 16)

            def load_ada_more(n):
                sp.wait_ge(acc_step, 2 * (ADA0 + n - 1))
                load_ada(2 + n // 8, n % 8, 5 + n % 2, ada_more[n % 2])

            sp.dma_start(x_in, x_v).then_inc(x_loaded, 16)
            sp.wait_ge(const_in, 16 * 13)
            for n in range(ADA0):
                if n >= ADA_FIRST:
                    sp.wait_ge(acc_step, 2 * (n - ADA_FIRST + 1))
                load_ada(n // 8, n % 8, 3 + n % ADA_FIRST, ada_in[n % ADA_FIRST])
            sp.wait_ge(cols_ready, 2)
            for q in range(G0):
                if q == 3:
                    sp.wait_ge(acc_step, 2 * (13))
                if q >= W_SLOTS:
                    sp.wait_ge(w_used, q - W_SLOTS + 1)
                load_w(q, q % 2, UNIT_COLS[q // 2])
                for n in {3: (0, 1), 4: (2, 3), 5: (4, 5), 6: (6, 7), 10: (8, 9), 13: (10, 11, 12)}.get(q, ()):
                    load_ada_more(n)

            def gate_w(g, x):
                q = G0 + x
                if isinstance(g, int) and x < W_SLOTS and g == 0:
                    sp.wait_ge(w_used, q - W_SLOTS + 1)
                else:
                    sp.wait_ge(g_used, 4 * (x - W_SLOTS + 1) + 32 * g)
                load_w(q, x % 2, OFF_G + x // 2 * MIX + g * D)

            def ada_tiles(vec, k, n, used):
                for i in range(n):
                    sp.wait_ge(acc_step, used + k + i - 1)
                    sp.dma_start(slot(ADA)[:, i % 2 * D:(i % 2 + 1) * D], ada_v[:, k + i, vec * D:(vec + 1) * D]
                                 ).then_inc(ada_tile[i % 2], 16)

            gate_w(0, 0)
            load_ada_more(13)
            load_ada_more(14)
            gate_w(0, 1)
            load_ada_more(15)
            for j in range(4):
                gate_w(0, 2 * j + 2)
                ada_tiles(SC2, 4 * j, 2, 64)
                if j == 0:
                    sp.dma_start(slot(BW)[:, 0:2048].rearrange("p (q n) -> p q n", q=4),
                                 pool_w.rearrange("q c n -> c q n")).then_inc(bw_in, 16)
                gate_w(0, 2 * j + 3)
                ada_tiles(SC2, 4 * j + 2, 2, 64)

            def branch_loads(g, last):
                for j in range(4):
                    for x in (2 * j + 2, 2 * j + 3):
                        if x < 8 or not last:
                            gate_w(g, x)
                    if not last:
                        for i in range(2):
                            sp.wait_ge(acc_step, 80 + 2 * j + i - 1 + 8 * (g - 1))
                            sp.dma_start(slot(ADA)[:, i * D:(i + 1) * D],
                                         ada_kp[bass.ds((g - 1) * 8 + 2 * j + i, 1), :, GT2 * D:(GT2 + 1) * D]
                                         .rearrange("k p n -> (k p) n")).then_inc(ada_tile[i], 16)
                    if j % 2 == 0:
                        sp.wait_ge(y_done, 4 * g + j)
                        sp.dma_start(slot(BW).rearrange("p (k n) -> p k n", k=4),
                                     br_v[bass.ds(g - 1, 1), :, :, j * MIX:(j + 2) * MIX]
                                     .rearrange("b p k n -> (b p) k n")).then_inc(bw_in, 16)

            with sp.Fori(1, N_BRANCH - 1) as g:
                branch_loads(g, False)
            branch_loads(N_BRANCH - 1, True)
            for n in range(8):
                if n == 2:
                    sp.wait_ge(g_used, 8 * 16)
                    sp.dma_start(x1, x_v).then_inc(x_again, 16)
                if n == 3:
                    sp.wait_ge(row_done, 1)
                    sp.dma_start(iota, iota_const).then_inc(iota_in, 16)
                    sp.dma_start(rw[:, :, 0:4], rg_w.rearrange("(k p) n -> p k n", p=P)).then_inc(iota_in, 16)
                    sp.dma_start(rw[:, :, 4:36], re_w.rearrange("(k p) n -> p k n", p=P)).then_inc(iota_in, 16)
                if n < W_SLOTS:
                    sp.wait_ge(g_used, 4 * (32 + n - W_SLOTS + 1))
                else:
                    sp.wait_ge(g_used, 128 + 4 * (n - W_SLOTS + 1))
                sp.dma_start(slot((WO0 + n) % W_SLOTS).rearrange("p (k n) -> p k n", k=2),
                             wo_v[:, 2 * n:2 * n + 2, :]).then_inc(w_in_sem[(WO0 + n) % W_SLOTS], 16)

            def load_w13(e, c):
                for m, w in enumerate((e1_v, e3_v)):
                    sp.dma_start(chunk(c % 4)[:, m * 1024:(m + 1) * 1024].rearrange("p (k n) -> p k n", k=2),
                                 w[bass.ds(e, 1), :, 2 * c:2 * c + 2, :].rearrange("e p k n -> (e p) k n")
                                 ).then_inc(w13_in[c % 4], 16)

            def load_w2(e, q):
                sp.dma_start(chunk(4 + q).rearrange("p (f n) -> p f n", f=FT),
                             e2_v[bass.ds(e, 1), :, :, q * MIX:(q + 1) * MIX].rearrange("e p f n -> (e p) f n")
                             ).then_inc(w2_in[q], 16)

            for s in (2, 3, 0, 1):
                if s == 1:
                    sp.wait_ge(wo_done, 8)
                else:
                    sp.wait_ge(g_used, 128 + 4 * (5 + (s - 2) % 4))
                for h in range(2):
                    if s < 2:
                        load_w13(0, 2 * s + h)
                    else:
                        load_w2(0, 2 * (s - 2) + h)
            sp.wait_ge(table_ready, 1)
            n_pass = sp.value_load(ntab[0:1, 0:1], min_val=NE, max_val=MAXPASS)
            for c in range(4, 8):
                sp.wait_ge(lo_done, 2 * c + 2)
                load_w13(0, c)
            with sp.Fori(1, MAXPASS) as p:
                with sp.If(p < n_pass):
                    before = sp.value_load(etab[0:1, bass.ds(p - 1, 1)], min_val=0, max_val=NE - 1)
                    e = sp.value_load(etab[0:1, bass.ds(p, 1)], min_val=0, max_val=NE - 1)
                    for c in range(8):
                        if c % 2 == 0:
                            with sp.If(p > 1):
                                sp.wait_ge(w2_used, 4 * p + c // 2 + 1)
                                load_w2(before, c // 2)
                        sp.wait_ge(lo_done, 16 * p + 2 * c + 2)
                        load_w13(e, c)
            last_e = sp.value_load(etab[0:1, bass.ds(n_pass - 1, 1)], min_val=0, max_val=NE - 1)
            for q in range(4):
                sp.wait_ge(w2_used, 4 * n_pass + q + 1)
                load_w2(last_e, q)
            sp.wait_ge(piece_used, 16 * n_pass + 4)
            sp.dma_start(fgrow, final_g.rearrange("(o d) -> o d", o=1).broadcast_to([P, D])).then_inc(fg_in, 16)
            for t in range(TT):
                sp.wait_ge(fin_ready, t + 1)
                sp.dma_start(out_v[:, t, :], slot(2)[:, t * D:(t + 1) * D]).then_inc(out_done, 16)
            sp.wait_ge(out_done, 32)

        @block.gpsimd
        def _(pool):
            pool.dma_start(r_c[:, :], mix_consts).then_inc(mixc_in, 16)
            flat = "p t d -> p (t d)"
            for i in range(2):
                pool.wait_ge(parts_act, i + 1)
                dst = remain[:, :] if i == 0 else xparts[:, 2, :, :].rearrange(flat)
                if i == 0:
                    pool.wait_ge(h2_t, 8)
                nc.gpsimd.tensor_tensor(dst, r_b[:, :], xparts[:, i, :, :].rearrange(flat),
                                        ALU.subtract).then_inc(parts_sub, 1)

        @block.tensor
        def _(pe):
            mm = nc.tensor.matmul

            pe.wait_ge(const_in, 16 * 13)
            nc.tensor.transpose(ps[:, 7, 0:128], prow[:, 0, :], ident)
            nc.tensor.transpose(ps[:, 7, 128:168], prow[0:40, 1, :], ident[0:40, 0:40])
            nc.tensor.transpose(ps[:, 7, 168:168 + CONF_K * MT], prow[0:CONF_K * MT, 2, :],
                                ident[0:CONF_K * MT, 0:CONF_K * MT])
            nc.tensor.transpose(ps[:, 7, 320:336], crow, ident[0:KT, 0:KT]).then_inc(cols_t, 1)
            pe.wait_ge(cols_ready, 2)
            for t in range(TT):
                pe.wait_ge(xn_ready, t + 1)
            for b in range(8):
                for k in (2 * b, 2 * b + 1):
                    for t in range(TT):
                        last = nc.tensor.transpose(tiles(b, 1)[:, k % 2, t * P:(t + 1) * P],
                                                   x_in[:, t, k * P:(k + 1) * P], ident)
                last.then_inc(xT_done, 1)

            def sum_ada(n, bank):
                pe.wait_ge(acc_step, 16 * (n + 1))
                for k in range(KT):
                    last = mm(ps[:, bank, k:k + 1], acc[:, k * P:(k + 1) * P], ones[:, 0:1], start=True, stop=True)
                last.then_inc(summed, 1)

            pe.wait_ge(xT_saved, 8)
            sum_ada(SH1, 2)
            pe.wait_ge(mod_ready, 1)
            sum_ada(SC1, 2)

            def unit_T(n, loaded):
                u = tiles(u_bank(n))
                for half in range(2):
                    q = (2 * n + half) % W_SLOTS
                    pe.wait_ge(w_in_sem[q], loaded)
                    w = slot(q).rearrange("p (k n) -> p k n", k=8)
                    for kk in range(8):
                        k = 8 * half + kk
                        if n == 0:
                            pe.wait_ge(h_ready, k + 1)
                        for f in range(4):
                            last = mm(u[:, f, :], w[:, kk, f * P:(f + 1) * P], hT[:, k, :],
                                      start=(k == 0 and f % 2 == 0), stop=(k == KT - 1), skip_group_check=True)
                    last.then_inc(w_used, 1)

            def unit_N(n, loaded):
                for half in range(2):
                    q = (2 * n + half) % W_SLOTS
                    pe.wait_ge(w_in_sem[q], loaded)
                    w = slot(q).rearrange("p (k n) -> p k n", k=8)
                    for kk in range(8):
                        k = 8 * half + kk
                        for t in range(TT):
                            last = mm(ps[:, u_bank(n) + t, :], hT[:, k, t * P:(t + 1) * P], w[:, kk, :],
                                      start=(k == 0), stop=(k == KT - 1))
                    last.then_inc(w_used, 1)

            pe.wait_ge(mod_ready, 2)
            for n in range(5):
                if n >= 2:
                    pe.wait_ge(unit_saved, n - 1)
                unit_T(n, 16 * (n // 2 + 1))
                if n == 3:
                    pe.wait_ge(conv_done, 1)
                    for m in range(MT):
                        last = mm(ps[:, y_bank(n), 0:S], ones, brT[:, 1, m, :], start=(m == 0), stop=(m == MT - 1))
                    last.then_inc(ln_sum, 1)
                if n == 4:
                    pe.wait_ge(ln_step, 1)
                    pe.wait_ge(sc_done, 1)
                    for m in range(MT):
                        last = mm(ps[:, y_bank(n), 0:S], ones, pq[:, m, 0:S], start=(m == 0), stop=(m == MT - 1))
                    last.then_inc(ln_sum, 1)
            sum_ada(2, 3)
            for n in (5, 6):
                pe.wait_ge(unit_saved, n - 1)
                unit_N(n, 16 * (n // 2 + 1))

            pe.wait_ge(unit_saved, 6)
            pe.wait_ge(ln_step, 2)
            pe.wait_ge(mod_ready, 3)
            pe.wait_ge(mixc_in, 16)
            for q in range(4):
                b = (2, 3, 6, 7)[q]
                for t in range(TT):
                    last = mm(ps[:, b, :], tmp[0][:, t * MIX + q * P:t * MIX + (q + 1) * P], dftp[:, t, :],
                              start=(t == 0), stop=(t == TT - 1))
                last.then_inc(dft_done, 1)
            pe.wait_ge(unit_saved, 7)
            pt = tiles(0)
            for q in range(4):
                for t in range(TT):
                    last = mm(pt[:, q, :], tmp[1][:, t * MIX + q * P:t * MIX + (q + 1) * P], pool_c[:, t, q, :],
                              start=(t == 0), stop=(t == TT - 1))
            last.then_inc(pool_done, 1)

            def gate_y(n, kts, lhs, rhs):
                y = tiles(y_bank(n))
                for f in range(4):
                    for k in range(kts):
                        last = mm(y[:, f, :], lhs(k, f), rhs(k), start=(k == 0), stop=(k == kts - 1))
                return last

            pe.wait_ge(dft_saved, 4)
            for q in range(4):
                mm(tiles(2)[:, q, :], dftc[:, 0:128], pq[:, q, 0:S], start=True, stop=False)
                last = mm(tiles(2)[:, q, :], dftc[:, 128:256], pq[:, q, S:2 * S], start=False, stop=True)
            last.then_inc(dft_done, 1)

            def gate_unit(g, j):
                u = tiles(u_bank(N_UNIT + j))
                for i in range(GATE_PIECES):
                    pe.wait_ge(g_lo_done, 8 * j + i + 1 + 32 * g)
                    hi = g_hi[i % 4]
                    lo = g_lo[:, (G0 + 2 * j + i // 4) % W_SLOTS, (i % 4) * 1024:(i % 4 + 1) * 1024]
                    for kk in range(2):
                        k = 2 * i + kk
                        if j == 0 and isinstance(g, int) and g == 0 and k % 4 == 0:
                            pe.wait_ge(h_parts, k // 4 + 1)
                        for f in range(4):
                            o = kk * MIX + f * P
                            mm(u[:, f, :], hi[:, o:o + P], h_hi[:, k, :], start=(k == 0 and f % 2 == 0), stop=False,
                               skip_group_check=True)
                            mm(u[:, f, :], hi[:, o:o + P], h_lo[:, k, :], start=False, stop=False,
                               skip_group_check=True)
                            last = mm(u[:, f, :], lo[:, o:o + P], h_hi[:, k, :], start=False, stop=(k == KT - 1),
                                      skip_group_check=True)
                    last.then_inc(g_used, 1)

            pw = slot(BW)[:, 0:2048].rearrange("p (q n) -> p q n", q=4)
            bw = slot(BW).rearrange("p (k n) -> p k n", k=4)
            for j in range(4):
                n = N_UNIT + j
                if j == 1:
                    pe.wait_ge(pool_ready, 1)
                elif j >= 2:
                    pe.wait_ge(unit_saved, n - 1)
                gate_unit(0, j)
                if j == 0:
                    pe.wait_ge(bw_in, 16)
                    pe.wait_ge(pool_ready, 1)
                    sum_ada(3, y_bank(n))
                    pe.wait_ge(mod_ready, 4)
                if j >= 2:
                    pe.wait_ge(y_saved, j - 1)
                if j == 1:
                    pe.wait_ge(dft_saved, 5)
                last = gate_y(n, 1, lambda k, f: pw[:, j, f * P:(f + 1) * P], lambda k: brT[:, 0, j, :])
                last.then_inc(y_done, 1)
            pe.wait_ge(y_saved, 3)
            pe.wait_ge(acc_step, 80)
            for k in range(KT):
                last = mm(ps[:, 6, k:k + 1], acc[:, k * P:(k + 1) * P], ones[:, 0:1], start=True, stop=True)
            last.then_inc(summed, 1)

            def branch_gate(g):
                for j in range(4):
                    n = N_UNIT + j
                    pe.wait_ge(unit_saved, N_UNIT - 1 + j + 4 * g)
                    gate_unit(g, j)
                    if j == 3 and isinstance(g, int):
                        pe.wait_ge(diag_ready, 1)
                        pe.wait_ge(y_saved, 15)
                        pe.wait_ge(unit_saved, UNITS - 1)
                        for m in range(4):
                            last = mm(ps[:, 4 + m, :], ones, diag[:, 4 * m:4 * m + 4, :], start=True, stop=True)
                        last.then_inc(row_done, 1)
                    if j % 2 == 0:
                        pe.wait_ge(bw_in, 16 * (2 * (g - 1) + j // 2 + 2))
                    pe.wait_ge(y_saved, 4 * g + j - 1)
                    if j == 0:
                        pe.wait_ge(mod_ready, 5)
                    last = gate_y(n, MT, lambda k, f: bw[:, k, (j % 2) * MIX + f * P:(j % 2) * MIX + (f + 1) * P],
                                  lambda k: r_b[:, bass.ds(g * MT * S + k * S, S)])
                    last.then_inc(y_done, 1)

            with pe.Fori(1, N_BRANCH - 1) as g:
                branch_gate(g)
            pe.wait_ge(y_saved, 11)
            pe.wait_ge(acc_step, 96)
            for k in range(KT):
                last = mm(ps[:, 6, k:k + 1], acc[:, k * P:(k + 1) * P], ones[:, 0:1], start=True, stop=True)
            last.then_inc(summed, 1)
            pe.wait_ge(mod_ready, 6)
            branch_gate(N_BRANCH - 1)

            pe.wait_ge(row_saved, 1)

            def wo_products(k, t, n):
                y = 2 * k + n // 2
                hi = g_hi[y % 4][:, (n % 2) * MIX:(n % 2 + 1) * MIX]
                o = (y % 4) * 1024 + (n % 2) * MIX
                lo = g_lo[:, (WO0 + y // 4) % W_SLOTS, o:o + MIX]
                m_hi = (m_hi_a, m_hi_b)[k // 8][:, k % 8, t * P:(t + 1) * P]
                mm(ps[:, 4 * t + n, :], m_hi, hi, start=(k == 0), stop=False)
                mm(ps[:, 4 * t + n, :], m_hi, lo, start=False, stop=False)
                return mm(ps[:, 4 * t + n, :], m_lo[:, k, t * P:(t + 1) * P], hi, start=False, stop=(k == KT - 1))

            for y in range(28):
                pe.wait_ge(g_lo_done, 128 + y + 1)
                if y % 8 == 0:
                    pe.wait_ge(m_parts, y // 8 + 1)
                for t in (1, 0):
                    if y == 0 and t == 0:
                        pe.wait_ge(y_saved, 16)
                        pe.wait_ge(unit_saved, UNITS)
                    for n in (2 * (y % 2), 2 * (y % 2) + 1):
                        last = wo_products(y // 2, t, n)
                last.then_inc(g_used, 1)
            pe.wait_ge(g_lo_done, 128 + 32)
            for t in range(TT):
                for n in range(4):
                    for k in (14, 15):
                        last = wo_products(k, t, n)
                    last.then_inc(wo_done, 1)

            pe.wait_ge(x1_ready, 8)
            for t in range(TT):
                pe.wait_ge(xn2_ready, t + 1)
            for b in range(8):
                for k in (2 * b, 2 * b + 1):
                    for t in range(TT):
                        last = nc.tensor.transpose(tiles(b, 1)[:, k % 2, t * P:(t + 1) * P],
                                                   xn2[:, t, k * P:(k + 1) * P], ident)
                last.then_inc(h2_t, 1)
            pe.wait_ge(iota_in, 48)
            for k in range(KT):
                if k % 2 == 0:
                    pe.wait_ge((h2_ready, h2_readyV)[k // 2 % 2], 2 * (k // 4) + 2)
                mm(ps[0:36, 0, 0:S], rw[:, k, :], h2T[:, k, :], start=(k == 0), stop=False)
            mm(ps[0:36, 0, 0:S], lrow[0:1, :], ones[0:1, :].unsqueeze(1).broadcast_to([1, TT, P]), start=False,
               stop=True).then_inc(logit_done, 1)
            pe.wait_ge(logit_saved, 1)
            for t in range(TT):
                last = nc.tensor.transpose(ps[:, 1, t * 36:(t + 1) * 36], logitT[:, t * P:(t + 1) * P],
                                           ident[0:36, 0:36])
            last.then_inc(logit_t, 1)
            pe.wait_ge(mask_ready, 1)
            mall = ra[:, :, :, :].rearrange("p t g e -> p t (g e)")
            mm(ps[:, 1, 0:32], tri, mall[:, 0, :], start=True, stop=True)
            mm(ps[:, 1, 32:64], ones, mall[:, 0, :], start=True, stop=False)
            mm(ps[:, 1, 32:64], tri, mall[:, 1, :], start=False, stop=True)
            mm(ps[0:32, 2, 0:P], mall[:, 0, :], ones, start=True, stop=False)
            mm(ps[0:32, 2, 0:P], mall[:, 1, :], ones, start=False, stop=True).then_inc(pos_done, 1)
            pe.wait_ge(cnt_ready, 1)
            mm(ps[:, 3, 0:32], ct[:, 0, :], tri[0:32, 0:32], start=True, stop=True)
            mm(ps[0:32, 3, 32:33], tri[0:32, 0:32], ct[:, 0, 0:1], start=True, stop=True)
            mm(ps[0:32, 3, 33:34], tri[0:32, 0:32], ct[:, 1, 0:1], start=True, stop=True).then_inc(start_done, 1)
            pe.wait_ge(pass_hot, 1)
            mm(ps[0:1, 2, 0:MAXPASS], keep[0:32, K_IDX:K_IDX + 1], eh[:, 0, :], start=True, stop=True)
            mm(ps[0:1, 2, 64:64 + MAXPASS], ones[0:32, 0:1], eh[:, 1, :], start=True, stop=True)
            mm(ps[0:1, 2, 128:129], ones[0:32, 0:1], ct[:, 1, 0:1], start=True, stop=True).then_inc(pass_done, 1)
            gat = ps[:, 0, :].rearrange("p (c n) -> p c n", n=NWIN)
            ye = ps[:, 4:8, :].rearrange("p b (c n) -> p (b c) n", n=P)

            def gather(half):
                for kk in range(HALF):
                    k = half * HALF + kk
                    for t in range(TT):
                        for i in range(3):
                            last = mm(gat[:, kk, :], xparts[:, i, t, k * P:(k + 1) * P], sel_e[:, t, :],
                                      start=(t == 0 and i == 0), stop=(t == TT - 1 and i == 2))
                last.then_inc(gathered, 1)

            def turn(p):
                for m in range(2):
                    pe.wait_ge((h1_saved, h3_saved)[m], p)
                    for f in range(FT):
                        o = (m * FT + f) * NWIN
                        last = mm(ps[:, 1, o:o + NWIN], h_sb[m][:, f * P:(f + 1) * P], ii, start=True, stop=True)
                last.then_inc(turned, 1)

            def second(p, first, end):
                for m in range(first, end):
                    q = m // 4
                    if m == 0:
                        pe.wait_ge(hid_ready, p)
                    if m % 4 == 0:
                        pe.wait_ge(w2_in[q], 16 * p)
                    for f in range(FT):
                        last = mm(ye[:, m, :], chunk(4 + q)[:, f * MIX + (m % 4) * P:f * MIX + (m % 4 + 1) * P],
                                  hid[:, f, :], start=(f == 0), stop=(f == FT - 1))
                    if m % 4 == 3:
                        last.then_inc(w2_used, 1)

            def first(p, with_second):
                for i in range(PIECES):
                    if i % HALF == 0:
                        pe.wait_ge(xe_ready, 2 * p + i // HALF + 1)
                    pe.wait_ge(lo_done, 16 * p + i + 1 + 8)
                    for m in range(2):
                        for part in (w_hi, w_lo):
                            last = mm(ps[:, 2 + m, :], xe[:, i, :], part[i % 4][:, m * F:(m + 1) * F],
                                      start=(i == 0 and part is w_hi), stop=(i == KT - 1 and part is w_lo))
                    last.then_inc(piece_used, 1)
                    if with_second and i >= ST2:
                        second(p, (i - ST2) * KT // (PIECES - ST2), (i - ST2 + 1) * KT // (PIECES - ST2))
                    if i == HALF:
                        pe.wait_ge(sel_ready, p + 2)
                        gather(0)

            pe.sem_inc(piece_used, 4)
            pe.sem_inc(w2_used, 8)
            pe.wait_ge(sel_ready, 1)
            pe.wait_ge(parts_sub, 2)
            gather(0)
            pe.wait_ge(xs_ready, 1)
            gather(1)
            pe.wait_ge(selw_ready, 1)
            for i in range(4):
                for t in range(TT):
                    last = nc.tensor.transpose(tiles(4)[:, i, t * P:(t + 1) * P],
                                               selw[:, t * PAIRS + i * P:t * PAIRS + (i + 1) * P], ident)
            last.then_inc(selw_t, 1)
            pe.wait_ge(wT_ready, 1)
            n_pass = pe.value_load(ntab[0:1, 0:1], min_val=NE, max_val=MAXPASS)
            first(0, False)
            with pe.Fori(1, MAXPASS) as p:
                with pe.If(p < n_pass):
                    pe.wait_ge(xs_ready, 2 * p + 1)
                    gather(1)
                    turn(p)
                    first(p, True)
            turn(n_pass)
            second(n_pass, 0, KT)

            for i in range(4):
                b = 4 * (i % 2)
                if i == 0:
                    pe.wait_ge(yT_savedV, 1)
                if i >= 2:
                    pe.wait_ge(yT_savedA, i - 1)
                    pe.wait_ge(yT_savedV, i)
                for k in range(KT):
                    last = nc.tensor.transpose(ps[:, b + k // 4, (k % 4) * P:(k % 4 + 1) * P],
                                               YS[:, k, i * P:(i + 1) * P], ident)
                last.then_inc(yT_done, 1)
            yn = ring[:, 0:2, :].rearrange("p s (i d) -> p (s i) d", d=D)
            for t in range(TT):
                pe.wait_ge(yT_savedA, 3 + t if t == 0 else 4)
                pe.wait_ge(yT_savedV, 4 + t if t == 0 else 5)
                if t == 0:
                    pe.wait_ge(yT_savedA, 4)
                    pe.wait_ge(yT_savedV, 5)
                for n in range(4):
                    for i in range(4):
                        last = mm(ps[:, 4 * t + n, :], wT[:, i, t * P:(t + 1) * P], yn[:, i, n * MIX:(n + 1) * MIX],
                                  start=(i == 0), stop=(i == 3))
                    last.then_inc(comb_done, 1)

        @block.scalar
        def _(act):
            A = nc.scalar.activation
            small = [
                (keep[:, :], keep_consts), (prow[0:16, 0, :], norm1_g.rearrange("(a p) -> a p", p=P)),
                (prow[16:112, 0, :], ada_b.rearrange("(a p) -> a p", p=P)),
                (prow[112:128, 0, :], norm2_g.rearrange("(a p) -> a p", p=P)),
                (prow[0:16, 1, :], pool_scale.rearrange("(a p) -> a p", p=P)),
                (prow[16:20, 1, :], conf_dw_b.rearrange("(a p) -> a p", p=P)),
                (prow[20:24, 1, :], conf_ln_g.rearrange("(a p) -> a p", p=P)),
                (prow[24:28, 1, :], conf_ln_b.rearrange("(a p) -> a p", p=P)),
                (prow[28:40, 1, :], sc_conv_w.rearrange("j (a p) -> (j a) p", p=P)),
                (prow[0:CONF_K * MT, 2, :], conf_dw_w.rearrange("j (a p) -> (j a) p", p=P)),
                (crow, c.rearrange("(a p) -> a p", p=P)),
                (lrow[0:1, 0:4], rg_b.rearrange("(o n) -> o n", o=1)),
                (lrow[0:1, 4:36], re_b.rearrange("(o n) -> o n", o=1)),
            ]
            for dst, src in small:
                act.dma_start(dst, src).then_inc(const_in, 16)
            act.wait_ge(x_loaded, 16)
            for t in range(TT):
                last = A(r_b[:, t * D:(t + 1) * D], x_in[:, t, :], ACT.Square, accum_out=stat[:, t:t + 1])
                last.then_inc(sq_done, 1)
            act.wait_ge(inv_ready, 1)
            A(stat[:, 2:4], stat[:, 2:4], ACT.Sqrt).then_inc(root_done, 1)
            act.wait_ge(root_done, 1)
            for t in range(TT):
                A(x_in[:, t, :], x_in[:, t, :], ACT.Copy, scale=stat[:, 2 + t:3 + t]).then_inc(xn_ready, 1)
            for b in range(8):
                act.wait_ge(xT_done, b + 1)
                A(r_h[:, b * 512:(b + 1) * 512], ps[:, b, :], ACT.Copy).then_inc(xT_saved, 1)
            act.wait_ge(mod_ready, 2)
            act.wait_ge(xT_saved, 8)
            act.wait_ge(cols_ready, 3)
            for k in range(KT):
                A(hT[:, k, :], hT[:, k, :], ACT.Identity, bias=mod[:, SH1, k:k + 1],
                  scale=scale1[:, k:k + 1]).then_inc(h_ready, 1)
            act.wait_ge(w_used, 2 * (1))
            A(tmp[0], ps[:, 0:2, :], ACT.Sigmoid).then_inc(unit_saved, 1)
            act.wait_ge(w_used, 2 * (3))
            act.wait_ge(unit_saved, 2)
            A(tmp[0], ps[:, 0:2, :], ACT.Copy).then_inc(unit_saved, 1)
            act.wait_ge(conv_done, 2)
            act.wait_ge(sc_done, 1)
            A(pq[:, :, 0:S], brT[:, 1, :, :], ACT.Square).then_inc(ln_step, 1)
            act.wait_ge(inv_ready, 2)
            A(tmp[1][:, 0:S], tmp[1][:, 0:S], ACT.Sqrt).then_inc(root_done, 1)
            act.wait_ge(conv_done, 3)
            for m in range(MT):
                A(brT[:, 1, m, :], brT[:, 1, m, :], ACT.Silu, bias=col[:, C_LNB + m:C_LNB + m + 1],
                  scale=col[:, C_LNG + m:C_LNG + m + 1]).then_inc(conf_ready, 1)
            act.wait_ge(w_used, 2 * (6))
            act.wait_ge(unit_saved, 5)
            A(tmp[0], ps[:, 4:6, :], ACT.Copy).then_inc(unit_saved, 1)
            act.wait_ge(w_used, 2 * (7))
            A(tmp[1], ps[:, 0:2, :], ACT.Copy).then_inc(unit_saved, 1)
            act.wait_ge(acc_step, 64)
            A(h_hi[:, :, :], hT, ACT.Copy).then_inc(h_split, 1)
            for q in range(4):
                act.wait_ge(dft_done, q + 1)
                act.wait_ge(ln_sum, 2)
                A(pq[:, q, :], ps[:, (2, 3, 6, 7)[q], :], ACT.Copy).then_inc(dft_saved, 1)
            act.wait_ge(pool_done, 1)
            A(r_b[:, 0:1024], ps[:, 0:2, :], ACT.Copy).then_inc(pool_ready, 1)

            act.wait_ge(dft_done, 5)
            A(r_b[:, 3072:4096], ps[:, 2:4, :], ACT.Copy).then_inc(dft_saved, 1)

            def gate(g, last):
                for j in range(4):
                    for x in range(8 * j + AHEAD, 8 * j + 8 + AHEAD):
                        if x < 32 or not last:
                            gate_high(g, x)
                        else:
                            wo_high(x - 32)
                    n = N_UNIT + j
                    if last and j >= 2:
                        merged_high(j - 2)
                    act.wait_ge(g_used, 8 * (j + 1) + 32 * g)
                    if not (isinstance(g, int) and 4 * g + j < 2):
                        act.wait_ge(y_saved, 4 * g + j - 1)
                    A(tmp[n % 2], ps[:, u_bank(n):u_bank(n) + 2, :], ACT.Sigmoid).then_inc(unit_saved, 1)

            def gate_high(g, x):
                q = G0 + x // 4
                if x % 4 == 0:
                    act.wait_ge(w_in_sem[q % W_SLOTS], 16 * (q // W_SLOTS + 1) + 32 * g)
                if not (isinstance(g, int) and 32 * g + x < 4):
                    act.wait_ge(g_used, x - 3 + 32 * g)
                A(g_hi[x % 4], slot(q % W_SLOTS)[:, (x % 4) * 1024:(x % 4 + 1) * 1024], ACT.Copy
                  ).then_inc(g_hi_done, 1)

            def wo_high(y):
                q = WO0 + y // 4
                if y % 4 == 0:
                    act.wait_ge(w_in_sem[q % W_SLOTS], 16 * (q // W_SLOTS + 1))
                act.wait_ge(g_used, 128 + y - 3)
                A(g_hi[y % 4], slot(q % W_SLOTS)[:, (y % 4) * 1024:(y % 4 + 1) * 1024], ACT.Copy
                  ).then_inc(g_hi_done, 1)

            def merged_high(j):
                act.wait_ge(y_saved, 13 + j)
                A((m_hi_a, m_hi_b)[j // 2][:, j % 2 * 4:j % 2 * 4 + 4, :], mergedT[:, 4 * j:4 * j + 4, :], ACT.Copy
                  ).then_inc(m_hi_done, 1)

            for x in range(AHEAD):
                gate_high(0, x)
            gate(0, False)
            with act.Fori(1, N_BRANCH - 1) as g:
                gate(g, False)
            gate(N_BRANCH - 1, True)
            merged_high(2)
            act.wait_ge(row_done, 1)
            A(gt1row, ps[:, 4:8, :], ACT.Copy).then_inc(row_saved, 1)
            wo_high(AHEAD)
            merged_high(3)
            for y in range(AHEAD + 1, 32):
                wo_high(y)

            for t in range(TT):
                act.wait_ge(x1_ready, 4 * t + 4)
                A(xn2[:, t, :], x1[:, t, :], ACT.Square, accum_out=stat[:, 4 + t:5 + t]).then_inc(sq_done, 1)
            for t in range(TT):
                r = stat[:, 6 + t:7 + t]
                act.wait_ge(inv_ready, 3 + t)
                A(r, r, ACT.Sqrt).then_inc(root_done, 1)
                act.wait_ge(root_done, 3 + t)
                A(xn2[:, t, :], x1[:, t, :], ACT.Copy, scale=stat[:, 6 + t:7 + t]).then_inc(xn2_ready, 1)
            act.wait_ge(xn2_ready, 2)
            act.wait_ge(x1_ready, 8)
            A(xparts[:, 0, :, :], xn2, ACT.Copy).then_inc(parts_act, 1)
            for b in range(0, 8, 2):
                act.wait_ge(h2_t, b + 1)
                for k in (2 * b, 2 * b + 1):
                    A(h2T[:, k, :], tiles(b, 1)[:, k % 2, :], ACT.Identity, bias=mod[:, SH2, k:k + 1],
                      scale=scale2[:, k:k + 1]).then_inc(h2_ready, 1)
            act.wait_ge(r_ask, 1)
            A(r8[:, :, 1, 0:4], r8[:, :, 0, 0:4], ACT.Exp).then_inc(r_exp, 1)
            act.wait_ge(r_ask, 2)
            A(rs[:, 8, :], rs[:, 7, :], ACT.Exp).then_inc(r_exp, 1)
            act.wait_ge(parts_sub, 1)
            A(xparts[:, 1, :, :].rearrange("p t d -> p (t d)"), remain[:, :], ACT.Copy).then_inc(parts_act, 1)
            act.wait_ge(table_ready, 1)
            A(sel_e, sel[:, :, 0:NWIN], ACT.Copy).then_inc(sel_ready, 1)
            for half in range(2):
                act.wait_ge(xs_ready, half + 1)
                A(xe[:, half * HALF:(half + 1) * HALF, 0:NWIN], xs, ACT.Copy).then_inc(xhi_done, 1)
            act.wait_ge(selw_t, 1)
            A(wT[:, :, :], tiles(4), ACT.Copy).then_inc(wT_ready, 1)

            def xe_high(p, half):
                act.wait_ge(xs_ready, 2 * p + half + 1)
                A(xe[:, half * HALF:(half + 1) * HALF, 0:NWIN], xs, ACT.Copy).then_inc(xhi_done, 1)

            def select(p):
                off = act.value_load(otab[0:1, bass.ds(p + 2, 1)], min_val=0, max_val=PAIRS)
                act.wait_ge(gathered, 2 * p + 2)
                A(sel_e, sel[:, :, bass.ds(off, NWIN)], ACT.Copy).then_inc(sel_ready, 1)

            def silu(p):
                act.wait_ge(turned, p)
                A(silu_sb, ps[:, 1, 0:FT * NWIN], ACT.Silu).then_inc(silu_done, 1)

            def pieces(p, later):
                for i in range(PIECES):
                    if i % 2 == 0:
                        act.wait_ge(w13_in[i // 2 % 4], 64 * p + 32 * (i // 8) + 32)
                    act.wait_ge(piece_used, 16 * p + i + 1)
                    A(w_hi[i % 4].rearrange("p (m n) -> p m n", m=2),
                      chunk(i // 2 % 4).rearrange("p (m k n) -> p m k n", m=2, k=2)[:, :, i % 2, :], ACT.Copy
                      ).then_inc(hi_done, 1)
                    if later and i == 1:
                        silu(p)
                    if later and i == 2:
                        xe_high(p, 1)
                        select(p)
                    if i == 13:
                        xe_high(p + 1, 0)
                act.wait_ge(piece_used, 16 * p + 16 + 4)
                A(h_sb[0], ps[:, 2, :], ACT.Copy).then_inc(h1_saved, 1)

            n_pass = act.value_load(ntab[0:1, 0:1], min_val=NE, max_val=MAXPASS)
            select(0)
            pieces(0, False)
            with act.Fori(1, MAXPASS) as p:
                with act.If(p < n_pass):
                    pieces(p, True)
            silu(n_pass)

            yn = ring[:, 0:2, :].rearrange("p s (i d) -> p (s i) d", d=D)
            for i in range(4):
                b = 4 * (i % 2)
                act.wait_ge(yT_done, i + 1)
                A(yn[:, i, 0:1024], ps[:, b:b + 2, :], ACT.Copy).then_inc(yT_savedA, 1)
            for t in range(TT):
                for n in range(4):
                    act.wait_ge(x2_ready, 4 * t + n + 1)
                    if t:
                        act.wait_ge(sq_done, 4 + n + 1)
                    A(squares[:, n * MIX:(n + 1) * MIX], x1[:, t, n * MIX:(n + 1) * MIX], ACT.Square,
                      accum_out=stat[:, 8 + 4 * t + n:9 + 4 * t + n]).then_inc(sq_done, 1)
                act.wait_ge(inv_ready, 5 + t)
                A(stat[:, 16 + t:17 + t], stat[:, 16 + t:17 + t], ACT.Sqrt).then_inc(root_done, 1)

        @block.vector
        def _(v):
            V = nc.vector
            steps = [0]

            def step(ins):
                steps[0] += 1
                ins.then_inc(chain_v, 1)
                v.wait_ge(chain_v, steps[0])

            v.wait_ge(cols_t, 1)
            V.tensor_copy(col[:, :], ps[:, 7, 0:N_COL]).then_inc(cols_ready, 1)
            V.tensor_copy(ccol[:, :], ps[:, 7, 320:336]).then_inc(cols_ready, 1)
            v.wait_ge(cols_ready, 2)
            v.wait_ge(sq_done, 2)
            step(V.tensor_scalar(stat[:, 2:4], stat[:, 0:2], 1.0 / D, EPS, ALU.mult, ALU.add))
            V.reciprocal(stat[:, 2:4], stat[:, 2:4]).then_inc(inv_ready, 1)

            def ada_chunk(s, k, first):
                w = slot(s).rearrange("p (k n) -> p k n", k=2)
                for i in range(2):
                    kk = 2 * k + i
                    if kk == 0:
                        ins = V.tensor_scalar(acc, w[:, i, :], ccol[:, kk:kk + 1], None, ALU.mult)
                    else:
                        ins = V.scalar_tensor_tensor(out=acc, in0=w[:, i, :], scalar=ccol[:, kk:kk + 1], in1=acc,
                                                     op0=ALU.mult, op1=ALU.add)
                    yield ins

            for n in range(ADA0):
                v.wait_ge(ada_in[n % ADA_FIRST], 16 * (n // ADA_FIRST + 1))
                if n == 8:
                    v.wait_ge(summed, 1)
                for i, ins in enumerate(ada_chunk(3 + n % ADA_FIRST, n % 8, n % 8 == 0)):
                    ins.then_inc(acc_step, 1)
                    v.wait_ge(acc_step, 2 * n + i + 1)
                if n % 8 == 7:
                    m = n // 8
                    v.wait_ge(summed, m + 1)
                    V.tensor_tensor(mod[:, m, :], ps[:, 2, 0:KT], col[:, C_ADA + m * KT:C_ADA + (m + 1) * KT],
                                    ALU.add).then_inc(mod_ready, 1)
            v.wait_ge(mod_ready, 2)
            V.scalar_tensor_tensor(out=scale1[:, :], in0=mod[:, SC1, :], scalar=1.0, in1=col[:, C_N1:C_N1 + KT],
                                   op0=ALU.add, op1=ALU.mult).then_inc(cols_ready, 1)
            V.memset(r_m[:, 6144:6144 + MT * (S + CONF_K - 1) + MT * (S + SC_K - 1)], 0.0).then_inc(cols_ready, 1)
            v.wait_ge(cols_ready, 4)

            def ada_more_chunk(n):
                v.wait_ge(ada_more[n % 2], 16 * (n // 2 + 1))
                if n == 8:
                    v.wait_ge(summed, 3)
                for i, ins in enumerate(ada_chunk(5 + n % 2, n % 8, n % 8 == 0)):
                    ins.then_inc(acc_step, 1)
                    v.wait_ge(acc_step, 2 * (ADA0 + n) + i + 1)

            def save_mod(m, bank):
                v.wait_ge(summed, m + 1)
                V.tensor_tensor(mod[:, m, :], ps[:, bank, 0:KT], col[:, C_ADA + m * KT:C_ADA + (m + 1) * KT],
                                ALU.add).then_inc(mod_ready, 1)

            for n in range(6):
                ada_more_chunk(n)
            v.wait_ge(w_used, 2 * (2))
            v.wait_ge(unit_saved, 1)
            step(V.tensor_tensor(vpad[:, :, 15:15 + S], tiles(4), tmp[0].rearrange("p (c t) -> p c t", c=MT), ALU.mult))
            v.sem_inc(unit_saved, 1)
            c0 = steps[0]
            for j in range(CONF_K):
                for m in range(MT):
                    wcol = col[:, C_DW + j * MT + m:C_DW + j * MT + m + 1]
                    if j:
                        v.wait_ge(chain_v, c0 + (j - 1) * MT + m + 1)
                        ins = V.scalar_tensor_tensor(out=brT[:, 1, m, :], in0=vpad[:, m, j:j + S], scalar=wcol,
                                                     in1=brT[:, 1, m, :], op0=ALU.mult, op1=ALU.add)
                    else:
                        ins = V.tensor_scalar(brT[:, 1, m, :], vpad[:, m, 0:S], wcol,
                                              col[:, C_DWB + m:C_DWB + m + 1], ALU.mult, ALU.add)
                    ins.then_inc(chain_v, 1)
            steps[0] += CONF_K * MT
            v.wait_ge(chain_v, steps[0])
            v.sem_inc(conv_done, 1)

            for n in (6, 7):
                ada_more_chunk(n)
            v.wait_ge(w_used, 2 * (4))
            v.wait_ge(unit_saved, 3)
            step(V.tensor_tensor(cxpad[:, :, 1:1 + S], tiles(4), tmp[0].rearrange("p (c t) -> p c t", c=MT), ALU.mult))
            v.sem_inc(unit_saved, 1)
            z = tmp[0].rearrange("p (c t) -> p c t", c=MT)
            c0 = steps[0]
            for j in range(SC_K):
                for m in range(MT):
                    wcol = col[:, C_SCW + j * MT + m:C_SCW + j * MT + m + 1]
                    if j:
                        v.wait_ge(chain_v, c0 + (j - 1) * MT + m + 1)
                        ins = V.scalar_tensor_tensor(out=z[:, m, :], in0=cxpad[:, m, j:j + S], scalar=wcol,
                                                     in1=z[:, m, :], op0=ALU.mult, op1=ALU.add)
                    else:
                        ins = V.tensor_scalar(z[:, m, :], cxpad[:, m, 0:S], wcol, None, ALU.mult)
                    ins.then_inc(chain_v, 1)
            steps[0] += SC_K * MT
            v.wait_ge(chain_v, steps[0])
            v.sem_inc(sc_done, 1)

            lb = y_bank(3)
            v.wait_ge(ln_sum, 1)
            mrow = tmp[1][:, 0:S]
            step(V.tensor_scalar(mrow, ps[:, lb, 0:S], 1.0 / MIX, None, ALU.mult))
            V.tensor_tensor(brT[:, 1, :, :], brT[:, 1, :, :], mrow.unsqueeze(1).broadcast_to([P, MT, S]),
                            ALU.subtract).then_inc(conv_done, 1)
            v.wait_ge(w_used, 2 * (5))
            V.tensor_tensor(brT[:, 2, :, :], tiles(0), z, ALU.mult).then_inc(unit_saved, 1)
            v.wait_ge(ln_sum, 2)
            step(V.tensor_scalar(mrow, ps[:, y_bank(4), 0:S], 1.0 / MIX, EPS, ALU.mult, ALU.add))
            v.sem_inc(ln_step, 1)
            V.reciprocal(mrow, mrow).then_inc(inv_ready, 1)
            v.wait_ge(root_done, 2)
            V.tensor_tensor(brT[:, 1, :, :], brT[:, 1, :, :], mrow.unsqueeze(1).broadcast_to([P, MT, S]),
                            ALU.mult).then_inc(conv_done, 1)

            save_mod(GT1, 3)
            for n in range(8, 16):
                ada_more_chunk(n)

            def ada_one(k, loaded, before, kcol):
                v.wait_ge(ada_tile[k % 2], loaded)
                w = slot(ADA)[:, k % 2 * D:(k % 2 + 1) * D]
                if k == 0:
                    ins = V.tensor_scalar(acc, w, kcol, None, ALU.mult)
                else:
                    ins = V.scalar_tensor_tensor(out=acc, in0=w, scalar=kcol, in1=acc, op0=ALU.mult, op1=ALU.add)
                ins.then_inc(acc_step, 1)
                v.wait_ge(acc_step, before + 1)

            def gate_low(g, x):
                q = (G0 + x // 4) % W_SLOTS
                v.wait_ge(g_hi_done, x + 1 + 32 * g)
                V.tensor_tensor(g_lo[:, q, (x % 4) * 1024:(x % 4 + 1) * 1024],
                                slot(q)[:, (x % 4) * 1024:(x % 4 + 1) * 1024], g_hi[x % 4].bitcast(F32),
                                ALU.subtract).then_inc(g_lo_done, 1)

            v.wait_ge(h_split, 1)
            v.wait_ge(w_used, G0)
            for i in range(4):
                V.tensor_tensor(h_lo[:, 4 * i:4 * i + 4, :], hT[:, 4 * i:4 * i + 4, :],
                                h_hi[:, 4 * i:4 * i + 4, :].bitcast(F32), ALU.subtract).then_inc(h_parts, 1)
            for x in range(AHEAD):
                gate_low(0, x)
            ADA_AT = {8 + 3 * k // 2: (k,) for k in range(16)}
            for j in range(4):
                n = N_UNIT + j
                for i in range(8):
                    gate_low(0, 8 * j + AHEAD + i)
                    for k in ADA_AT.get(8 * j + i, ()):
                        ada_one(k, 16 * (k // 2 + 1), 64 + k, ccol[:, k:k + 1])
                if j == 0:
                    save_mod(SH2, y_bank(n))
                v.wait_ge(y_done, j + 1)
                v.wait_ge(unit_saved, n + 1)
                for f in range(4):
                    ins = V.scalar_tensor_tensor(out=mergedT[:, 4 * j + f, :], in0=tiles(y_bank(n))[:, f, :],
                                                 scalar=col[:, C_PS + 4 * j + f:C_PS + 4 * j + f + 1],
                                                 in1=tmp[n % 2][:, f * S:(f + 1) * S], op0=ALU.mult, op1=ALU.mult)
                ins.then_inc(y_saved, 1)
            save_mod(SC2, 6)
            V.memset(acc, 0.0).then_inc(acc_zero, 1)
            v.wait_ge(acc_zero, 1)

            def branch_gate(g, last):
                for j in range(4):
                    n = N_UNIT + j
                    for i in range(8):
                        x = 8 * j + AHEAD + i
                        if x < 32 or not last:
                            gate_low(g, x)
                        else:
                            wo_low(x - 32)
                        if not last and i in (2, 5):
                            k = 2 * j + i // 4
                            ada_one(k + 16, 128 + 16 * (k // 2 + 1) + 64 * (g - 1), 80 + k + 8 * (g - 1),
                                    ccol[:, bass.ds(8 * (g - 1) + k, 1)])
                    v.wait_ge(y_done, 4 * g + j + 1)
                    v.wait_ge(unit_saved, n + 1 + 4 * g)
                    gy = tmp[n % 2]
                    V.tensor_tensor(gy, ps[:, y_bank(n):y_bank(n) + 2, :].rearrange("p b n -> p (b n)"), gy,
                                    ALU.mult).then_inc(merge_step, 1)
                    v.wait_ge(merge_step, 4 * g + j - 3)
                    v.wait_ge(y_saved, 4 * g + j - 3)
                    m = r_m[:, j * 1024:(j + 1) * 1024]
                    V.tensor_tensor(m, m, gy, ALU.add).then_inc(y_saved, 1)
                    if last and j == 2:
                        merged_low(0)

            def wo_low(y):
                q = (WO0 + y // 4) % W_SLOTS
                v.wait_ge(g_hi_done, 128 + y + 1)
                V.tensor_tensor(g_lo[:, q, (y % 4) * 1024:(y % 4 + 1) * 1024],
                                slot(q)[:, (y % 4) * 1024:(y % 4 + 1) * 1024], g_hi[y % 4].bitcast(F32),
                                ALU.subtract).then_inc(g_lo_done, 1)

            def merged_low(j):
                v.wait_ge(y_saved, 13 + j)
                v.wait_ge(m_hi_done, j + 1)
                V.tensor_tensor(m_lo[:, 4 * j:4 * j + 4, :], mergedT[:, 4 * j:4 * j + 4, :],
                                (m_hi_a, m_hi_b)[j // 2][:, j % 2 * 4:j % 2 * 4 + 4, :].bitcast(F32), ALU.subtract
                                ).then_inc(m_parts, 1)

            with v.Fori(1, N_BRANCH - 1) as g:
                branch_gate(g, False)
            save_mod(GT2, 6)
            v.wait_ge(mod_ready, 6)
            V.tensor_tensor(diag, ident.unsqueeze(1).broadcast_to([P, KT, P]),
                            mod[:, GT1, :].unsqueeze(2).broadcast_to([P, KT, P]), ALU.mult).then_inc(diag_ready, 1)
            branch_gate(N_BRANCH - 1, True)
            wo_low(AHEAD)
            merged_low(1)
            merged_low(2)
            wo_low(AHEAD + 1)
            merged_low(3)
            for y in range(AHEAD + 2, 32):
                wo_low(y)
            step(V.scalar_tensor_tensor(out=scale2[:, :], in0=mod[:, SC2, :], scalar=1.0, in1=col[:, C_N2:C_N2 + KT],
                                        op0=ALU.add, op1=ALU.mult))

            v.wait_ge(x_again, 16)
            v.wait_ge(row_saved, 1)
            for t in range(TT):
                for n in range(4):
                    v.wait_ge(wo_done, 4 * t + n + 1)
                    prod = slot(5)[:, (n % 2) * MIX:(n % 2 + 1) * MIX]
                    step(V.tensor_tensor(prod, ps[:, 4 * t + n, :], gt1row[:, n * MIX:(n + 1) * MIX], ALU.mult))
                    x1n = x1[:, t, n * MIX:(n + 1) * MIX]
                    V.tensor_tensor(x1n, x1n, prod, ALU.add).then_inc(x1_ready, 1)
            for t in range(TT):
                v.wait_ge(sq_done, 3 + t)
                step(V.tensor_scalar(stat[:, 6 + t:7 + t], stat[:, 4 + t:5 + t], 1.0 / D, EPS, ALU.mult, ALU.add))
                V.reciprocal(stat[:, 6 + t:7 + t], stat[:, 6 + t:7 + t]).then_inc(inv_ready, 1)
            for b in range(1, 8, 2):
                v.wait_ge(h2_t, b + 1)
                for k in (2 * b, 2 * b + 1):
                    V.tensor_scalar(h2T[:, k, :], tiles(b, 1)[:, k % 2, :], scale2[:, k:k + 1], mod[:, SH2, k:k + 1],
                                    ALU.mult, ALU.add).then_inc(h2_readyV, 1)

            def b8(ap, n):
                return ap.unsqueeze(2).broadcast_to([P, TT, n])

            def first_of(out_hot, key, least, n):
                step(V.scalar_tensor_tensor(out=key, in0=key, scalar=-float(PER_GROUP), in1=io8[:, :, 0:n],
                                            op0=ALU.mult, op1=ALU.add))
                step(V.tensor_reduce(least, key, AX_X, ALU.min))
                step(V.tensor_tensor(out_hot, key, b8(least, n), ALU.is_equal))

            step(V.memset(hid, 0.0))
            v.wait_ge(logit_done, 1)
            V.tensor_copy(logitT, ps[0:36, 0, 0:S]).then_inc(logit_saved, 1)
            v.wait_ge(logit_t, 1)
            step(V.tensor_copy(lg[:, :, :], ps[:, 1, 0:72].rearrange("p (t n) -> p t n", t=TT)))
            step(V.tensor_reduce(rs[:, 0, :], lg[:, :, 0:4], AX_X, ALU.max))
            V.tensor_tensor(r8[:, :, 0, 0:4], lg[:, :, 0:4], b8(rs[:, 0, :], 4), ALU.subtract).then_inc(r_ask, 1)
            ghot = r8[:, :, 2, 0:4]
            step(V.tensor_tensor(ghot, lg[:, :, 0:4], b8(rs[:, 0, :], 4), ALU.is_equal))
            first_of(ghot, ghot, rs[:, 1, :], 4)
            v.wait_ge(r_exp, 1)
            step(V.tensor_reduce(rs[:, 2, :], r8[:, :, 1, 0:4], AX_X, ALU.add))
            step(V.reciprocal(rs[:, 3, :], rs[:, 2, :]))
            for t in range(TT):
                step(V.tensor_tensor(ra[:, t, :, :], lg[:, t, 4:36].rearrange("p (g e) -> p g e", g=4),
                                     r8[:, t, 2, 0:4].unsqueeze(2).broadcast_to([P, 4, PER_GROUP]), ALU.mult))
            le = r8[:, :, 0, :]
            v.wait_ge(r_exp, 1)
            for t in range(TT):
                step(V.tensor_reduce(r8[:, t, 0, :], ra[:, t, :, :].rearrange("p g e -> p e g"), AX_X, ALU.add))
            hot1, hot2, le2 = r8[:, :, 3, :], r8[:, :, 4, :], r8[:, :, 1, :]
            step(V.tensor_reduce(rs[:, 4, :], le, AX_X, ALU.max))
            step(V.tensor_tensor(hot1, le, b8(rs[:, 4, :], 8), ALU.is_equal))
            first_of(hot1, hot1, rs[:, 5, :], 8)
            step(V.scalar_tensor_tensor(out=le2, in0=hot1, scalar=-3.0e38, in1=le, op0=ALU.mult, op1=ALU.add))
            step(V.tensor_reduce(rs[:, 6, :], le2, AX_X, ALU.max))
            step(V.tensor_tensor(rs[:, 7, :], rs[:, 6, :], rs[:, 4, :], ALU.subtract))
            v.sem_inc(r_ask, 1)
            step(V.tensor_tensor(hot2, le2, b8(rs[:, 6, :], 8), ALU.is_equal))
            first_of(hot2, hot2, rs[:, 9, :], 8)
            for t in range(TT):
                for m, hot in ((m1, 3), (m2, 4)):
                    step(V.tensor_tensor(m[:, t, :, :], r8[:, t, 2, 0:4].unsqueeze(2).broadcast_to([P, 4, PER_GROUP]),
                                         r8[:, t, hot, :].unsqueeze(1).broadcast_to([P, 4, PER_GROUP]), ALU.mult))
            flat = "p t g e -> p (t g e)"
            V.tensor_tensor(ra[:, :, :, :].rearrange(flat), m1[:, :, :, :].rearrange(flat),
                            m2[:, :, :, :].rearrange(flat), ALU.add).then_inc(mask_ready, 1)
            v.wait_ge(r_exp, 2)
            step(V.tensor_scalar(rs[:, 10, :], rs[:, 8, :], 1.0, None, ALU.add))
            step(V.reciprocal(rs[:, 10, :], rs[:, 10, :]))
            step(V.tensor_tensor(rs[:, 11, :], rs[:, 3, :], rs[:, 10, :], ALU.mult))
            step(V.tensor_tensor(rs[:, 12, :], rs[:, 11, :], rs[:, 8, :], ALU.mult))
            v.wait_ge(pos_done, 1)
            step(V.tensor_copy(ct[:, 0, :], ps[0:32, 2, 0:P]))
            step(V.tensor_scalar(ct[:, 1, :], ct[:, 0, :], float(NWIN), 1.0, ALU.is_gt, ALU.add))
            for w in range(2, MAXWIN):
                ins = V.scalar_tensor_tensor(out=ct[:, 1, :], in0=ct[:, 0, :], scalar=float(w * NWIN), in1=ct[:, 1, :],
                                             op0=ALU.is_gt, op1=ALU.add)
                if w < MAXWIN - 1:
                    step(ins)
            ins.then_inc(cnt_ready, 1)
            v.wait_ge(start_done, 1)
            v.wait_ge(cnt_ready, 1)
            step(V.tensor_copy(st[:, 0, :], ps[:, 3, 0:32]))
            step(V.tensor_copy(ec[:, 0:2], ps[0:32, 3, 32:34]))
            passes = keep[0:32, K_PASS:K_PASS + MAXPASS]
            for w in range(MAXWIN):
                step(V.tensor_scalar(ec[:, 2:3], ec[:, 1:2], float(w), None, ALU.add))
                step(V.tensor_scalar(ec[:, 3:4], ct[:, 1, 0:1], float(w), None, ALU.is_gt))
                step(V.tensor_scalar(ec[:, 4:5], ec[:, 0:1], float(w * NWIN), None, ALU.add))
                hot = eh[:, 2, :] if w else eh[:, 0, :]
                step(V.tensor_scalar(hot, passes, ec[:, 2:3], ec[:, 3:4], ALU.is_equal, ALU.mult))
                if w == 0:
                    step(V.tensor_scalar(eh[:, 1, :], hot, ec[:, 4:5], None, ALU.mult))
                else:
                    step(V.scalar_tensor_tensor(out=eh[:, 1, :], in0=hot, scalar=ec[:, 4:5], in1=eh[:, 1, :],
                                                op0=ALU.mult, op1=ALU.add))
                    step(V.tensor_tensor(eh[:, 0, :], eh[:, 0, :], hot, ALU.add))
            v.sem_inc(pass_hot, 1)
            mall = ra[:, :, :, :].rearrange("p t g e -> p t (g e)")
            for t in range(TT):
                step(V.tensor_tensor(mall[:, t, :], ps[:, 1, t * 32:(t + 1) * 32], st[:, 0, :], ALU.add))
            for m, r in ((m1, 13), (m2, 14)):
                mm_ = m[:, :, :, :].rearrange("p t g e -> p t (g e)")
                step(V.tensor_tensor(mm_, mm_, mall, ALU.mult))
                step(V.tensor_reduce(rs[:, r, :], mm_, AX_X, ALU.add))
            step(V.memset(otab[:, :], 0))
            step(V.memset(etab[:, :], 0))
            v.wait_ge(pass_done, 1)
            step(V.tensor_copy(etab[0:1, 0:MAXPASS], ps[0:1, 2, 0:MAXPASS]))
            step(V.tensor_copy(otab[0:1, 1:1 + MAXPASS], ps[0:1, 2, 64:64 + MAXPASS]))
            step(V.tensor_copy(ntab[:, :], ps[0:1, 2, 128:129]))
            v.wait_ge(iota_in, 48)
            for t in range(TT):
                step(V.tensor_scalar(sel[:, t, 0:PAIRS], iota, rs[:, 13, t:t + 1], None, ALU.is_equal))
                step(V.scalar_tensor_tensor(out=sel[:, t, 0:PAIRS], in0=iota, scalar=rs[:, 14, t:t + 1],
                                            in1=sel[:, t, 0:PAIRS], op0=ALU.is_equal, op1=ALU.add))
            step(V.memset(sel[:, :, PAIRS:PADDED], 0.0))
            v.sem_inc(table_ready, 1)
            v.wait_ge(parts_act, 2)
            v.wait_ge(parts_sub, 2)
            for t in range(TT):
                sw = selw[:, t * PAIRS:(t + 1) * PAIRS]
                sw2 = selw[:, (2 + t) * PAIRS:(3 + t) * PAIRS]
                step(V.tensor_scalar(sw, iota, rs[:, 13, t:t + 1], rs[:, 11, t:t + 1], ALU.is_equal, ALU.mult))
                step(V.tensor_scalar(sw2, iota, rs[:, 14, t:t + 1], rs[:, 12, t:t + 1], ALU.is_equal, ALU.mult))
                step(V.tensor_tensor(sw, sw, sw2, ALU.add))
            v.sem_inc(selw_ready, 1)

            gat = ps[:, 0, :].rearrange("p (c n) -> p c n", n=NWIN)
            ye = ps[:, 4:8, :].rearrange("p b (c n) -> p (b c) n", n=P)[:, :, 0:NWIN]

            def wide(ap, n):
                return ap.unsqueeze(2).broadcast_to([P, n, NWIN])

            def xs_made(p, half):
                ks = slice(half * HALF, (half + 1) * HALF)
                v.wait_ge(gathered, 2 * p + half + 1)
                if not (isinstance(p, int) and 2 * p + half == 0):
                    v.wait_ge(xe_ready, 2 * p + half)
                V.tensor_tensor(xs, gat, wide(scale2[:, ks], HALF), ALU.mult).then_inc(xe_step, 1)
                v.wait_ge(xe_step, 2 * p + half + 1)
                V.tensor_tensor(xs, xs, wide(mod[:, SH2, ks], HALF), ALU.add).then_inc(xs_ready, 1)

            def xe_low(p, half):
                ks = slice(half * HALF, (half + 1) * HALF)
                v.wait_ge(xhi_done, 2 * p + half + 1)
                V.tensor_tensor(xe[:, ks, NWIN:2 * NWIN], xs, xe[:, ks, 0:NWIN].bitcast(F32), ALU.subtract
                                ).then_inc(xe_ready, 1)

            def save_output(p, off, q):
                v.wait_ge(w2_used, 4 * p + q + 5)
                V.tensor_tensor(YS[:, 4 * q:4 * q + 4, bass.ds(off, NWIN)], ye[:, 4 * q:4 * q + 4, :],
                                wide(mod[:, GT2, 4 * q:4 * q + 4], 4), ALU.mult).then_inc(ye_saved, 1)

            def hidden(p):
                v.wait_ge(silu_done, p)
                V.tensor_tensor(hid[:, :, 0:NWIN], silu_sb.rearrange("p (f n) -> p f n", f=FT),
                                ps[:, 1, FT * NWIN:2 * FT * NWIN].rearrange("p (f n) -> p f n", f=FT), ALU.mult
                                ).then_inc(hid_ready, 1)

            def pieces(p, off):
                for i in range(PIECES):
                    v.wait_ge(hi_done, 16 * p + i + 1)
                    V.tensor_tensor(w_lo[i % 4].rearrange("p (m n) -> p m n", m=2),
                                    chunk(i // 2 % 4).rearrange("p (m k n) -> p m k n", m=2, k=2)[:, :, i % 2, :],
                                    w_hi[i % 4].bitcast(F32).rearrange("p (m n) -> p m n", m=2), ALU.subtract
                                    ).then_inc(lo_done, 1)
                    if off is not None:
                        if i == 1:
                            xs_made(p, 1)
                            hidden(p)
                        if i == 2:
                            xe_low(p, 1)
                        if i == 11:
                            save_output(p, off, 0)
                        if i == 14:
                            save_output(p, off, 1)
                    if i == 12:
                        xs_made(p + 1, 0)
                    if i == 13:
                        xe_low(p + 1, 0)
                if off is not None:
                    save_output(p, off, 2)
                v.wait_ge(piece_used, 16 * p + 16 + 4)
                V.tensor_copy(h_sb[1], ps[:, 3, :]).then_inc(h3_saved, 1)
                if off is not None:
                    save_output(p, off, 3)

            v.sem_inc(lo_done, 8)
            for half in range(2):
                xs_made(0, half)
                xe_low(0, half)
            n_pass = v.value_load(ntab[0:1, 0:1], min_val=NE, max_val=MAXPASS)
            pieces(0, None)
            with v.Fori(1, MAXPASS) as p:
                with v.If(p < n_pass):
                    pieces(p, v.value_load(otab[0:1, bass.ds(p, 1)], min_val=0, max_val=PAIRS))
            hidden(n_pass)
            last_off = v.value_load(otab[0:1, bass.ds(n_pass, 1)], min_val=0, max_val=PAIRS)
            for q in range(4):
                save_output(n_pass, last_off, q)
            v.wait_ge(ye_saved, 4 * n_pass)
            v.sem_inc(yT_savedV, 1)

            yn = ring[:, 0:2, :].rearrange("p s (i d) -> p (s i) d", d=D)
            for i in range(4):
                b = 4 * (i % 2) + 2
                v.wait_ge(yT_done, i + 1)
                V.tensor_copy(yn[:, i, 1024:2048], ps[:, b:b + 2, :].rearrange("p b n -> p (b n)")).then_inc(yT_savedV, 1)
            v.wait_ge(fg_in, 16)

            def add_moe(t, n):
                v.wait_ge(comb_done, 4 * t + n + 1)
                x1n = x1[:, t, n * MIX:(n + 1) * MIX]
                V.tensor_tensor(x1n, x1n, ps[:, 4 * t + n, :], ALU.add).then_inc(x2_ready, 1)

            def last_norm(t):
                v.wait_ge(sq_done, 4 + 4 * (t + 1))
                r = stat[:, 16 + t:17 + t]
                step(V.tensor_reduce(r, stat[:, 8 + 4 * t:12 + 4 * t], AX_X, ALU.add))
                step(V.tensor_scalar(r, r, 1.0 / D, EPS, ALU.mult, ALU.add))
                V.reciprocal(r, r).then_inc(inv_ready, 1)
                v.wait_ge(root_done, 5 + t)
                V.scalar_tensor_tensor(out=slot(2)[:, t * D:(t + 1) * D], in0=x1[:, t, :], scalar=r,
                                       in1=fgrow, op0=ALU.mult, op1=ALU.mult).then_inc(fin_ready, 1)

            for n in range(4):
                add_moe(0, n)
            add_moe(1, 0)
            last_norm(0)
            for n in range(1, 4):
                add_moe(1, n)
            last_norm(1)


def constants():
    import numpy as np

    i = np.arange(P)
    keep = np.zeros((P, N_KEEP), np.float32)
    keep[:, 0:128] = np.eye(P)
    keep[:, 128:256] = 1.0
    keep[:, 256:384] = i[:, None] < i[None, :]
    keep[:, 384:400] = np.tile(np.arange(8), 2)
    keep[:, K_II:K_II + 64] = i[:, None] % 64 == np.arange(64)
    keep[:, K_IDX] = i
    keep[:, K_PASS:] = np.arange(MAXPASS)
    t = np.arange(S)
    pool = np.zeros((S, 4, S))
    for q, w in enumerate(POOL_WINDOWS):
        left = w // 2
        lo, hi = np.clip(t - left, 0, S), np.clip(t + w - left, 0, S)
        inside = (t[:, None] >= lo[None, :]) & (t[:, None] < hi[None, :])
        pool[:, q, :] = inside / (hi - lo)[None, :] - np.eye(S)
    a = 2 * np.pi * (np.outer(t, t) % S) / S
    norm = 1 / np.sqrt(S * P)
    pos = np.concatenate([np.cos(a), np.sin(a)], 1) * norm
    b = 2 * np.pi * (np.outer(i, i) % P) / P
    ch = np.concatenate([np.cos(b), -np.sin(b)], 1)
    halves = lambda m: m.reshape(2, P, -1).transpose(1, 0, 2).reshape(P, -1)
    mix = np.concatenate([halves(pool.reshape(S, -1)), halves(pos), ch], 1).astype(np.float32)
    iota = np.tile(np.arange(512, dtype=np.float32), (P, 1))
    return keep, np.ascontiguousarray(mix), iota


_INS = ["x", "c", "ada_w", "ada_b", "norm1_g", "w_in", "pool_w", "pool_scale", "conf_dw_w", "conf_dw_b", "conf_ln_g",
        "conf_ln_b", "branch_w", "sc_conv_w", "w_o", "norm2_g", "rg_w", "rg_b", "re_w", "re_b", "exp_w1", "exp_w3",
        "exp_w2", "final_g"]


def kernel(**inputs):
    import numpy as _np
    import concourse.bacc as _bacc
    from concourse import mybir as _mybir
    from concourse.bass_utils import run_bass_kernel_spmd as _run

    given = dict(inputs)
    given["branch_w"] = _np.stack([_np.asarray(inputs[n])[0] for n in ("conf_w_out", "sc_w_out", "fnet_w_out")])
    nc = _bacc.Bacc("TRN2", target_bir_lowering=False, num_devices=1)
    arrays, args = {}, []
    for name in _INS:
        a = _np.asarray(given[name])
        if name not in ("final_g", "branch_w"):
            a = a[0]
        a = _np.ascontiguousarray(a)
        arrays[f"in_{name}"] = a
        args.append(nc.dram_tensor(f"in_{name}", a.shape, _mybir.dt.from_np(a.dtype), kind="ExternalInput").ap())
    for name, a in zip(("keep_consts", "mix_consts", "iota_const"), constants()):
        arrays[f"in_{name}"] = a
        args.append(nc.dram_tensor(f"in_{name}", a.shape, _mybir.dt.from_np(a.dtype), kind="ExternalInput").ap())
    args.append(nc.dram_tensor("out_0", (S, D), F32, kind="ExternalOutput").ap())
    build(nc, *args)
    r = _run(nc, [arrays], core_ids=[0])
    return r.results[0]["out_0"].reshape(1, S, D)
```
